# Optimizing a Trainium2 kernel written in Bass

```python
import jax, jax.numpy as jnp
from jax import lax
import numpy as np

D_MODEL = 1024
BATCH = 1
SEQ = 1024
DEPTH = 2
DEC_BATCH = 1
DEC_SEQ = 32
PAST_LEN = 256

CHUNK = 64
N_EVEN = (DEPTH + 1) // 2
N_ODD = DEPTH // 2
EPS = 1e-6

A_CHUNK = 128
A_GROUPS = 4
A_WIDTH = D_MODEL
A_GROUP_DIM = A_WIDTH // A_GROUPS
B_HEAD_DIM = 64
B_WIDTH = D_MODEL
B_HEADS = B_WIDTH // B_HEAD_DIM
B_GROUPS = 2
B_STATE = 128
B_CONV = 4
B_CONV_DIM = B_WIDTH + 2 * B_GROUPS * B_STATE
SSD_BLOCK = 128
C_HEADS = 8
C_HEAD_DIM = D_MODEL // C_HEADS
C_WIDTH = C_HEADS * C_HEAD_DIM
Q_BLOCK = 128

EVEN_IN = 3 * A_WIDTH + B_WIDTH + B_CONV_DIM + B_HEADS
EVEN_SPLITS = (A_WIDTH, 2 * A_WIDTH, 3 * A_WIDTH, 3 * A_WIDTH + B_WIDTH, 3 * A_WIDTH + B_WIDTH + B_CONV_DIM)
ODD_IN = 4 * C_WIDTH + C_HEADS
ODD_SPLITS = (C_WIDTH, 2 * C_WIDTH, 3 * C_WIDTH, 4 * C_WIDTH)

kernel_name = "hybrid_stream_gmlp_ssd_fox_step"

def rmsnorm(x, g):
    xf = x.astype(jnp.float32)
    y = xf * lax.rsqrt(jnp.mean(xf * xf, axis=-1, keepdims=True) + EPS) * g.astype(jnp.float32)
    return y.astype(x.dtype)

def causal_dwconv(x, ctx, w, b):
    L = x.shape[1]
    xp = jnp.concatenate([ctx.astype(x.dtype), x], axis=1)
    y = b.astype(x.dtype) + sum(xp[:, k:k + L] * w[:, k].astype(x.dtype) for k in range(B_CONV))
    return y, xp[:, xp.shape[1] - (B_CONV - 1):]

def gmlp_branch(u, v, z, ws, bs, gv):
    b, L, _ = u.shape
    u = jax.nn.gelu(u, approximate=False)
    v = rmsnorm(jax.nn.gelu(v, approximate=False).reshape(b, L, A_GROUPS, A_GROUP_DIM), gv)
    n = min(L, A_CHUNK)
    nc = L // n
    pos = jnp.arange(n)
    mask = (pos[None, :] // CHUNK) <= (pos[:, None] // CHUNK)
    w = jnp.where(mask[None], ws[:, :n, :n], 0.0).astype(v.dtype)
    s = jnp.einsum('gij,bcjgk->bcigk', w, v.reshape(b, nc, n, A_GROUPS, A_GROUP_DIM))
    s = s + bs[:, :n].T[None, None, :, :, None].astype(s.dtype)
    s = s.reshape(b, L, A_WIDTH)
    return jax.nn.silu(z) * u * s, v.reshape(b, L, A_WIDTH)

def ssd_scan(x, dt, a, bm, cm, s0, blk):
    b, L, H, P = x.shape
    G, N = bm.shape[2], bm.shape[3]
    R = H // G
    nb = L // blk
    x = x.reshape(b, nb, blk, G, R, P)
    dt = dt.reshape(b, nb, blk, G, R)
    acs = jnp.cumsum(dt * a.reshape(G, R), axis=2)
    bm = bm.reshape(b, nb, blk, G, N)
    cm = cm.reshape(b, nb, blk, G, N)
    dtx = dt[..., None] * x
    causal = jnp.tril(jnp.ones((blk, blk), dtype=bool))
    seg = acs[:, :, :, None] - acs[:, :, None, :]
    decay = jnp.exp(jnp.where(causal[:, :, None, None], seg, -jnp.inf))
    cb = jnp.einsum('bclgn,bcsgn->bclsg', cm, bm)
    y_intra = jnp.einsum('bclsg,bclsgr,bcsgrp->bclgrp', cb, decay, dtx)
    to_end = jnp.exp(acs[:, :, -1:] - acs)
    ds = jnp.einsum('bclgr,bclgrp,bclgn->bcgrpn', to_end, dtx, bm)
    blk_decay = jnp.exp(acs[:, :, -1])

    def step(s, inp):
        ds_c, dec_c = inp
        return dec_c[..., None, None] * s + ds_c, s

    s_fin, s_prev = lax.scan(step, s0.reshape(b, G, R, P, N),
                             (jnp.moveaxis(ds, 1, 0), jnp.moveaxis(blk_decay, 1, 0)))
    s_prev = jnp.moveaxis(s_prev, 0, 1)
    y_state = jnp.einsum('bclgn,bcgrpn,bclgr->bclgrp', cm, s_prev, jnp.exp(acs))
    return (y_intra + y_state).reshape(b, L, H, P), s_fin.reshape(b, H, P, N)

def ssd_branch(zb, xbc, dt_raw, conv_ctx, s0, conv_w, conv_b, dt_bias, a_log, d_skip, g_ssd):
    b, L, _ = xbc.shape
    xbc, new_ctx = causal_dwconv(xbc, conv_ctx, conv_w, conv_b)
    xbc = jax.nn.silu(xbc).astype(jnp.float32)
    xs = xbc[..., :B_WIDTH].reshape(b, L, B_HEADS, B_HEAD_DIM)
    bm = xbc[..., B_WIDTH:B_WIDTH + B_GROUPS * B_STATE].reshape(b, L, B_GROUPS, B_STATE)
    cm = xbc[..., B_WIDTH + B_GROUPS * B_STATE:].reshape(b, L, B_GROUPS, B_STATE)
    dt = jax.nn.softplus(dt_raw.astype(jnp.float32) + dt_bias.astype(jnp.float32))
    a = -jnp.exp(a_log.astype(jnp.float32))
    blk = SSD_BLOCK if L % SSD_BLOCK == 0 else L
    y, s_fin = ssd_scan(xs, dt, a, bm, cm, s0.astype(jnp.float32), blk)
    y = y + d_skip.astype(jnp.float32)[:, None] * xs
    y = y.reshape(b, L, B_WIDTH) * jax.nn.silu(zb.astype(jnp.float32))
    y = rmsnorm(y.reshape(b, L, B_GROUPS, B_WIDTH // B_GROUPS),
                g_ssd.reshape(B_GROUPS, B_WIDTH // B_GROUPS)).reshape(b, L, B_WIDTH)
    return y.astype(zb.dtype), s_fin, new_ctx

def fox_branch(q, k, v, z, f_logit, past_k, past_v, past_logf, gq, gk):
    b, L, _ = q.shape
    q = rmsnorm(q.reshape(b, L, C_HEADS, C_HEAD_DIM), gq)
    k = rmsnorm(k.reshape(b, L, C_HEADS, C_HEAD_DIM), gk)
    v = v.reshape(b, L, C_HEADS, C_HEAD_DIM)
    logf = jax.nn.log_sigmoid(f_logit.astype(jnp.float32))
    p0 = past_k.shape[1]
    k_all = jnp.concatenate([past_k.astype(k.dtype), k], axis=1)
    v_all = jnp.concatenate([past_v.astype(v.dtype), v], axis=1)
    f_cum = jnp.cumsum(jnp.concatenate([past_logf.astype(jnp.float32), logf], axis=1), axis=1)
    f_k = jnp.moveaxis(f_cum, 2, 1)
    key_pos = jnp.arange(p0 + L)
    q_pos = p0 + jnp.arange(L)
    qb = Q_BLOCK if L % Q_BLOCK == 0 else L
    nb = L // qb
    scale = C_HEAD_DIM ** -0.5

    def attend(args):
        q_blk, fq_blk, pos_blk = args
        s = jnp.einsum('blhd,bshd->bhls', q_blk, k_all).astype(jnp.float32) * scale
        s = s + jnp.moveaxis(fq_blk, 2, 1)[..., None] - f_k[:, :, None, :]
        s = jnp.where(key_pos[None, :] <= pos_blk[:, None], s, -jnp.inf)
        p = jax.nn.softmax(s, axis=-1).astype(v_all.dtype)
        return jnp.einsum('bhls,bshd->blhd', p, v_all)

    out = lax.map(attend, (jnp.moveaxis(q.reshape(b, nb, qb, C_HEADS, C_HEAD_DIM), 1, 0),
                           jnp.moveaxis(f_cum[:, p0:].reshape(b, nb, qb, C_HEADS), 1, 0),
                           q_pos.reshape(nb, qb)))
    out = jnp.moveaxis(out, 0, 1).reshape(b, L, C_WIDTH)
    return jax.nn.silu(z) * out, k, v, logf

def even_layer(x, g_pre, g_post, w_in, w_out, ws, bs, gv, conv_w, conv_b, dt_bias, a_log, d_skip, g_ssd,
               conv_ctx, s0):
    h = rmsnorm(x, g_pre)
    proj = jnp.einsum('bld,de->ble', h, w_in)
    u, v, za, zb, xbc, dt_raw = jnp.split(proj, EVEN_SPLITS, axis=-1)
    ya, v_rows = gmlp_branch(u, v, za, ws, bs, gv)
    yb, s_fin, new_ctx = ssd_branch(zb, xbc, dt_raw, conv_ctx, s0, conv_w, conv_b, dt_bias, a_log, d_skip, g_ssd)
    o = jnp.einsum('ble,ed->bld', jnp.concatenate([ya, yb.astype(ya.dtype)], axis=-1), w_out)
    return x + rmsnorm(o, g_post), v_rows, s_fin, new_ctx

def odd_layer(x, g_pre, g_post, w_in, b_f, w_out, gq, gk, past_k, past_v, past_logf):
    h = rmsnorm(x, g_pre)
    proj = jnp.einsum('bld,de->ble', h, w_in)
    q, k, v, z, f_logit = jnp.split(proj, ODD_SPLITS, axis=-1)
    yc, k_rows, v_rows, logf_rows = fox_branch(q, k, v, z, f_logit + b_f.astype(f_logit.dtype),
                                               past_k, past_v, past_logf, gq, gk)
    o = jnp.einsum('ble,ed->bld', yc, w_out)
    return x + rmsnorm(o, g_post), k_rows, v_rows, logf_rows

def setup_inputs(seed: int = 0) -> dict:
    key = jax.random.key(seed)
    ks = jax.random.split(key, 32)
    f32 = jnp.float32
    nrm = lambda k, shape, s=1.0: s * jax.random.normal(k, shape, f32)
    dt0 = jnp.exp(jax.random.uniform(ks[0], (N_EVEN, B_HEADS), f32) * (np.log(0.1) - np.log(0.001)) + np.log(0.001))
    return {
        "x_prompt": nrm(ks[1], (BATCH, SEQ, D_MODEL)),
        "x_sample": nrm(ks[2], (DEC_BATCH, DEC_SEQ, D_MODEL)),
        "cache_fox_k": nrm(ks[3], (N_ODD, DEC_BATCH, PAST_LEN, C_HEADS, C_HEAD_DIM)),
        "cache_fox_v": nrm(ks[4], (N_ODD, DEC_BATCH, PAST_LEN, C_HEADS, C_HEAD_DIM)),
        "cache_fox_logf": jax.nn.log_sigmoid(2.0 + nrm(ks[5], (N_ODD, DEC_BATCH, PAST_LEN, C_HEADS), 0.5)),
        "state_ssd": nrm(ks[6], (N_EVEN, DEC_BATCH, B_HEADS, B_HEAD_DIM, B_STATE), 0.1),
        "state_conv": nrm(ks[7], (N_EVEN, DEC_BATCH, B_CONV - 1, B_CONV_DIM)),
        "norm_pre": 1.0 + nrm(ks[8], (DEPTH, D_MODEL), 0.1),
        "norm_post": 1.0 + nrm(ks[9], (DEPTH, D_MODEL), 0.1),
        "w_in_even": nrm(ks[10], (N_EVEN, D_MODEL, EVEN_IN), D_MODEL ** -0.5),
        "w_out_even": nrm(ks[11], (N_EVEN, A_WIDTH + B_WIDTH, D_MODEL), (A_WIDTH + B_WIDTH) ** -0.5),
        "gmlp_ws": nrm(ks[12], (N_EVEN, A_GROUPS, A_CHUNK, A_CHUNK), A_CHUNK ** -0.5),
        "gmlp_bs": 1.0 + nrm(ks[13], (N_EVEN, A_GROUPS, A_CHUNK), 0.1),
        "gmlp_gv": 1.0 + nrm(ks[14], (N_EVEN, A_GROUPS, A_GROUP_DIM), 0.1),
        "ssd_conv_w": nrm(ks[15], (N_EVEN, B_CONV_DIM, B_CONV), B_CONV ** -0.5),
        "ssd_conv_b": nrm(ks[16], (N_EVEN, B_CONV_DIM), 0.01),
        "ssd_dt_bias": dt0 + jnp.log(-jnp.expm1(-dt0)),
        "ssd_a_log": jnp.log(jax.random.uniform(ks[17], (N_EVEN, B_HEADS), f32, 1.0, 16.0)),
        "ssd_d": 1.0 + nrm(ks[18], (N_EVEN, B_HEADS), 0.1),
        "ssd_norm_g": 1.0 + nrm(ks[19], (N_EVEN, B_WIDTH), 0.1),
        "w_in_odd": nrm(ks[20], (N_ODD, D_MODEL, ODD_IN), D_MODEL ** -0.5),
        "fox_b_forget": 2.0 + nrm(ks[21], (N_ODD, C_HEADS), 0.5),
        "w_out_odd": nrm(ks[22], (N_ODD, C_WIDTH, D_MODEL), C_WIDTH ** -0.5),
        "fox_gq": 1.0 + nrm(ks[23], (N_ODD, C_HEAD_DIM), 0.1),
        "fox_gk": 1.0 + nrm(ks[24], (N_ODD, C_HEAD_DIM), 0.1),
    }

def reference(x_prompt, x_sample, cache_fox_k, cache_fox_v, cache_fox_logf, state_ssd, state_conv,
              norm_pre, norm_post, w_in_even, w_out_even, gmlp_ws, gmlp_bs, gmlp_gv,
              ssd_conv_w, ssd_conv_b, ssd_dt_bias, ssd_a_log, ssd_d, ssd_norm_g,
              w_in_odd, fox_b_forget, w_out_odd, fox_gq, fox_gk):
    xp, xs = x_prompt, x_sample
    bp = xp.shape[0]
    kp_l, vp_l, lp_l, sp_l, cp_l = [], [], [], [], []
    ks_l, vs_l, ls_l, ss_l, cs_l, gs_l = [], [], [], [], [], []
    for i in range(DEPTH):
        j = i // 2
        if i % 2 == 0:
            ew = (w_in_even[j], w_out_even[j], gmlp_ws[j], gmlp_bs[j], gmlp_gv[j], ssd_conv_w[j], ssd_conv_b[j],
                  ssd_dt_bias[j], ssd_a_log[j], ssd_d[j], ssd_norm_g[j])
            xp, _, sp, cp = even_layer(xp, norm_pre[i], norm_post[i], *ew,
                                       jnp.zeros((bp, B_CONV - 1, B_CONV_DIM), xp.dtype),
                                       jnp.zeros((bp, B_HEADS, B_HEAD_DIM, B_STATE), jnp.float32))
            xs, gv_s, ss, cs = even_layer(xs, norm_pre[i], norm_post[i], *ew, state_conv[j], state_ssd[j])
            sp_l.append(sp); cp_l.append(cp)
            ss_l.append(ss); cs_l.append(cs); gs_l.append(gv_s)
        else:
            ow = (w_in_odd[j], fox_b_forget[j], w_out_odd[j], fox_gq[j], fox_gk[j])
            xp, kp, vp, lp = odd_layer(xp, norm_pre[i], norm_post[i], *ow,
                                       jnp.zeros((bp, 0, C_HEADS, C_HEAD_DIM), xp.dtype),
                                       jnp.zeros((bp, 0, C_HEADS, C_HEAD_DIM), xp.dtype),
                                       jnp.zeros((bp, 0, C_HEADS), jnp.float32))
            xs, ksr, vsr, lsr = odd_layer(xs, norm_pre[i], norm_post[i], *ow,
                                          cache_fox_k[j], cache_fox_v[j], cache_fox_logf[j])
            kp_l.append(kp); vp_l.append(vp); lp_l.append(lp)
            ks_l.append(ksr); vs_l.append(vsr); ls_l.append(lsr)
    fox_k_prompt = jnp.stack(kp_l)
    fox_v_prompt = jnp.stack(vp_l)
    fox_logf_prompt = jnp.stack(lp_l)
    ssd_state_prompt = jnp.stack(sp_l)
    conv_state_prompt = jnp.stack(cp_l)
    fox_k_sample = jnp.stack(ks_l)
    fox_v_sample = jnp.stack(vs_l)
    fox_logf_sample = jnp.stack(ls_l)
    ssd_state_sample = jnp.stack(ss_l)
    conv_state_sample = jnp.stack(cs_l)
    gmlp_v_sample = jnp.stack(gs_l)
    return (xp, xs, fox_k_prompt, fox_v_prompt, fox_logf_prompt, ssd_state_prompt, conv_state_prompt,
            fox_k_sample, fox_v_sample, fox_logf_sample, ssd_state_sample, conv_state_sample, gmlp_v_sample)


_drawn_inputs = setup_inputs


def setup_inputs(seed=0):
    import zlib

    import numpy as np

    out = dict(_drawn_inputs(seed))
    spreads = {}
    factors = {'cache_fox_logf': 3.547, 'ssd_conv_b': 3.313}
    for name, (base, spread) in spreads.items():
        noise = np.random.default_rng([zlib.crc32(name.encode()), seed]).standard_normal(out[name].shape)
        drawn = base * np.exp(spread * noise) if base else spread * noise
        out[name] = __import__('jax').numpy.asarray(drawn.astype(out[name].dtype))
    for name, factor in factors.items():
        out[name] = (out[name] * factor).astype(out[name].dtype)
    return out
```

```python
import concourse.bass as bass
from concourse import mybir
from contextlib import ExitStack, contextmanager

f32 = mybir.dt.float32
f32r = mybir.dt.float32r
ALU = mybir.AluOpType
ACT = mybir.ActivationFunctionType
AX = mybir.AxisListType

P = 128
D = 1024
KT = D // P
SEQ, DEC = 1024, 32
TOK = SEQ + DEC
NB = SEQ // P
CH = TOK // 3
PAST = 256
EPS = 1e-6
EVEN_IN, XBC0, DT0 = 5648, 4096, 5632
XBC_TILES = 12
HEADS_B, GROUPS_B, HP = 16, 2, 64
A_GROUPS = 4
HEADS_C = 8
SCALE = float(P) ** -0.5
TAPS = 4
PADW = 3 + SEQ + 3 + DEC
CONVW = PADW - 3
SAMP = 3 + SEQ + 3
KEYS = SEQ + PAST + DEC
NEG = -30000.0
NEGBIG = -1e30

W_BC, W_DT, W_XZ, W_V, W_UZ, W_OE, W_F, W_QKVZ, W_OO, W_END = 0, 4, 5, 21, 29, 45, 61, 62, 94, 102

PRE0, POST0, PRE1, POST1, GSSD, CONVB, GQ, GK, CTX = 0, 8, 16, 24, 32, 40, 52, 53, 54
N_ROWS = CTX + 36
QUADS = [(0, 4, P), (4, 4, P), (8, 1, DEC)]


def tile_no(first, per, t):
    return first, per, t


def times(w, k, add):
    first, per, t = w
    return first * k + add + per * k * t


def loads_of_slot(w):
    first, per, t = w
    if per == 1:
        assert isinstance(t, int)
        first, t = first + t, 0
    return 16 * (first // 2 + 1) + 16 * (per // 2) * t


def slot(w):
    first, per, t = w
    return (first + (t if per == 1 else 0)) % 2


class Order:

    def __init__(self, eng, sem):
        self.eng, self.sem, self.base, self.n = eng, sem, 0, 0

    def __call__(self, ins):
        ins.then_inc(self.sem, 1)
        self.n += 1
        return ins

    def fence(self):
        self.eng.wait_ge(self.sem, self.base + self.n)

    @contextmanager
    def loop(self, start, end, per):
        before = self.base + self.n
        with self.eng.Fori(start, end) as t:
            self.base, self.n = before - per * start + per * t, 0
            yield t
            assert self.n == per, f"the loop's body counts {self.n}, not {per}"
        self.base, self.n = before + per * (end - start), 0


def hybrid_trunk(nc, x_prompt, x_sample, cache_k, cache_v, cache_logf, state_ssd, state_conv,
                 norm_pre, norm_post, w_in_even, w_out_even, gmlp_ws, gmlp_bs, gmlp_gv,
                 conv_w, conv_b, dt_bias, a_log, ssd_d, ssd_norm_g,
                 w_in_odd, b_forget, w_out_odd, gq, gk,
                 y_prompt, y_sample, k_prompt, v_prompt, logf_prompt, ssd_prompt, conv_prompt,
                 k_sample, v_sample, logf_sample, ssd_sample, conv_sample, gv_sample):
    ctx = ExitStack()
    ctx.enter_context(nc.allow_non_contiguous_dma(reason="small parameter vectors"))
    sems = {}

    def S(name):
        if name not in sems:
            sems[name] = ctx.enter_context(nc.semaphore(name))
        return sems[name]

    base = (nc.sbuf_base + 63) // 64 * 64
    end = nc.sbuf_usable_end
    BIG = KT * TOK * 4
    A_H, A_R3 = 0, 2 * BIG
    A_R4 = A_R3 + 8 * 9 * P * 4
    A_R5 = A_R4 + BIG
    A_W = A_R5 + BIG
    A_C = A_W + 6 * 4096

    def at(name, offset, shape, dt=f32):
        size = 4
        for s in shape[1:]:
            size *= s
        assert base + offset + size <= end, (name, base + offset + size - end)
        return nc.alloc_sbuf_tensor_at(name, shape, dt, offset=base + offset)

    class Region:
        def __init__(self, offset, limit):
            self.at, self.limit = offset, limit

        def __call__(self, name, shape, dt=f32):
            t = at(name, self.at, shape, dt)
            size = 4
            for s in shape[1:]:
                size *= s
            self.at += (size + 31) // 32 * 32
            assert self.at <= self.limit, (name, self.at - self.limit)
            return t

    HH = at("HH", A_H, [P, KT, TOK], f32r)
    HL = at("HL", A_H + BIG, [P, KT, TOK], f32r)
    HX = at("HX", A_H + BIG, [P, KT, TOK])
    WRAW = at("WRAW", A_W, [P, 2, KT, P])
    WH = at("WH", A_W + 8192, [P, 2, KT, P], f32r)
    WL = at("WL", A_W + 16384, [P, 2, KT, P], f32r)

    const = Region(A_C, end - base)
    IDENT = const("IDENT", [P, P])
    ONES = const("ONES", [P, P])
    COLS = const("COLS", [P, N_ROWS])
    CONVW_SB = const("CONVW", [P, XBC_TILES, TAPS])
    DCOL = const("DCOL", [P, 8])
    small = const("small", [P, 64])
    SS, MS, RT, RR = small[:, 0:9], small[:, 9:18], small[:, 18:27], small[:, 27:36]
    DTB, AL, EAL, BF = small[:, 36:37], small[:, 37:38], small[:, 38:39], small[:, 39:40]
    MX, MXR, NBIAS, RSUM, RINV = small[:, 40:44], small[:, 44:45], small[:, 45:46], small[:, 46:47], small[:, 47:48]
    c_phase = const.at

    XS = at("XS", A_R3, [P, NB + 1, D])
    r = Region(A_R4, A_W)
    SQJ = r("SQJ", [P, D])
    ROWS = r("ROWS", [P, P])
    DEXP = r("DEXP", [8, 2, HP])
    DSM = r("DSM", [8, 2])

    r = Region(A_R3, A_R5)
    CT = r("CT", [P, 2, TOK])
    BTOK = r("BTOK", [P, 2, 9, P])
    CBT = r("CBT", [P, 2, 9, P])
    m_at = r.at
    M = r("M", [P, 2, 9, P])
    BT = at("BT", m_at, [P, 2, TOK])
    ACSROW = r("ACSROW", [HEADS_B, TOK])
    XR = r("XR", [P, PADW])
    ACC = r("ACC", [P, CONVW])
    rows_at = r.at
    XC = r("XC", [P, TOK])
    XD = r("XD", [P, 9, P])
    XW = r("XW", [P, 9, P])
    YT = XW
    ST = r("ST", [P, 9, P])
    rows_end = r.at
    r = Region(c_phase, end - base)
    MASKT = r("MASKT", [P, P])
    CST = r("CST", [P, 6, XBC_TILES])
    SEL = r("SEL", [HEADS_B, 2, P])
    DECB = r("DECB", [P, HEADS_B, 9])
    DECR = r("DECR", [HEADS_B, HEADS_B, 9])
    TOKQ = r("TOKQ", [P, 4, 9, HEADS_B])
    FS = r("FS", [P, 2, P])
    FSO = r("FSO", [P, 2, P])
    SI = r("SI", [P, P])
    ZS = r("ZS", [P, TOK])
    CSO = r("CSO", [6 * XBC_TILES, P])
    r = Region(rows_at, rows_end)
    RW = [r(f"DTROW{i}", [HEADS_B, TOK]) for i in range(4)]
    r = Region(A_R5, A_W)
    RW += [r(f"DTROW{i}", [HEADS_B, TOK]) for i in range(4, 8)]
    YB = at("YB", A_R5, [P, 8, TOK])

    V = at("V", A_R3, [P, 8, 9 * P])
    YA = at("YA", A_R3, [P, 8, 9 * P])
    r = Region(A_R4, A_R5)
    VG = r("VG", [P, TOK])
    GVB = r("GVB", [P, A_GROUPS, 2 * P])
    vs_at = r.at
    SQV = r("SQV", [P, 9, 2 * P])
    VS = at("VS", vs_at, [P, 9, P])
    WS = r("WS", [P, A_GROUPS, P])
    WT = r("WT", [P, A_GROUPS, P])
    BSB = r("BSB", [P, A_GROUPS, P])
    UG = r("UG", [P, TOK])
    ZG = r("ZG", [P, TOK])
    r = Region(c_phase, end - base)
    TMP = r("TMP", [P, TOK])
    RSY = r("RSY", [P, 2, TOK])
    GSM = r("GSM", [P, 4, 16])

    YAH = at("YAH", A_R4, [P, 8, TOK], f32r)
    YAL = at("YAL", A_R5, [P, 8, TOK], f32r)
    O0 = at("O0", A_R3, [P, 8, TOK])
    XS2 = at("XS2", A_R4, [P, NB + 1, D])
    RSO = RSY[:, 0, :]
    SQA = RSY[:, 1, :]
    O1 = at("O1", A_R5, [P, 8, TOK])
    YO = at("YO", A_R4, [P, 2, 9, P])

    Y1 = at("Y1", A_R5, [P, 8, TOK])
    r = Region(A_R4, A_R5)
    QT = r("QT", [P, TOK])
    KALL = r("KALL", [P, KEYS])
    VTOK = r("VTOK", [P, 11, P])
    NFB = r("NFB", [P, KEYS])
    KTOK = at("KTOK", r.at - 4 * KEYS, [P, 9, P])
    SB = r("SB", [P, SEQ])
    PT = r("PT", [P, NB, P])
    ZSB = r("ZSB", [P, TOK])
    r = Region(A_R4, A_R5)
    FW = [r(f"FROW{i}", [HEADS_C, TOK]) for i in range(6)]
    r = Region(A_R5, A_W)
    LROW = r("LROW", [HEADS_C, KEYS])
    ONEROW = r("ONEROW", [HEADS_C, KEYS])
    LT = r("LT", [P, 9, HEADS_C])
    CLT = r("CLT", [P, 2, HEADS_C])
    r = Region(c_phase, end - base)
    TMPQ = r("TMPQ", [P, TOK])
    NFROW = r("NFROW", [HEADS_C, KEYS])
    SEL8 = r("SEL8", [HEADS_C, P])
    MASKD = r("MASKD", [P, P])
    KC = r("KC", [P, 2, P])

    PB = [ctx.enter_context(nc.psum_tensor(f"PB{i}", [P, 512], f32)) for i in range(8)]

    w_even = w_in_even[0].rearrange("(k p) e -> p k e", p=P)
    w_oe = w_out_even[0].rearrange("(s k p) e -> s p k e", s=2, p=P)
    w_odd = w_in_odd[0].rearrange("(k p) e -> p k e", p=P)
    w_oo = w_out_odd[0].rearrange("(k p) e -> p k e", p=P)
    xp = x_prompt[0].rearrange("(b p) d -> p b d", p=P)
    yp = y_prompt[0].rearrange("(b p) d -> p b d", p=P)

    block = ctx.enter_context(nc.Block())


    @block.sync
    def _(sp):
        def load_w(w, src, cols=P):
            if not isinstance(w[2], int) or w[0] + w[1] * w[2] >= 2:
                sp.wait_ge(S("w_low"), times(w, 1, -1))
            sp.dma_start(WRAW[:, slot(w), :, 0:cols], src).then_inc(S(f"w_raw{slot(w)}"), 16)

        def even(col, n=P):
            return w_even[:, :, bass.ds(col, n)]

        for i, (src, rows) in enumerate([
                (norm_pre[0].rearrange("(k p) -> k p", p=P), (PRE0, 8)),
                (norm_post[0].rearrange("(k p) -> k p", p=P), (POST0, 8)),
                (norm_pre[1].rearrange("(k p) -> k p", p=P), (PRE1, 8)),
                (norm_post[1].rearrange("(k p) -> k p", p=P), (POST1, 8)),
                (ssd_norm_g[0].rearrange("(k p) -> k p", p=P), (GSSD, 8)),
                (conv_b[0].rearrange("(k p) -> k p", p=P), (CONVB, XBC_TILES)),
                (gq[0:1, :], (GQ, 1)), (gk[0:1, :], (GK, 1)),
                (state_conv[0, 0].rearrange("r (k p) -> (r k) p", p=P), (CTX, 36))]):
            sp.dma_start(ROWS[rows[0]:rows[0] + rows[1], :], src).then_inc(S("rows_in"), 16)
        sp.dma_start(DSM[:, :], ssd_d[0].rearrange("(t j) -> t j", j=2)).then_inc(S("rows_in"), 16)
        for b in range(NB):
            sp.dma_start(XS[:, b, :], xp[:, b, :]).then_inc(S(f"x_in{b}"), 16)
            if b == 1:
                load_w(tile_no(W_BC, 1, 0), even(XBC0 + 8 * P))
        sp.dma_start(XS[0:DEC, NB, :], x_sample[0]).then_inc(S(f"x_in{NB}"), 16)
        sp.dma_start(CONVW_SB[:, :, :], conv_w[0].rearrange("(t p) k -> p t k", p=P)).then_inc(S("par_in"), 16)
        sp.dma_start(DTB[0:HEADS_B, :], dt_bias[0].unsqueeze(1)).then_inc(S("par_in"), 16)
        sp.dma_start(AL[0:HEADS_B, :], a_log[0].unsqueeze(1)).then_inc(S("par_in"), 16)
        sp.dma_start(BF[0:HEADS_C, :], b_forget[0].unsqueeze(1)).then_inc(S("par_in"), 16)
        for j in range(1, 4):
            load_w(tile_no(W_BC, 1, j), even(XBC0 + (8 + j) * P))
        load_w(tile_no(W_DT, 1, 0), even(DT0, HEADS_B), HEADS_B)

        def states_out(t):
            sp.wait_ge(S("fs_out"), t + 1)
            for j, dst in enumerate((ssd_prompt, ssd_sample)):
                sp.dma_start(dst[0, 0].rearrange("(t h) p n -> t (h p) n", h=2)[t], FSO[:, j, :]) \
                    .then_inc(S("ssd_stored"), 16)

        def pair_loads(t):
            load_w(tile_no(W_XZ, 2, t), even(XBC0 + P * t))
            load_w(tile_no(W_XZ + 1, 2, t), even(3 * D + P * t))
            if not isinstance(t, int) or t > 0:
                sp.wait_ge(S("si_used"), t)
            sp.dma_start(SI[:, :], state_ssd[0, 0].rearrange("(t h) p n -> t (h p) n", h=2)[t]) \
                .then_inc(S("si_in"), 16)

        pair_loads(0)
        with sp.Fori(1, 8) as t:
            pair_loads(t)
            states_out(t - 1)
        load_w(tile_no(W_V, 1, 0), even(D))
        load_w(tile_no(W_V, 1, 1), even(D + P))
        states_out(7)
        sp.wait_ge(S("cso"), 1)
        for j, dst in enumerate((conv_prompt, conv_sample)):
            for q in range(3):
                sp.dma_start(dst[0, 0, q].rearrange("(t p) -> t p", p=P),
                             CSO[(3 * j + q) * XBC_TILES:(3 * j + q + 1) * XBC_TILES, :]).then_inc(S("conv_stored"), 16)
        sp.wait_ge(S("yb"), 8)
        sp.wait_ge(S("y_turn"), 24)
        sp.dma_start(GVB[:, :, :].rearrange("p g k -> p (g k)"),
                     gmlp_gv[0:1].rearrange("a g k -> a (g k)").broadcast_to([P, D])).then_inc(S("gv_in"), 16)
        sp.dma_start(BSB[:, :, :].rearrange("p g k -> p (g k)"),
                     gmlp_bs[0:1].rearrange("a g k -> a (g k)").broadcast_to([P, A_GROUPS * P])).then_inc(S("gv_in"), 16)
        sp.dma_start(WS[:, :, :], gmlp_ws[0].rearrange("g i j -> i g j")).then_inc(S("gv_in"), 16)
        with sp.Fori(1, 4) as i:
            for j in range(2):
                load_w(tile_no(W_V + j, 2, i), even(D + P * j + 2 * P * i))
        load_w(tile_no(W_UZ, 1, 0), even(0))
        load_w(tile_no(W_UZ, 1, 1), even(2 * D))
        sp.wait_ge(S("v_normed"), 4)
        sp.dma_start(gv_sample[0, 0].rearrange("t (k f) -> t k f", f=P), V[0:DEC, :, NB * P:]) \
            .then_inc(S("gv_stored"), 16)
        with sp.Fori(1, 8) as t:
            load_w(tile_no(W_UZ, 2, t), even(P * t))
            load_w(tile_no(W_UZ + 1, 2, t), even(2 * D + P * t))
        with sp.Fori(0, 8) as n:
            load_w(tile_no(W_OE, 2, n), w_oe[1][:, :, bass.ds(P * n, P)])
            load_w(tile_no(W_OE + 1, 2, n), w_oe[0][:, :, bass.ds(P * (n + 1) - P, P)])

        def qkvz(h, j):
            load_w(tile_no(W_QKVZ + j, 4, h), w_odd[:, :, bass.ds(D * j + P * h, P)])

        load_w(tile_no(W_F, 1, 0), w_odd[:, :, 4 * D:4 * D + HEADS_C], HEADS_C)
        qkvz(0, 0)
        sp.wait_ge(S("p_chunk"), 3 * W_F)
        for b in range(NB):
            sp.dma_start(XS2[:, b, :], xp[:, b, :]).then_inc(S(f"x_in{b}"), 16)
        sp.dma_start(XS2[0:DEC, NB, :], x_sample[0]).then_inc(S(f"x_in{NB}"), 16)
        sp.wait_ge(S("x_turn"), 8)
        sp.dma_start(CLT[:, :, :], cache_logf[0, 0].rearrange("(b p) h -> p b h", p=P)).then_inc(S("clf_in"), 16)
        qkvz(0, 1)
        sp.wait_ge(S("lt"), 1)
        sp.dma_start(logf_prompt[0, 0].rearrange("(b p) h -> p b h", p=P), LT[:, 0:NB, :]).then_inc(S("lf_stored"), 16)
        sp.dma_start(logf_sample[0, 0], LT[0:DEC, NB, :]).then_inc(S("lf_stored"), 16)

        def out_odd_w(i, j):
            load_w(tile_no(W_OO + j, 2, i), w_oo[:, :, bass.ds(P * j + 2 * P * i, P)])

        def head_cols(h):
            return bass.ds(P * (h + 3) - 3 * P, P)

        def head(h, last=False):
            qkvz(h, 2)
            if isinstance(h, int) and h == 0:
                sp.wait_ge(S("lt"), 1)
            else:
                sp.wait_ge(S("y_read"), 9 * h)
                sp.wait_ge(S("v_stored"), 32 * (h + 1) - 32)
            for past, there, sem in ((cache_k, KC[:, :, :], "kc_in"), (cache_v, VTOK[:, NB:NB + 2, :], "vc_in")):
                sp.dma_start(there, past[0, 0].rearrange("(b p) h d -> p b (h d)", p=P)[:, :, head_cols(h)]) \
                    .then_inc(S(sem), 16)
            qkvz(h, 3)
            for j in range(2):
                out_odd_w(0, j) if last else qkvz(h + 1, j)
            sp.wait_ge(S("vt_read"), 3 * h + 3)
            sp.dma_start(v_prompt[0, 0].rearrange("(b p) h d -> p b (h d)", p=P)[:, :, head_cols(h)], VTOK[:, 0:NB, :]) \
                .then_inc(S("v_stored"), 16)
            sp.dma_start(v_sample[0, 0].rearrange("t h d -> t (h d)")[:, head_cols(h)], VTOK[0:DEC, NB + 2, :]).then_inc(S("v_stored"), 16)
            sp.wait_ge(S("k_tok"), 3 * h + 3)
            sp.dma_start(k_prompt[0, 0].rearrange("(b p) h d -> p b (h d)", p=P)[:, :, head_cols(h)], KTOK[:, 0:NB, :]) \
                .then_inc(S("k_stored"), 16)
            sp.dma_start(k_sample[0, 0].rearrange("t h d -> t (h d)")[:, head_cols(h)], KTOK[0:DEC, NB, :]).then_inc(S("k_stored"), 16)

        head(0)
        with sp.Fori(1, 7) as h:
            head(h)
        head(7, last=True)
        with sp.Fori(1, 4) as i:
            for j in range(2):
                out_odd_w(i, j)
        for k in range(8):
            sp.wait_ge(S("y_tok"), 3 * k + 3)
            sp.dma_start(yp[:, :, k * P:(k + 1) * P], YO[:, k % 2, 0:NB, :]).then_inc(S(f"y_stored{k % 2}"), 16)
            sp.dma_start(y_sample[0][:, k * P:(k + 1) * P], YO[0:DEC, k % 2, NB, :]).then_inc(S(f"y_stored{k % 2}"), 16)
        for name, n in (("ssd_stored", 16), ("conv_stored", 6), ("gv_stored", 1), ("lf_stored", 2),
                        ("k_stored", 16), ("v_stored", 16), ("y_stored0", 8), ("y_stored1", 8)):
            sp.wait_ge(S(name), 16 * n)

    @block.gpsimd
    def _(pool):
        order = Order(pool, S("pool_order"))

        def split_low(w):
            pool.wait_ge(S("w_high"), times(w, 1, 1))
            if not isinstance(w[2], int) or w[0] + w[1] * w[2] >= 2:
                pool.wait_ge(S("p_chunk"), times(w, 3, -3))
            pool.tensor_tensor(WL[:, slot(w), :, :], WRAW[:, slot(w), :, :], WH[:, slot(w), :, :].bitcast(f32),
                               ALU.subtract).then_inc(S("w_low"), 1)

        def split_lows(ws):
            for w in ws:
                split_low(w)

        order(pool.memset(IDENT[:, :], 0.0))
        order.fence()
        order(pool.affine_select(out=IDENT[:, :], in_=IDENT[:, :], compare_op=ALU.not_equal, fill=1.0, base=0,
                                 pattern=[[-1, P]], channel_multiplier=1))
        order(pool.memset(MASKT[:, :], 0.0))
        order.fence()
        pool.affine_select(out=MASKT[:, :], in_=MASKT[:, :], compare_op=ALU.is_ge, fill=NEG, base=0,
                           pattern=[[1, P]], channel_multiplier=-1).then_inc(S("masks"), 1)
        for w in range(W_XZ):
            split_low(tile_no(w, 1, 0))
        with pool.Fori(0, 8) as t:
            split_lows([tile_no(W_XZ + j, 2, t) for j in range(2)])
        with pool.Fori(0, 4) as i:
            split_lows([tile_no(W_V + j, 2, i) for j in range(2)])
        with pool.Fori(0, 8) as t:
            split_lows([tile_no(W_UZ + j, 2, t) for j in range(2)])
        with pool.Fori(0, 8) as n:
            split_lows([tile_no(W_OE + j, 2, n) for j in range(2)])
        split_low(tile_no(W_F, 1, 0))
        pool.wait_ge(S("h1_lo"), 8)
        order(pool.memset(MASKD[:, :], 0.0))
        order.fence()
        pool.affine_select(out=MASKD[:, :], in_=MASKD[:, :], compare_op=ALU.is_ge, fill=NEGBIG, base=0,
                           pattern=[[-1, P]], channel_multiplier=1).then_inc(S("masks"), 1)
        with pool.Fori(0, 8) as h:
            split_lows([tile_no(W_QKVZ + j, 4, h) for j in range(4)])
        with pool.Fori(0, 4) as i:
            split_lows([tile_no(W_OO + j, 2, i) for j in range(2)])

    def sample_rows(b):
        return DEC if b == NB else P

    def span(b, n=1):
        return slice(b * P, b * P + (DEC if b == NB else n * P))

    def groups_before(b):
        return b if b < 4 else (4 + 2 * (b - 4) if b < NB else 12)

    @block.tensor
    def _(pe):
        def mm(out, lhsT, rhs, start=True, stop=True):
            return pe.matmul(out, lhsT, rhs, start=start, stop=stop)

        def turn(out, in_):
            n = in_.shape[0]
            return pe.transpose(out, in_, IDENT[0:n, 0:n])

        def key_wait(rows):
            if rows <= DEC:
                pe.wait_ge(S("masks"), 1)

        def project(w, u, hi, lo, start=True, stop=True, ready=None):
            pe.wait_ge(S("w_low"), times(w, 1, 1))
            for c in range(3):
                if start and not (isinstance(u[2], int) and u[0] + u[1] * u[2] == 0):
                    pe.wait_ge(S(f"c_read{c}"), times(u, 1, 0))
                cols = slice(c * CH, (c + 1) * CH)
                for k in range(KT):
                    if ready and c == 0:
                        pe.wait_ge(S(ready), k + 1)
                    wh, wl = WH[:, slot(w), k, :], WL[:, slot(w), k, :]
                    mm(PB[c][:, 0:CH], wh, hi[:, k, cols], start=start and k == 0, stop=False)
                    mm(PB[c][:, 0:CH], wh, lo[:, k, cols], start=False, stop=False)
                    last = mm(PB[c][:, 0:CH], wl, hi[:, k, cols], start=False, stop=stop and k == KT - 1)
                last.then_inc(S("p_chunk"), 1)

        pe.wait_ge(S("masks"), 1)
        pe.wait_ge(S("rows_in"), 160)
        turn(PB[3][:, 0:N_ROWS], ROWS[0:N_ROWS, :])
        pe.wait_ge(S("dexp"), 1)
        turn(PB[3][:, P:P + 8], DEXP[:, :, :].rearrange("t j p -> t (j p)")).then_inc(S("rows_turn"), 1)
        pe.wait_ge(S("cols"), 1)
        for q, (b0, nb, rows) in enumerate(QUADS):
            pe.wait_ge(S("xn"), b0 + nb)
            for k in range(KT):
                i = q * KT + k
                if i >= 4:
                    pe.wait_ge(S("h_lo"), i - 3)
                for j in range(nb):
                    last = turn(PB[3 + i % 4][:, j * P:j * P + rows], XS[0:rows, b0 + j, k * P:(k + 1) * P])
                last.then_inc(S("x_t"), 1)
        pe.wait_ge(S("h_lo"), 24)
        for w in range(W_XZ):
            project(tile_no(w, 1, 0), tile_no(w, 1, 0), HH, HL)

        pe.wait_ge(S("conv_act"), 4)
        n = 0
        for g in range(GROUPS_B):
            for b0, nb, rows in QUADS:
                for what in range(2):
                    if n >= 3:
                        pe.wait_ge(S("cb_read"), n - 2)
                    bank = PB[5 + n % 3]
                    for j in range(nb):
                        cols = slice((b0 + j) * P, (b0 + j) * P + rows)
                        if what == 0:
                            last = mm(bank[0:rows, j * P:j * P + rows], BT[:, g, cols], CT[:, g, cols])
                        else:
                            last = turn(bank[0:rows, j * P:(j + 1) * P], BT[:, g, cols])
                    last.then_inc(S("cb_mm"), 1)
                    n += 1

        pe.wait_ge(S("dt_rows"), 1)
        for i, row in enumerate((RW[0], RW[2], RW[3], ACSROW)):
            for b in range(NB + 1):
                out = PB[3] if i < 3 else PB[4]
                o = (i * 9 if i < 3 else 0) + b
                turn(out[0:sample_rows(b), o * HEADS_B:(o + 1) * HEADS_B], row[:, span(b)])
        mm(PB[4][:, 256:256 + 9 * HEADS_B], ONES[0:HEADS_B, :], DECR[:, :, :].rearrange("k h b -> k (h b)")) \
            .then_inc(S("dt_turn"), 1)

        def pair_front(g, t):
            pe.wait_ge(S("conv_act"), 5 + t)
            if isinstance(t, int) and t == 0:
                pe.wait_ge(S("tokq"), 1)
                pe.wait_ge(S("cb_read"), 12)
            else:
                pe.wait_ge(S("yf"), 3 * t)
            for q, (b0, nb, rows) in enumerate(QUADS):
                for j in range(nb):
                    last = turn(PB[3 + q][0:rows, j * P:(j + 1) * P], XC[:, (b0 + j) * P:(b0 + j) * P + rows])
                last.then_inc(S("xc_turn"), 1)
            pe.wait_ge(S("sel"), t + 1)

            def decay_rows(n):
                j, q = ((0, 0), (0, 1), (1, 0), (1, 1), (0, 2), (1, 2))[n]
                if n >= 2:
                    pe.wait_ge(S("seg"), 6 * t + n - 1)
                b0, nb, rows = QUADS[q]
                width = nb * rows
                mm(PB[6 + n % 2][:, 0:width], SEL[:, j, :], ACSROW[:, b0 * P:b0 * P + width]).then_inc(S("bc"), 1)

            decay_rows(0)
            decay_rows(1)
            for q, (b0, nb, rows) in enumerate(QUADS):
                pe.wait_ge(S("xw"), 3 * t + q + 1)
                if q == 2:
                    pe.wait_ge(S("si_in"), 16 * t + 16)
                    turn(PB[5][:, P:2 * P], SI[:, :]).then_inc(S("si_used"), 1)
                for j in range(nb):
                    last = mm(PB[3 + q][:, j * P:(j + 1) * P], BTOK[0:rows, g, b0 + j, :], XW[0:rows, b0 + j, :])
                last.then_inc(S("ds"), 1)
            for n in range(2, 6):
                decay_rows(n)
            pe.wait_ge(S("st"), t + 1)
            turn(PB[5][:, 2 * P:3 * P], FS[:, 0, :])
            turn(PB[5][:, 3 * P:4 * P], FS[:, 1, :]).then_inc(S("fs_turn"), 1)

        def pair_back(g, t):
            pe.wait_ge(S("m"), 6 * t + 6)
            pe.wait_ge(S("fs_out"), t + 1)
            for q, (b0, nb, rows) in enumerate(QUADS):
                intra, state = PB[(3, 5, 7)[q]], PB[(4, 6, 7)[q]]
                off = P if q == 2 else 0
                for j in range(nb):
                    b = b0 + j
                    for i in range(2):
                        mm(intra[0:rows, j * P + i * HP:j * P + (i + 1) * HP], M[0:rows, i, b, 0:rows],
                           XD[0:rows, b, i * HP:(i + 1) * HP])
                    last = mm(state[0:rows, off + j * P:off + (j + 1) * P], CT[:, g, b * P:b * P + rows], ST[:, b, :])
                last.then_inc(S("y_mm"), 1)
            for q, (b0, nb, rows) in enumerate(QUADS):
                if q < 2:
                    pe.wait_ge(S("yt"), 3 * t + (1 if q == 0 else 3))
                for j in range(nb):
                    last = turn(PB[3 + q][:, j * P:j * P + rows], YT[0:rows, b0 + j, :])
                last.then_inc(S("y_turn"), 1)

        for g in range(GROUPS_B):
            t0 = 4 * g
            xz = [tile_no(W_XZ + j, 2, t0) for j in range(2)]
            project(xz[0], xz[0], HH, HL)
            project(xz[1], xz[1], HH, HL)
            pair_front(g, t0)
            with pe.Fori(t0 + 1, t0 + 4) as t:
                xz = [tile_no(W_XZ + j, 2, t) for j in range(2)]
                project(xz[0], xz[0], HH, HL)
                pair_back(g, t - 1)
                project(xz[1], xz[1], HH, HL)
                pair_front(g, t)
            pair_back(g, t0 + 3)

        pe.wait_ge(S("yf"), 24)
        turn(PB[3][0:6 * XBC_TILES, 0:P], CST[:, :, :].rearrange("p r t -> p (r t)")).then_inc(S("cst_turn"), 1)

        with pe.Fori(0, 4) as i:
            vt = [tile_no(W_V + j, 2, i) for j in range(2)]
            project(vt[0], vt[0], HH, HL)
            project(vt[1], vt[1], HH, HL)
            pe.wait_ge(S("v_tok"), 6 * i)
            pe.wait_ge(S("cso"), 1)
            for j, src in enumerate((VG, UG)):
                pe.wait_ge(S("c_read2"), times(vt[j], 1, 1))
                for q, (b0, nb, rows) in enumerate(QUADS):
                    if j == 1 and q == 2:
                        pe.wait_ge(S("v_tok"), 6 * i + 1)
                    key_wait(rows)
                    for n in range(nb):
                        last = turn(PB[(3, 4, 5, 6, 7, 3)[3 * j + q]][0:rows, n * P:(n + 1) * P],
                                    src[:, (b0 + n) * P:(b0 + n) * P + rows])
                    last.then_inc(S("v_turn"), 1)
        pe.wait_ge(S("v_tok"), 24)
        for n in range(6):
            g, c = n // 3, n % 3
            pe.wait_ge(S("y_sq"), 4 + 4 * g)
            if n == 5:
                pe.wait_ge(S("gs_ms"), 1)
            mm(PB[(3, 4, 5, 6, 7, 3)[n]][:, 0:CH], ONES[:, :], RSY[:, g, c * CH:(c + 1) * CH]).then_inc(S("gs_mm"), 1)
        pe.wait_ge(S("gv_in"), 48)
        pe.wait_ge(S("gs_ms"), 4)
        for g in range(A_GROUPS):
            last = turn(PB[6][:, g * P:(g + 1) * P], WS[:, g, :])
        last.then_inc(S("ws_turn"), 1)
        pe.wait_ge(S("wt"), 1)
        with pe.Fori(0, 4) as i:
            for j in range(2):
                uz = [tile_no(W_UZ + 2 * j + n, 4, i) for n in range(2)]
                project(uz[0], uz[0], HH, HL)
                project(uz[1], uz[1], HH, HL)
                pe.wait_ge(S("vs"), 2 * i + j + 1)
                for q, (b0, nb, rows) in enumerate(QUADS):
                    if j > 0:
                        pe.wait_ge(S("s_read"), 6 * i + 3 * j - 3 + q + 1)
                    else:
                        pe.wait_ge(S("s_read"), 6 * i)
                    for n in range(nb):
                        last = mm(PB[3 + q][:, n * P:n * P + rows], VS[:, b0 + n, :], WT[:, i, 0:rows])
                    last.then_inc(S("s_mm"), 1)

        def out_sums(name, at_count):
            pe.wait_ge(S(name), at_count)
            for c in range(3):
                mm(PB[3 + c][:, 0:CH], ONES[:, :], SQA[:, c * CH:(c + 1) * CH]).then_inc(S("ss_mm"), 1)

        def out_even(n, first):
            pe_u = tile_no(W_OE, 1, n)
            project(tile_no(W_OE, 2, n), pe_u, HH, HL, stop=False, ready="yb_lo" if first else None)
            project(tile_no(W_OE + 1, 2, n), pe_u, YAH, YAL, start=False, ready="ya_lo" if first else None)

        out_even(0, True)
        with pe.Fori(1, 8) as n:
            out_even(n, False)
        pe.wait_ge(S("s_read"), 24)
        out_sums("o_sq", 8)
        for k in range(8):
            if k < 2:
                pe.wait_ge(S("ss_ms"), 3)
            else:
                pe.wait_ge(S("x1"), k - 1)
            for q, (b0, nb, rows) in enumerate(QUADS):
                bank = ((3, 4, 5), (6, 7, 0))[k % 2][q]
                for j in range(nb):
                    if k == 0:
                        pe.wait_ge(S(f"x_in{b0 + j}"), 32)
                    last = turn(PB[bank][:, j * P:j * P + rows], XS2[0:rows, b0 + j, k * P:(k + 1) * P])
            last.then_inc(S("x_turn"), 1)
        pe.wait_ge(S("x1"), 8)
        out_sums("x1_sq", 8)

        project(tile_no(W_F, 1, 0), tile_no(W_F - 8, 1, 0), HH, HL, ready="h1_lo")
        pe.wait_ge(S("clf_in"), 16)
        pe.wait_ge(S("ss_ms"), 6)
        for b in range(2):
            last = turn(PB[3][0:HEADS_C, b * P:(b + 1) * P], CLT[:, b, :])
        last.then_inc(S("clf_turn"), 1)
        pe.wait_ge(S("lrow"), 1)
        for b in range(NB + 1):
            cols = slice(SEQ + PAST, KEYS) if b == NB else span(b)
            last = turn(PB[4][0:sample_rows(b), b * HEADS_C:(b + 1) * HEADS_C], LROW[:, cols])
        last.then_inc(S("lt_turn"), 1)

        pe.wait_ge(S("masks"), 2)

        def square_sums(h, j):
            pe.wait_ge(S("n_sq"), 2 * h + j + 1)
            for c in range(3):
                last = mm(PB[3 + c][:, 0:CH], ONES[:, :], TMPQ[:, c * CH:(c + 1) * CH])
            last.then_inc(S("n_ss"), 1)

        def head(h):
            ws = [tile_no(W_QKVZ + j, 4, h) for j in range(4)]
            us = [tile_no(W_QKVZ - 8 + j, 4, h) for j in range(4)]
            if not isinstance(h, int):
                pe.wait_ge(S("y_read"), 9 * h)
            project(ws[0], us[0], HH, HL)
            project(ws[1], us[1], HH, HL)
            if isinstance(h, int):
                pe.wait_ge(S("lt"), 1)
            square_sums(h, 0)
            project(ws[2], us[2], HH, HL)
            pe.wait_ge(S("n_done"), 2 * h + 1)
            square_sums(h, 1)
            pe.wait_ge(S("c_read2"), times(us[2], 1, 1))
            for q, (b0, nb, rows) in enumerate(QUADS):
                bank, off = (6, 7, 3)[q], 0
                if q == 2:
                    pe.wait_ge(S("n_ms"), 2 * h + 2)
                key_wait(rows)
                for j in range(nb):
                    last = turn(PB[bank][0:rows, off + j * P:off + (j + 1) * P],
                                ZSB[:, (b0 + j) * P:(b0 + j) * P + rows])
                last.then_inc(S("vt_turn"), 1)
            project(ws[3], us[3], HH, HL)
            pe.wait_ge(S("n_done"), 2 * h + 2)
            for q, (b0, nb, rows) in enumerate(QUADS):
                pe.wait_ge(S("vt_read"), 3 * h + q + 1)
                key_wait(rows)
                bank, off = (6, 7, 3)[q], 0
                for j in range(nb):
                    c0 = SEQ + PAST if q == 2 else (b0 + j) * P
                    last = turn(PB[bank][0:rows, off + j * P:off + (j + 1) * P], KALL[:, c0:c0 + rows])
                last.then_inc(S("kt_turn"), 1)
            pe.wait_ge(S("kc_in"), 16 * h + 16)
            for b in range(2):
                last = turn(PB[4][:, b * P:(b + 1) * P], KC[:, b, :])
            last.then_inc(S("kc_turn"), 1)
            pe.wait_ge(S("sel8"), h + 1)
            pe.wait_ge(S("kc_done"), h + 1)
            pe.wait_ge(S("k_tok"), 3 * h + 3)
            for c in range(3):
                cols = slice(c * 512, min(KEYS, c * 512 + 512))
                last = mm(PB[3 + c][:, 0:cols.stop - cols.start], SEL8[:, :], NFROW[:, cols])
            last.then_inc(S("nf_mm"), 1)
            for c in range(3):
                pe.wait_ge(S(f"c_read{c}"), times(us[3], 1, 1))
            pe.wait_ge(S("nf"), h + 1)

            def scores(b):
                rows = sample_rows(b)
                banks = (3, 4) if b % 2 == 0 else (5, 6)
                if b >= 2:
                    pe.wait_ge(S("sm"), 9 * h + b - 1)
                q = QT[:, b * P:b * P + rows]
                key0, keys = (SEQ, PAST + DEC) if b == NB else (0, (b + 1) * P)
                for i, c0 in enumerate(range(0, keys, 512)):
                    c1 = min(c0 + 512, keys)
                    mm(PB[banks[i]][0:rows, 0:c1 - c0], q, KALL[:, key0 + c0:key0 + c1], stop=c1 < keys)
                last = mm(PB[banks[i]][0:rows, keys - rows - c0:keys - c0], IDENT[0:rows, 0:rows],
                          MASKD[0:rows, 0:rows], start=False)
                last.then_inc(S("sc_mm"), 1)

            def values(b):
                rows = sample_rows(b)
                blocks = [(j, j, P) for j in range(b + 1)] if b < NB else [(0, 8, P), (1, 9, P), (2, 10, DEC)]
                before = groups_before(b)
                pe.wait_ge(S("pn"), 9 * h + b + 1)
                pe.wait_ge(S("pt_read"), 13 * h + before)
                for g in range(0, len(blocks), 4):
                    for j, _, keys in blocks[g:g + 4]:
                        turned = P if keys == P else rows
                        last = turn(PB[g // 4][0:keys, (j % 4) * P:(j % 4) * P + turned],
                                    SB[0:turned, j * P:j * P + keys])
                    last.then_inc(S("p_turn"), 1)
                out = PB[2 if b % 2 == 0 else 7]
                pe.wait_ge(S("y_read"), 9 * h + b - 1) if b >= 2 else None
                pe.wait_ge(S("pt_read"), 13 * h + before + (len(blocks) + 3) // 4)
                for i, (j, src, keys) in enumerate(blocks):
                    last = mm(out[:, 0:rows], VTOK[0:keys, src, :], PT[0:keys, j, 0:rows],
                              start=i == 0, stop=i == len(blocks) - 1)
                last.then_inc(S("pv"), 1)

            scores(0)
            for b in range(NB):
                scores(b + 1)
                values(b)
            values(NB)

        head(0)
        with pe.Fori(1, 8) as h:
            head(h)

        def out_odd(i, j, ready=None):
            project(tile_no(W_OO + j, 2, i), tile_no(W_OO - 8 + j, 2, i), HH, HL, ready=ready)

        pe.wait_ge(S("y_read"), 72)
        out_odd(0, 0, "y1_lo")
        out_odd(0, 1)
        with pe.Fori(1, 4) as i:
            out_odd(i, 0)
            out_odd(i, 1)
        out_sums("o_sq", 16)
        pe.wait_ge(S("ss_ms"), 9)
        for k in range(8):
            pe.wait_ge(S("x2"), k + 1)
            for q, (b0, nb, rows) in enumerate(QUADS):
                if k >= 2:
                    pe.wait_ge(S("y_tok"), 3 * (k - 2) + q + 1)
                bank, off = ((3, 4, 5), (6, 7, 0))[k % 2][q], 0
                for j in range(nb):
                    last = turn(PB[bank][0:rows, off + j * P:off + (j + 1) * P],
                                O1[:, k, (b0 + j) * P:(b0 + j) * P + rows])
                last.then_inc(S("o_turn"), 1)

    @block.scalar
    def _(act):
        def copy(out, in_, scale=1.0):
            return act.activation(out, in_, ACT.Copy, scale=scale)

        order = Order(act, S("act_order"))

        def split_high(w):
            act.wait_ge(S(f"w_raw{slot(w)}"), loads_of_slot(w))
            if not isinstance(w[2], int) or w[0] + w[1] * w[2] >= 2:
                act.wait_ge(S("p_chunk"), times(w, 3, -3))
            copy(WH[:, slot(w), :, :], WRAW[:, slot(w), :, :]).then_inc(S("w_high"), 1)

        def read_chunks(w, outs, func=ACT.Copy, rows=P):
            for c in range(3):
                act.wait_ge(S("p_chunk"), times(w, 3, c + 1))
                for i, (cols, out) in enumerate(outs[c]):
                    last = act.activation(out, PB[c][0:rows, cols], func)
                last.then_inc(S(f"c_read{c}"), 1)

        def whole(t, rows=P):
            return [[(slice(0, CH), t[0:rows, c * CH:(c + 1) * CH])] for c in range(3)]

        def parted(t, prompt0, sample0):
            two = SEQ - 2 * CH
            return [[(slice(0, CH), t[:, prompt0:prompt0 + CH])],
                    [(slice(0, CH), t[:, prompt0 + CH:prompt0 + 2 * CH])],
                    [(slice(0, two), t[:, prompt0 + 2 * CH:prompt0 + SEQ]),
                     (slice(two, CH), t[:, sample0:sample0 + DEC])]]

        act.wait_ge(S("rows_turn"), 1)
        order(copy(COLS[:, :], PB[3][:, 0:N_ROWS]))
        copy(DCOL[:, :], PB[3][:, P:P + 8]).then_inc(S("cols"), 1)
        order.fence()
        for b in range(NB + 2):
            if b <= NB:
                rows = sample_rows(b)
                act.wait_ge(S(f"x_in{b}"), 16)
                if b > 0:
                    act.wait_ge(S("x_ss"), b)
                act.activation(SQJ[0:rows, :], XS[0:rows, b, :], ACT.Square, accum_out=SS[0:rows, b:b + 1]) \
                    .then_inc(S("x_ss"), 1)
            if b == 0:
                continue
            b -= 1
            rows = sample_rows(b)
            act.wait_ge(S("x_ms"), b + 1)
            act.activation(RT[0:rows, b:b + 1], MS[0:rows, b:b + 1], ACT.Sqrt).then_inc(S("x_rt"), 1)
        for w in range(2):
            split_high(tile_no(w, 1, 0))
        for q, (b0, nb, rows) in enumerate(QUADS):
            for k in range(KT):
                i = q * KT + k
                act.wait_ge(S("x_t"), i + 1)
                act.activation(HH[:, k, b0 * P:b0 * P + nb * rows], PB[3 + i % 4][:, 0:nb * rows], ACT.Copy,
                               scale=COLS[:, PRE0 + k:PRE0 + k + 1]).then_inc(S("h_hi"), 1)

        def conv_silu(n, out):
            act.wait_ge(S("conv"), n + 1)
            order(act.activation(out[:, 0:SEQ], ACC[:, 0:SEQ], ACT.Silu))
            act.activation(out[:, SEQ:TOK], ACC[:, SEQ + 3:CONVW], ACT.Silu).then_inc(S("conv_act"), 1)

        for j in range(4):
            w = tile_no(W_BC, 1, j)
            if j > 0:
                act.wait_ge(S("conv"), j)
            read_chunks(w, parted(XR, 3, SAMP))
            split_high(tile_no(W_BC, 1, j + 2))
            conv_silu(j, (BT, CT)[j // 2][:, j % 2, :])
        w = tile_no(W_DT, 1, 0)
        read_chunks(w, whole(RW[4], HEADS_B), rows=HEADS_B)
        split_high(tile_no(W_DT + 2, 1, 0))
        n = 0
        for g in range(GROUPS_B):
            for b0, nb, rows in QUADS:
                for what in range(2):
                    act.wait_ge(S("cb_mm"), n + 1)
                    width = rows if what == 0 else P
                    dst = (CBT, BTOK)[what][0:rows, g, b0:b0 + nb, 0:width]
                    src = PB[5 + n % 3][0:rows, 0:nb * P].rearrange("p (b c) -> p b c", c=P)[:, :, 0:width]
                    copy(dst, src).then_inc(S("cb_read"), 1)
                    n += 1

        def log1p_exp_steps(rows, neg, e, w1, lg, name, first):
            act.wait_ge(S(name), first)
            act.activation(e, neg, ACT.Exp).then_inc(S(name + "_a"), 1)
            act.wait_ge(S(name), first + 1)
            act.activation(lg, w1, ACT.Ln).then_inc(S(name + "_a"), 1)

        log1p_exp_steps(HEADS_B, RW[5][:, :], RW[6][:, :], RW[1][:, :], RW[2][:, :], "dtc", 1)
        act.wait_ge(S("par_in"), 64)
        act.activation(EAL[0:HEADS_B, :], AL[0:HEADS_B, :], ACT.Exp).then_inc(S("dtc_a"), 1)
        act.wait_ge(S("dtc"), 3)
        order(act.activation(RW[5][:, :], RW[5][:, :], ACT.Exp))
        act.activation(RW[3][:, :], ACSROW[:, :], ACT.Exp).then_inc(S("dtc_a"), 1)
        act.wait_ge(S("dt_turn"), 1)
        b3 = PB[3][:, 0:3 * 9 * HEADS_B].rearrange("p (q b h) -> p q b h", q=3, h=HEADS_B)
        b4 = PB[4][:, 0:9 * HEADS_B].rearrange("p (b h) -> p b h", h=HEADS_B)
        order(copy(TOKQ[:, 0:3, 0:NB, :], b3[:, :, 0:NB, :]))
        order(copy(TOKQ[0:DEC, 0:3, NB, :], b3[0:DEC, :, NB, :]))
        order(copy(TOKQ[:, 3, 0:NB, :], b4[:, 0:NB, :]))
        order(copy(TOKQ[0:DEC, 3, NB, :], b4[0:DEC, NB, :]))
        copy(DECB[:, :, :].rearrange("p h b -> p (h b)"), PB[4][:, 256:256 + 9 * HEADS_B]).then_inc(S("tokq"), 1)

        def read_x(t):
            act.wait_ge(S("conv"), 4 + t)
            read_chunks(tile_no(W_XZ, 2, t), parted(XR, 3, SAMP))
            split_high(tile_no(W_XZ + 2, 2, t))

        def read_gate(t):
            if isinstance(t, int) and t == 0:
                act.wait_ge(S("dt_rows"), 1)
                act.wait_ge(S("dt_turn"), 1)
            else:
                act.wait_ge(S("yb"), t)
            conv_silu(4 + t, XC)
            read_chunks(tile_no(W_XZ + 1, 2, t), whole(ZS), ACT.Silu)
            split_high(tile_no(W_XZ + 3, 2, t))

        def front(t):
            for n, (j, q) in enumerate(((0, 0), (0, 1), (1, 0), (1, 1), (0, 2), (1, 2))):
                b0, nb, rows = QUADS[q]
                act.wait_ge(S("seg"), 6 * t + n + 1)
                m = M[0:rows, j, b0:b0 + nb, 0:rows]
                act.activation(m, m, ACT.Exp).then_inc(S("mexp"), 1)
            act.wait_ge(S("fs_turn"), t + 1)
            if not isinstance(t, int) or t > 0:
                act.wait_ge(S("ssd_stored"), 32 * t)
            copy(FSO[:, :, :].rearrange("p j n -> p (j n)"), PB[5][:, 2 * P:4 * P]).then_inc(S("fs_out"), 1)

        read_x(0)
        read_gate(0)
        front(0)
        with order.loop(1, 8, 1) as t:
            read_x(t)
            read_gate(t)
            front(t)
        act.wait_ge(S("cst_turn"), 1)
        copy(CSO[:, :], PB[3][0:6 * XBC_TILES, 0:P]).then_inc(S("cso"), 1)
        act.wait_ge(S("yb"), 8)
        act.wait_ge(S("y_turn"), 24)

        def roots(src, name, at_count, done):
            act.wait_ge(S(name), at_count)
            act.activation(src, src, ACT.Sqrt).then_inc(S(done), 1)

        with order.loop(0, 4, 0) as i:
            act.wait_ge(S("v_turn"), 6 * i)
            for j, out in enumerate((VG, UG)):
                w = tile_no(W_V + j, 2, i)
                read_chunks(w, whole(out), ACT.Gelu)
                split_high(tile_no(W_V + j + 2, 2, i))
            roots(GSM[:, 2, 0:9], "v_ms", i + 1, "v_rt")
        roots(RSY[:, :, :].rearrange("p g c -> p (g c)"), "gs_ms", 6, "gs_rt")
        with order.loop(0, 8, 0) as t:
            act.wait_ge(S("ya"), t)
            read_chunks(tile_no(W_UZ, 2, t), whole(UG), ACT.Gelu)
            split_high(tile_no(W_UZ + 2, 2, t))
            read_chunks(tile_no(W_UZ + 1, 2, t), whole(ZG), ACT.Silu)
            split_high(tile_no(W_UZ + 3, 2, t))
        for k in range(8):
            act.wait_ge(S("yb_x"), k + 1)
            copy(HH[:, k, :], HX[:, k, :]).then_inc(S("hi"), 1)
        act.wait_ge(S("ya"), 8)
        for k in range(8):
            copy(YAH[:, k, :], YA[:, k, 0:TOK]).then_inc(S("ya_hi"), 1)
        with order.loop(0, 8, 0) as n:
            w0, w1 = tile_no(W_OE, 2, n), tile_no(W_OE + 1, 2, n)
            split_high(tile_no(W_OE + 2, 2, n))
            read_chunks(w1, whole(O0[:, n, :]))
            split_high(tile_no(W_OE + 3, 2, n))
        roots(RSO, "ss_ms", 3, "ss_rt")
        for k in range(8):
            act.wait_ge(S("x1"), k + 1)
            if k > 0:
                act.wait_ge(S("x1_sq"), k)
            act.activation(TMP[:, :], O0[:, k, :], ACT.Square).then_inc(S("x1_s"), 1)
        roots(RSO, "ss_ms", 6, "ss_rt")
        for k in range(8):
            act.wait_ge(S("h1_x"), k + 1)
            copy(HH[:, k, :], HX[:, k, :]).then_inc(S("hi"), 1)

        read_chunks(tile_no(W_F, 1, 0), whole(FW[0], HEADS_C), rows=HEADS_C)
        split_high(tile_no(W_F + 2, 1, 0))
        log1p_exp_steps(HEADS_C, FW[2][:, :], FW[3][:, :], FW[4][:, :], FW[5][:, :], "fc", 1)

        def norm_steps(h, j, parts):
            if j == 1:
                act.wait_ge(S("n_done"), 2 * h + 1)
            for n, (src, dst) in enumerate(parts):
                last = act.activation(dst, src, ACT.Square)
            last.then_inc(S("n_sq"), 1)

        def norm_root(h, j):
            act.wait_ge(S("n_ms"), 2 * h + j + 1)
            act.activation(TMPQ[:, :], TMPQ[:, :], ACT.Sqrt).then_inc(S("n_rt"), 1)

        def head(h):
            ws = [tile_no(W_QKVZ + j, 4, h) for j in range(4)]
            nxt = [tile_no(W_QKVZ + 2 + j, 4, h) for j in range(4)]
            if isinstance(h, int):
                act.wait_ge(S("lt"), 1)
            else:
                act.wait_ge(S("y_read"), 9 * h)
            read_chunks(ws[0], whole(QT))
            act.wait_ge(S("c_read2"), 55 + 4 * h)
            norm_steps(h, 0, [(QT[:, :], TMPQ[:, :])])
            split_high(nxt[0])
            norm_root(h, 0)
            read_chunks(ws[1], parted(KALL, 0, SEQ + PAST))
            act.wait_ge(S("c_read2"), 56 + 4 * h)
            norm_steps(h, 1, [(KALL[:, 0:SEQ], TMPQ[:, 0:SEQ]), (KALL[:, SEQ + PAST:KEYS], TMPQ[:, SEQ:TOK])])
            split_high(nxt[1])
            read_chunks(ws[2], whole(ZSB))
            split_high(nxt[2])
            norm_root(h, 1)
            if not isinstance(h, int):
                act.wait_ge(S("v_stored"), 32 * h)
            for q, (b0, nb, rows) in enumerate(QUADS):
                bank, off = (6, 7, 3)[q], 0
                act.wait_ge(S("vt_turn"), 3 * h + q + 1)
                v0 = NB + 2 if q == 2 else b0
                copy(VTOK[0:rows, v0:v0 + nb, :],
                     PB[bank][0:rows, off:off + nb * P].rearrange("p (b d) -> p b d", d=P)).then_inc(S("vt_read"), 1)
            read_chunks(ws[3], whole(ZSB), ACT.Silu)
            split_high(nxt[3])
            for q, (b0, nb, rows) in enumerate(QUADS):
                bank, off = (6, 7, 3)[q], 0
                act.wait_ge(S("kt_turn"), 3 * h + q + 1)
                copy(KTOK[0:rows, b0:b0 + nb, :],
                     PB[bank][0:rows, off:off + nb * P].rearrange("p (b d) -> p b d", d=P)).then_inc(S("k_tok"), 1)
            act.wait_ge(S("kc_turn"), h + 1)
            copy(KALL[:, SEQ:SEQ + PAST], PB[4][:, 0:PAST]).then_inc(S("kc_done"), 1)
            act.wait_ge(S("nf_mm"), h + 1)
            act.wait_ge(S("k_stored"), 32 * h + 32)
            for c in range(3):
                c0, c1 = c * 512, min(KEYS, c * 512 + 512)
                last = copy(NFB[:, c0:c1], PB[3 + c][:, 0:c1 - c0])
            last.then_inc(S("nf"), 1)
            for b in range(NB + 1):
                rows = sample_rows(b)
                width = PAST + DEC if b == NB else (b + 1) * P
                act.wait_ge(S("sm"), 9 * h + b + 1)
                act.activation(SB[0:rows, 0:width], SB[0:rows, 0:width], ACT.Exp, scale=SCALE,
                               bias=NBIAS[0:rows, :], accum_out=RSUM[0:rows, :]).then_inc(S("ex"), 1)
                blocks = b + 1 if b < NB else 3
                for g in range(0, blocks, 4):
                    nb = min(4, blocks - g)
                    act.wait_ge(S("p_turn"), 13 * h + groups_before(b) + g // 4 + 1)
                    if g == 0:
                        act.wait_ge(S("pv"), 9 * h + b)
                    bank = PB[g // 4]
                    if b < NB:
                        last = copy(PT[:, g:g + nb, :], bank[:, 0:nb * P].rearrange("p (b l) -> p b l", l=P))
                    else:
                        src = bank[:, 0:3 * P].rearrange("p (b l) -> p b l", l=P)
                        copy(PT[:, 0:2, 0:DEC], src[:, 0:2, 0:DEC])
                        last = copy(PT[0:DEC, 2, 0:DEC], src[0:DEC, 2, 0:DEC])
                    last.then_inc(S("pt_read"), 1)

        head(0)
        with act.Fori(1, 8) as h:
            head(h)
        act.wait_ge(S("y_read"), 72)
        for k in range(8):
            copy(HH[:, k, :], Y1[:, k, :]).then_inc(S("hi"), 1)

        def out_odd(i, j, more):
            n = tile_no(W_OO + j, 2, i)
            k = 2 * i + j
            read_chunks(n, whole(O1[:, k, :]))
            if more:
                split_high(tile_no(W_OO + j + 2, 2, i))

        act.wait_ge(S("y1_lo"), 8)
        with act.Fori(0, 3) as i:
            out_odd(i, 0, True)
            out_odd(i, 1, True)
        out_odd(3, 0, False)
        out_odd(3, 1, False)
        roots(RSO, "ss_ms", 9, "ss_rt")
        for k in range(8):
            for q, (b0, nb, rows) in enumerate(QUADS):
                bank, off = ((3, 4, 5), (6, 7, 0))[k % 2][q], 0
                act.wait_ge(S("o_turn"), 3 * k + q + 1)
                if q == 0 and k >= 2:
                    act.wait_ge(S(f"y_stored{k % 2}"), 32 * (k // 2))
                copy(YO[0:rows, k % 2, b0:b0 + nb, :],
                     PB[bank][0:rows, off:off + nb * P].rearrange("p (b d) -> p b d", d=P)).then_inc(S("y_tok"), 1)

    @block.vector
    def _(dve):
        order = Order(dve, S("dve_order"))

        def tt(out, a, b, op):
            return dve.tensor_tensor(out, a, b, op)

        def ts(out, a, s1, s2, op0, op1=ALU.bypass):
            return dve.tensor_scalar(out, a, s1, s2, op0, op1) if s2 is not None else \
                dve.tensor_scalar(out, a, s1, None, op0)

        def stt(out, a, s, b, op0, op1):
            return dve.scalar_tensor_tensor(out=out, in0=a, scalar=s, in1=b, op0=op0, op1=op1)

        order(dve.memset(ONES[:, :], 1.0))
        dve.wait_ge(S("rows_in"), 160)
        dve.tensor_copy(DEXP[:, :, :], DSM[:, :].unsqueeze(2).broadcast_to([8, 2, HP])).then_inc(S("dexp"), 1)
        for b in range(NB + 2):
            if b <= NB:
                rows = sample_rows(b)
                dve.wait_ge(S("x_ss"), b + 1)
                ts(MS[0:rows, b:b + 1], SS[0:rows, b:b + 1], 1.0 / D, EPS, ALU.mult, ALU.add).then_inc(S("x_ms"), 1)
            if b == 0:
                continue
            b -= 1
            rows = sample_rows(b)
            dve.wait_ge(S("x_rt"), b + 1)
            order(dve.reciprocal(RR[0:rows, b:b + 1], RT[0:rows, b:b + 1]))
            order.fence()
            ts(XS[0:rows, b, :], XS[0:rows, b, :], RR[0:rows, b:b + 1], None, ALU.mult).then_inc(S("xn"), 1)
        for q, (b0, nb, rows) in enumerate(QUADS):
            for k in range(KT):
                i = q * KT + k
                cols = slice(b0 * P, b0 * P + nb * rows)
                dve.wait_ge(S("h_hi"), i + 1)
                stt(HL[:, k, cols], PB[3 + i % 4][:, 0:nb * rows], COLS[:, PRE0 + k:PRE0 + k + 1],
                    HH[:, k, cols].bitcast(f32), ALU.mult, ALU.subtract).then_inc(S("h_lo"), 1)

        def conv(n, tile, w):
            dve.wait_ge(S("c_read2"), times(w, 1, 1))
            if not isinstance(n, int) or n > 0:
                dve.wait_ge(S("conv_act"), n)
            past = COLS[:, CTX:CTX + 36].rearrange("p (r t) -> p r t", t=XBC_TILES)
            order(dve.tensor_copy(XR[:, 3 + SEQ:SAMP], past[:, :, tile]))
            order(dve.tensor_copy(CST[:, 0:3, tile], XR[:, SEQ:SEQ + 3]))
            order(dve.tensor_copy(CST[:, 3:6, tile], XR[:, SAMP + DEC - 3:SAMP + DEC]))
            order.fence()
            taps = CONVW_SB[:, tile, :]
            order(ts(ACC[:, :], XR[:, 0:CONVW], taps[:, 0:1], COLS[:, CONVB:CONVB + XBC_TILES][:, bass.ds(tile, 1)],
                     ALU.mult, ALU.add))
            for k in range(1, TAPS):
                order.fence()
                ins = stt(ACC[:, :], XR[:, k:k + CONVW], taps[:, k:k + 1], ACC[:, :], ALU.mult, ALU.add)
                if k < TAPS - 1:
                    order(ins)
            ins.then_inc(S("conv"), 1)

        dve.wait_ge(S("par_in"), 64)
        dve.wait_ge(S("p_chunk"), 1)
        order(dve.memset(XR[:, 0:3], 0.0))
        for j in range(4):
            conv(j, 8 + j, tile_no(W_BC, 1, j))

        def log1p_exp(raw, bias, x, neg, e, w1, lg, c, name, first):
            order(ts(x, raw, bias, None, ALU.add))
            order.fence()
            order(ts(neg, x, -1.0, None, ALU.mult))
            order.fence()
            tt(neg, x, neg, ALU.min).then_inc(S(name), 1)
            dve.wait_ge(S(name + "_a"), 1)
            ts(w1, e, 1.0, None, ALU.add).then_inc(S(name), 1)
            dve.wait_ge(S(name), 2)
            order(ts(c, w1, -1.0, None, ALU.add))
            order(dve.reciprocal(neg, w1))
            order.fence()
            order(tt(c, e, c, ALU.subtract))
            order.fence()
            order(tt(c, c, neg, ALU.mult))
            order.fence()
            dve.wait_ge(S(name + "_a"), 2)
            order(tt(lg, lg, c, ALU.add))
            order.fence()

        dve.wait_ge(S("c_read2"), W_DT + 1)
        log1p_exp(RW[4][:, :], DTB[0:HEADS_B, :], RW[0][:, :], RW[5][:, :], RW[6][:, :], RW[1][:, :], RW[2][:, :],
                  RW[7][:, :], "dtc", 1)
        order(stt(RW[0][:, :], RW[0][:, :], 0.0, RW[2][:, :], ALU.max, ALU.add))
        order.fence()
        dve.wait_ge(S("dtc_a"), 3)
        order(ts(RW[6][:, :], RW[0][:, :], EAL[0:HEADS_B, :], -1.0, ALU.mult, ALU.mult))
        order(dve.memset(RW[4][:, :], 1.0))
        order.fence()
        order(dve.memset(RW[4][:, 0:TOK:P], 0.0))
        order.fence()
        order(dve.tensor_tensor_scan(ACSROW[:, :], RW[4][:, :], RW[6][:, :], 0.0, ALU.mult, ALU.add))
        order.fence()
        ends = ACSROW[:, P - 1:SEQ:P]
        order(tt(RW[5][:, 0:SEQ].rearrange("h (b l) -> h b l", l=P), ends.unsqueeze(2).broadcast_to([HEADS_B, NB, P]),
                 ACSROW[:, 0:SEQ].rearrange("h (b l) -> h b l", l=P), ALU.subtract))
        tt(RW[5][:, SEQ:TOK], ACSROW[:, TOK - 1:TOK].broadcast_to([HEADS_B, DEC]), ACSROW[:, SEQ:TOK], ALU.subtract) \
            .then_inc(S("dtc"), 1)
        dve.wait_ge(S("dtc_a"), 4)
        order(tt(RW[2][:, :], RW[5][:, :], RW[0][:, :], ALU.mult))
        one = IDENT[0:HEADS_B, 0:HEADS_B].unsqueeze(2)
        order(tt(DECR[:, :, 0:NB], one.broadcast_to([HEADS_B, HEADS_B, NB]),
                 RW[3][:, P - 1:SEQ:P].unsqueeze(1).broadcast_to([HEADS_B, HEADS_B, NB]), ALU.mult))
        tt(DECR[:, :, NB:NB + 1], one,
           RW[3][:, TOK - 1:TOK].unsqueeze(1).broadcast_to([HEADS_B, HEADS_B, 1]), ALU.mult).then_inc(S("dt_rows"), 1)

        def heads_of(q, t, b0, nb, rows):
            return TOKQ[0:rows, q, b0:b0 + nb, bass.ds(2 * t, 2)].unsqueeze(3).broadcast_to([rows, nb, 2, HP])

        def front(g, t):
            if not isinstance(t, int) or t > 0:
                dve.wait_ge(S("bc"), 6 * t)
            if isinstance(t, int) and t == 0:
                dve.wait_ge(S("tokq"), 1)
            order(ts(SEL[:, 0, :], ONES[0:HEADS_B, :], IDENT[0:HEADS_B, bass.ds(2 * t, 1)], None, ALU.mult))
            ts(SEL[:, 1, :], ONES[0:HEADS_B, :], IDENT[0:HEADS_B, bass.ds(2 * t + 1, 1)], None, ALU.mult) \
                .then_inc(S("sel"), 1)
            for q, (b0, nb, rows) in enumerate(QUADS):
                dve.wait_ge(S("xc_turn"), 3 * t + q + 1)
                src = PB[3 + q][0:rows, 0:nb * P].rearrange("p (b j d) -> p b j d", j=2, d=HP)
                for i, dst in enumerate((XD, XW)):
                    last = tt(dst[0:rows, b0:b0 + nb, :].rearrange("p b (j d) -> p b j d", j=2), src,
                              heads_of(i, t, b0, nb, rows), ALU.mult)
                last.then_inc(S("xw"), 1)

            def decays(n):
                j, q = ((0, 0), (0, 1), (1, 0), (1, 1), (0, 2), (1, 2))[n]
                b0, nb, rows = QUADS[q]
                dve.wait_ge(S("bc"), 6 * t + n + 1)
                for i in range(nb):
                    last = stt(M[0:rows, j, b0 + i, 0:rows], PB[6 + n % 2][0:rows, i * P:i * P + rows],
                               TOKQ[0:rows, 3, b0 + i, bass.ds(2 * t + j, 1)], MASKT[0:rows, 0:rows],
                               ALU.subtract, ALU.min)
                last.then_inc(S("seg"), 1)

            decays(0)
            decays(1)
            dve.wait_ge(S("ds"), 3 * t + 3)
            if not isinstance(t, int) or t > 0:
                dve.wait_ge(S("fs_turn"), t)
            order(dve.memset(ST[:, 0, :], 0.0))
            order(dve.tensor_copy(ST[:, 1, :], PB[3][:, 0:P]))
            dve.wait_ge(S("si_used"), t + 1)
            order(dve.tensor_copy(ST[:, NB, :], PB[5][:, P:2 * P]))
            for b in range(1, NB + 1):
                order.fence()
                dst = ST[:, b + 1, :] if b < NB - 1 else FS[:, b - NB + 1, :]
                new = PB[3 + b // 4][:, (b % 4) * P:(b % 4 + 1) * P]
                for i in range(2):
                    cols = slice(i * HP, (i + 1) * HP)
                    ins = stt(dst[:, cols], ST[:, b, cols], DECB[:, bass.ds(2 * t + i, 1), b:b + 1].rearrange("p a b -> p (a b)"),
                              new[:, cols], ALU.mult, ALU.add)
                    if b < NB or i == 0:
                        order(ins)
            ins.then_inc(S("st"), 1)
            for n in range(2, 6):
                decays(n)
            for n, (j, q) in enumerate(((0, 0), (0, 1), (1, 0), (1, 1), (0, 2), (1, 2))):
                b0, nb, rows = QUADS[q]
                dve.wait_ge(S("mexp"), 6 * t + n + 1)
                m = M[0:rows, j, b0:b0 + nb, 0:rows]
                tt(m, m, CBT[0:rows, g, b0:b0 + nb, 0:rows], ALU.mult).then_inc(S("m"), 1)

        def back(t):
            for q, (b0, nb, rows) in enumerate(QUADS):
                intra, state = PB[(3, 5, 7)[q]], PB[(4, 6, 7)[q]]
                off = P if q == 2 else 0
                dve.wait_ge(S("y_mm"), 3 * t + q + 1)
                yt = YT[0:rows, b0:b0 + nb, :]
                order(tt(yt.rearrange("p b (j d) -> p b j d", j=2),
                         state[0:rows, off:off + nb * P].rearrange("p (b j d) -> p b j d", j=2, d=HP),
                         heads_of(2, t, b0, nb, rows), ALU.mult))
                order.fence()
                tt(yt, yt, intra[0:rows, 0:nb * P].rearrange("p (b d) -> p b d", d=P), ALU.add).then_inc(S("yt"), 1)
            for q, (b0, nb, rows) in enumerate(QUADS):
                cols = slice(b0 * P, b0 * P + nb * rows)
                dve.wait_ge(S("y_turn"), 3 * t + q + 1)
                stt(YB[:, t, cols], XC[:, cols], DCOL[:, bass.ds(t, 1)], PB[3 + q][:, 0:nb * rows], ALU.mult, ALU.add) \
                    .then_inc(S("yf"), 1)
            dve.wait_ge(S("yf"), 3 * t + 3)
            dve.wait_ge(S("c_read2"), times(tile_no(W_XZ + 1, 2, t), 1, 1))
            tt(YB[:, t, :], YB[:, t, :], ZS[:, :], ALU.mult).then_inc(S("yb"), 1)

        PAIR = 28
        for g in range(GROUPS_B):
            t0 = 4 * g
            conv(4 + t0, t0, tile_no(W_XZ, 2, t0))
            front(g, t0)
            with order.loop(t0 + 1, t0 + 4, PAIR) as t:
                back(t - 1)
                conv(4 + t, t, tile_no(W_XZ, 2, t))
                front(g, t)
            back(t0 + 3)

        dve.wait_ge(S("cso"), 1)
        dve.wait_ge(S("ssd_stored"), 256)
        dve.wait_ge(S("conv_stored"), 96)
        dve.wait_ge(S("yb"), 8)
        order(dve.memset(V[:, :, NB * P:], 0.0))
        order(dve.memset(RSY[:, :, :], 0.0))
        order.fence()
        dve.wait_ge(S("gv_in"), 48)
        for g in range(GROUPS_B):
            with order.loop(2 * g, 2 * g + 2, 9) as i:
                for j in range(2):
                    for q, (b0, nb, rows) in enumerate(QUADS):
                        bank = (3, 4, 5, 6, 7, 3)[3 * j + q]
                        dve.wait_ge(S("v_turn"), 6 * i + 3 * j + q + 1)
                        dve.tensor_copy(V[0:rows, 2 * i + j, b0 * P:(b0 + nb) * P], PB[bank][0:rows, 0:nb * P]) \
                            .then_inc(S("v_tok"), 1)
                dve.wait_ge(S("v_tok"), 6 * i + 6)
                vj = [V[:, 2 * i + j, :].rearrange("p (b f) -> p b f", f=P) for j in range(2)]
                for j in range(2):
                    order(tt(SQV[:, :, j * P:(j + 1) * P], vj[j], vj[j], ALU.mult))
                order.fence()
                order(dve.tensor_reduce(GSM[:, 0, 0:9], SQV[:, :, :], AX.X, ALU.add))
                order.fence()
                ts(GSM[:, 2, 0:9], GSM[:, 0, 0:9], 1.0 / (2 * P), EPS, ALU.mult, ALU.add).then_inc(S("v_ms"), 1)
                for j in range(2):
                    yb = YB[:, 2 * i + j, :]
                    order(tt(TMP[:, :], yb, yb, ALU.mult))
                    order.fence()
                    tt(RSY[:, g, :], RSY[:, g, :], TMP[:, :], ALU.add).then_inc(S("y_sq"), 1)
                    dve.wait_ge(S("y_sq"), 2 * i + j + 1)
                dve.wait_ge(S("v_rt"), i + 1)
                order(dve.reciprocal(GSM[:, 3, 0:9], GSM[:, 2, 0:9]))
                order.fence()
                for j in range(2):
                    order(tt(vj[j], vj[j], GSM[:, 3, 0:9].unsqueeze(2).broadcast_to([P, 9, P]), ALU.mult))
                order.fence()
                order(tt(vj[0], vj[0], GVB[:, i, 0:P].unsqueeze(1).broadcast_to([P, 9, P]), ALU.mult))
                order.fence()
                tt(vj[1], vj[1], GVB[:, i, P:2 * P].unsqueeze(1).broadcast_to([P, 9, P]), ALU.mult) \
                    .then_inc(S("v_normed"), 1)
        for n in range(6):
            g, c = n // 3, n % 3
            dve.wait_ge(S("gs_mm"), 3 * g + 3 if n < 5 else 6)
            dve.wait_ge(S("gs_mm"), n + 1)
            ts(RSY[:, g, c * CH:(c + 1) * CH], PB[(3, 4, 5, 6, 7, 3)[n]][:, 0:CH], 1.0 / 512, EPS, ALU.mult, ALU.add) \
                .then_inc(S("gs_ms"), 1)
        dve.wait_ge(S("ws_turn"), 1)
        order(dve.tensor_copy(WT[:, :, :].rearrange("p g i -> p (g i)"), PB[6][:, :]))
        order.fence()
        dve.memset(WT[P // 2:P, :, 0:P // 2], 0.0).then_inc(S("wt"), 1)
        dve.wait_ge(S("gs_rt"), 1)
        order(dve.reciprocal(RSY[:, :, :], RSY[:, :, :]))
        dve.wait_ge(S("gv_stored"), 16)
        with order.loop(0, 4, 2) as i:
            for j in range(2):
                t = 2 * i + j
                if j == 0:
                    dve.wait_ge(S("s_mm"), 6 * i)
                else:
                    dve.wait_ge(S("s_mm"), 6 * i + 3)
                dve.tensor_copy(VS[:, :, :], V[:, t, :].rearrange("p (b f) -> p b f", f=P)).then_inc(S("vs"), 1)
                dve.wait_ge(S("c_read2"), 31 + 4 * i + 2 * j)
                order(tt(UG[:, :], UG[:, :], ZG[:, :], ALU.mult))
                order.fence()
                for q, (b0, nb, rows) in enumerate(QUADS):
                    dve.wait_ge(S("s_mm"), 6 * i + 3 * j + q + 1)
                    tt(ZG[:, b0 * P:b0 * P + nb * rows].rearrange("p (b l) -> p b l", l=rows),
                       PB[3 + q][:, 0:nb * rows].rearrange("p (b l) -> p b l", l=rows),
                       BSB[:, i, 0:rows].unsqueeze(1).broadcast_to([P, nb, rows]), ALU.add).then_inc(S("s_read"), 1)
                dve.wait_ge(S("s_read"), 6 * i + 3 * j + 3)
                dve.wait_ge(S("vs"), t + 1)
                tt(YA[:, t, 0:TOK], ZG[:, :], UG[:, :], ALU.mult).then_inc(S("ya"), 1)

        dve.wait_ge(S("p_chunk"), 3 * W_OE)
        for k in range(9):
            if k < 8:
                stt(HX[:, k, :], YB[:, k, :], COLS[:, GSSD + k:GSSD + k + 1], RSY[:, k // 4, :], ALU.mult, ALU.mult) \
                    .then_inc(S("yb_x"), 1)
            if k > 0:
                dve.wait_ge(S("hi"), k)
                tt(HL[:, k - 1, :], HX[:, k - 1, :], HH[:, k - 1, :].bitcast(f32), ALU.subtract).then_inc(S("yb_lo"), 1)
        for k in range(8):
            dve.wait_ge(S("ya_hi"), k + 1)
            tt(YAL[:, k, :], YA[:, k, 0:TOK], YAH[:, k, :].bitcast(f32), ALU.subtract).then_inc(S("ya_lo"), 1)

        def add_squares(tile, last, sem):
            order(tt(TMP[:, :], tile, tile, ALU.mult))
            order.fence()
            tt(SQA, SQA, TMP[:, :], ALU.add).then_inc(S(sem), 1)

        dve.wait_ge(S("yb_lo"), 8)
        order(dve.memset(SQA, 0.0))
        order.fence()
        with order.loop(0, 8, 1) as n:
            dve.wait_ge(S("c_read2"), times(tile_no(W_OE, 1, n), 1, 1))
            if True:
                dve.wait_ge(S("o_sq"), n)
            add_squares(O0[:, n, :], None, "o_sq")

        def rstd(first):
            for c in range(3):
                dve.wait_ge(S("ss_mm"), first + c + 1)
                ts(RSO[:, c * CH:(c + 1) * CH], PB[3 + c][:, 0:CH], 1.0 / D, EPS, ALU.mult, ALU.add) \
                    .then_inc(S("ss_ms"), 1)
            dve.wait_ge(S("ss_rt"), first // 3 + 1)
            order(dve.reciprocal(RSO, RSO))
            order.fence()

        rstd(0)
        order(dve.memset(SQA, 0.0))
        order.fence()
        for k in range(9):
            if k < 8:
                order(stt(O0[:, k, :], O0[:, k, :], COLS[:, POST0 + k:POST0 + k + 1], RSO, ALU.mult, ALU.mult))
                order.fence()
                dve.wait_ge(S("x_turn"), k + 1)
                for q, (b0, nb, rows) in enumerate(QUADS):
                    bank = ((3, 4, 5), (6, 7, 0))[k % 2][q]
                    cols = slice(b0 * P, b0 * P + nb * rows)
                    last = tt(O0[:, k, cols], O0[:, k, cols], PB[bank][:, 0:nb * rows], ALU.add)
                last.then_inc(S("x1"), 1)
            if k > 0:
                dve.wait_ge(S("x1_s"), k)
                if k > 1:
                    dve.wait_ge(S("x1_sq"), k - 1)
                tt(SQA, SQA, TMP[:, :], ALU.add).then_inc(S("x1_sq"), 1)
        rstd(3)
        for k in range(9):
            if k < 8:
                stt(HX[:, k, :], O0[:, k, :], COLS[:, PRE1 + k:PRE1 + k + 1], RSO, ALU.mult, ALU.mult) \
                    .then_inc(S("h1_x"), 1)
            if k > 0:
                dve.wait_ge(S("hi"), 8 + k)
                tt(HL[:, k - 1, :], HX[:, k - 1, :], HH[:, k - 1, :].bitcast(f32), ALU.subtract).then_inc(S("h1_lo"), 1)

        dve.wait_ge(S("c_read2"), W_F - 8 + 1)
        log1p_exp(FW[0][:, :], BF[0:HEADS_C, :], FW[1][:, :], FW[2][:, :], FW[3][:, :], FW[4][:, :], FW[5][:, :],
                  FW[0][:, :], "fc", 1)
        order(ts(FW[1][:, :], FW[1][:, :], 0.0, None, ALU.min))
        order.fence()
        order(tt(LROW[:, 0:SEQ], FW[1][:, 0:SEQ], FW[5][:, 0:SEQ], ALU.subtract))
        order(tt(LROW[:, SEQ + PAST:KEYS], FW[1][:, SEQ:TOK], FW[5][:, SEQ:TOK], ALU.subtract))
        dve.wait_ge(S("clf_turn"), 1)
        dve.tensor_copy(LROW[:, SEQ:SEQ + PAST], PB[3][0:HEADS_C, 0:PAST]).then_inc(S("lrow"), 1)
        order(dve.memset(ONEROW[:, :], 1.0))
        order.fence()
        order(dve.memset(ONEROW[:, 0:KEYS:SEQ], 0.0))
        order.fence()
        dve.wait_ge(S("lrow"), 1)
        order(dve.tensor_tensor_scan(NFROW[:, :], ONEROW[:, :], LROW[:, :], 0.0, ALU.mult, ALU.add))
        order.fence()
        order(ts(NFROW[:, :], NFROW[:, :], -1.0 / SCALE, None, ALU.mult))
        dve.wait_ge(S("lt_turn"), 1)
        order(dve.tensor_copy(LT[:, 0:NB, :], PB[4][:, 0:NB * HEADS_C].rearrange("p (b h) -> p b h", h=HEADS_C)))
        dve.tensor_copy(LT[0:DEC, NB, :], PB[4][0:DEC, NB * HEADS_C:(NB + 1) * HEADS_C]).then_inc(S("lt"), 1)
        order.fence()
        dve.wait_ge(S("masks"), 2)
        dve.wait_ge(S("lf_stored"), 32)

        def head_norm(h, j, parts, gain):
            dve.wait_ge(S("n_ss"), 2 * h + j + 1)
            for c in range(3):
                last = ts(TMPQ[:, c * CH:(c + 1) * CH], PB[3 + c][:, 0:CH], 1.0 / P, EPS, ALU.mult, ALU.add)
            last.then_inc(S("n_ms"), 1)
            dve.wait_ge(S("n_rt"), 2 * h + j + 1)
            order(dve.reciprocal(TMPQ[:, :], TMPQ[:, :]))
            order.fence()
            for src, r in parts:
                last = stt(src, src, COLS[:, gain:gain + 1], r, ALU.mult, ALU.mult)
            last.then_inc(S("n_done"), 1)

        def head(h):
            head_norm(h, 0, [(QT[:, :], TMPQ[:, :])], GQ)
            ts(SEL8[:, :], ONES[0:HEADS_C, :], IDENT[0:HEADS_C, bass.ds(h, 1)], None, ALU.mult).then_inc(S("sel8"), 1)
            head_norm(h, 1, [(KALL[:, 0:SEQ], TMPQ[:, 0:SEQ]), (KALL[:, SEQ + PAST:KEYS], TMPQ[:, SEQ:TOK])], GK)
            dve.wait_ge(S("nf"), h + 1)
            for b in range(NB + 1):
                rows = sample_rows(b)
                banks = (3, 4) if b % 2 == 0 else (5, 6)
                dve.wait_ge(S("sc_mm"), 9 * h + b + 1)
                if b > 0:
                    dve.wait_ge(S("p_turn"), 13 * h + groups_before(b))
                key0, width = (SEQ, PAST + DEC) if b == NB else (0, (b + 1) * P)
                n = (width + 511) // 512
                order(dve.memset(MX[0:rows, n:n + 1], -3.0e38))
                for i in range(n):
                    c0, c1 = i * 512, min(width, i * 512 + 512)
                    order(dve.tensor_tensor_reduce(SB[0:rows, c0:c1], PB[banks[i]][0:rows, 0:c1 - c0],
                                                   NFB[0:rows, key0 + c0:key0 + c1], 1.0, -3.0e38,
                                                   ALU.add, ALU.max, MX[0:rows, i:i + 1]))
                order.fence()
                order(dve.tensor_reduce(MXR[0:rows, :], MX[0:rows, 0:n + 1], AX.X, ALU.max))
                order.fence()
                ts(NBIAS[0:rows, :], MXR[0:rows, :], -SCALE, None, ALU.mult).then_inc(S("sm"), 1)
                dve.wait_ge(S("ex"), 9 * h + b + 1)
                order(dve.reciprocal(RINV[0:rows, :], RSUM[0:rows, :]))
                order.fence()
                ts(SB[0:rows, 0:width], SB[0:rows, 0:width], RINV[0:rows, :], None, ALU.mult).then_inc(S("pn"), 1)
                dve.wait_ge(S("pv"), 9 * h + b + 1)
                tt(Y1[:, h, b * P:b * P + rows], PB[2 if b % 2 == 0 else 7][:, 0:rows], ZSB[:, b * P:b * P + rows],
                   ALU.mult).then_inc(S("y_read"), 1)

        head(0)
        with order.loop(1, 8, 42) as h:
            head(h)
        dve.wait_ge(S("p_chunk"), 3 * W_OO)
        for k in range(8):
            dve.wait_ge(S("hi"), 16 + k + 1)
            tt(HL[:, k, :], Y1[:, k, :], HH[:, k, :].bitcast(f32), ALU.subtract).then_inc(S("y1_lo"), 1)
        order(dve.memset(SQA, 0.0))
        order.fence()
        with order.loop(0, 8, 1) as n:
            dve.wait_ge(S("c_read2"), times(tile_no(W_OO - 8, 1, n), 1, 1))
            dve.wait_ge(S("o_sq"), 8 + n)
            add_squares(O1[:, n, :], None, "o_sq")
        rstd(6)
        for k in range(8):
            order(stt(O1[:, k, :], O1[:, k, :], COLS[:, POST1 + k:POST1 + k + 1], RSO, ALU.mult, ALU.mult))
            order.fence()
            tt(O1[:, k, :], O1[:, k, :], O0[:, k, :], ALU.add).then_inc(S("x2"), 1)

    ctx.close()


_INS = ["x_prompt", "x_sample", "cache_fox_k", "cache_fox_v", "cache_fox_logf", "state_ssd", "state_conv",
        "norm_pre", "norm_post", "w_in_even", "w_out_even", "gmlp_ws", "gmlp_bs", "gmlp_gv",
        "ssd_conv_w", "ssd_conv_b", "ssd_dt_bias", "ssd_a_log", "ssd_d", "ssd_norm_g",
        "w_in_odd", "fox_b_forget", "w_out_odd", "fox_gq", "fox_gk"]
_OUTS = [(1, 1024, 1024), (1, 32, 1024),
         (1, 1, 1024, 8, 128), (1, 1, 1024, 8, 128), (1, 1, 1024, 8),
         (1, 1, 16, 64, 128), (1, 1, 3, 1536),
         (1, 1, 32, 8, 128), (1, 1, 32, 8, 128), (1, 1, 32, 8),
         (1, 1, 16, 64, 128), (1, 1, 3, 1536), (1, 1, 32, 1024)]


def kernel(**inputs):
    import numpy as _np
    import concourse.bacc as _bacc
    from concourse import mybir as _mybir
    from concourse.bass_utils import run_bass_kernel_spmd as _run

    nc = _bacc.Bacc("TRN2", target_bir_lowering=False, num_devices=1)
    arrays, args = {}, []
    for name in _INS:
        a = _np.ascontiguousarray(inputs[name])
        arrays[f"in_{name}_dram"] = a
        args.append(nc.dram_tensor(f"in_{name}_dram", a.shape, _mybir.dt.from_np(a.dtype), kind="ExternalInput").ap())
    for i, shape in enumerate(_OUTS):
        args.append(nc.dram_tensor(f"out_{i}_dram", shape, _mybir.dt.float32, kind="ExternalOutput").ap())
    hybrid_trunk(nc, *args)
    r = _run(nc, [arrays], core_ids=[0])
    return tuple(r.results[0][f"out_{i}_dram"] for i in range(len(_OUTS)))
```

```python
import concourse.bass as bass
from concourse import mybir
from contextlib import ExitStack, contextmanager

f32 = mybir.dt.float32
f32r = mybir.dt.float32r
ALU = mybir.AluOpType
ACT = mybir.ActivationFunctionType
AX = mybir.AxisListType

P = 128
D = 1024
KT = D // P
SEQ, DEC = 1024, 32
TOK = SEQ + DEC
NB = SEQ // P
CH = TOK // 3
PAST = 256
EPS = 1e-6
EVEN_IN, XBC0, DT0 = 5648, 4096, 5632
XBC_TILES = 12
HEADS_B, GROUPS_B, HP = 16, 2, 64
A_GROUPS = 4
HEADS_C = 8
SCALE = float(P) ** -0.5
TAPS = 4
PADW = 3 + SEQ + 3 + DEC
CONVW = PADW - 3
SAMP = 3 + SEQ + 3
KEYS = SEQ + PAST + DEC
NEG = -30000.0
NEGBIG = -1e30

W_BC, W_DT, W_XZ, W_V, W_UZ, W_OE, W_F, W_QKVZ, W_OO, W_END = 0, 4, 5, 21, 29, 45, 61, 62, 94, 102

PRE0, POST0, PRE1, POST1, GSSD, CONVB, GQ, GK, CTX = 0, 8, 16, 24, 32, 40, 52, 53, 54
N_ROWS = CTX + 36
QUADS = [(0, 4, P), (4, 4, P), (8, 1, DEC)]


def tile_no(first, per, t):
    return first, per, t


def times(w, k, add):
    first, per, t = w
    return first * k + add + per * k * t


def loads_of_slot(w):
    first, per, t = w
    if per == 1:
        assert isinstance(t, int)
        first, t = first + t, 0
    return 16 * (first // 2 + 1) + 16 * (per // 2) * t


def slot(w):
    first, per, t = w
    return (first + (t if per == 1 else 0)) % 2


class Order:

    def __init__(self, eng, sem):
        self.eng, self.sem, self.base, self.n = eng, sem, 0, 0

    def __call__(self, ins):
        ins.then_inc(self.sem, 1)
        self.n += 1
        return ins

    def fence(self):
        self.eng.wait_ge(self.sem, self.base + self.n)

    @contextmanager
    def loop(self, start, end, per):
        before = self.base + self.n
        with self.eng.Fori(start, end) as t:
            self.base, self.n = before - per * start + per * t, 0
            yield t
            assert self.n == per, f"the loop's body counts {self.n}, not {per}"
        self.base, self.n = before + per * (end - start), 0


def hybrid_trunk(nc, x_prompt, x_sample, cache_k, cache_v, cache_logf, state_ssd, state_conv,
                 norm_pre, norm_post, w_in_even, w_out_even, gmlp_ws, gmlp_bs, gmlp_gv,
                 conv_w, conv_b, dt_bias, a_log, ssd_d, ssd_norm_g,
                 w_in_odd, b_forget, w_out_odd, gq, gk,
                 y_prompt, y_sample, k_prompt, v_prompt, logf_prompt, ssd_prompt, conv_prompt,
                 k_sample, v_sample, logf_sample, ssd_sample, conv_sample, gv_sample):
    ctx = ExitStack()
    ctx.enter_context(nc.allow_non_contiguous_dma(reason="small parameter vectors"))
    sems = {}

    def S(name):
        if name not in sems:
            sems[name] = ctx.enter_context(nc.semaphore(name))
        return sems[name]

    base = (nc.sbuf_base + 63) // 64 * 64
    end = nc.sbuf_usable_end
    BIG = KT * TOK * 4
    A_H, A_R3 = 0, 2 * BIG
    A_R4 = A_R3 + 8 * 9 * P * 4
    A_R5 = A_R4 + BIG
    A_W = A_R5 + BIG
    A_C = A_W + 6 * 4096

    def at(name, offset, shape, dt=f32):
        size = 4
        for s in shape[1:]:
            size *= s
        assert base + offset + size <= end, (name, base + offset + size - end)
        return nc.alloc_sbuf_tensor_at(name, shape, dt, offset=base + offset)

    class Region:
        def __init__(self, offset, limit):
            self.at, self.limit = offset, limit

        def __call__(self, name, shape, dt=f32):
            t = at(name, self.at, shape, dt)
            size = 4
            for s in shape[1:]:
                size *= s
            self.at += (size + 31) // 32 * 32
            assert self.at <= self.limit, (name, self.at - self.limit)
            return t

    HH = at("HH", A_H, [P, KT, TOK], f32r)
    HL = at("HL", A_H + BIG, [P, KT, TOK], f32r)
    HX = at("HX", A_H + BIG, [P, KT, TOK])
    WRAW = at("WRAW", A_W, [P, 2, KT, P])
    WH = at("WH", A_W + 8192, [P, 2, KT, P], f32r)
    WL = at("WL", A_W + 16384, [P, 2, KT, P], f32r)

    const = Region(A_C, end - base)
    IDENT = const("IDENT", [P, P])
    ONES = const("ONES", [P, P])
    COLS = const("COLS", [P, N_ROWS])
    CONVW_SB = const("CONVW", [P, XBC_TILES, TAPS])
    DCOL = const("DCOL", [P, 8])
    small = const("small", [P, 64])
    SS, MS, RT, RR = small[:, 0:9], small[:, 9:18], small[:, 18:27], small[:, 27:36]
    DTB, AL, EAL, BF = small[:, 36:37], small[:, 37:38], small[:, 38:39], small[:, 39:40]
    MX, MXR, NBIAS, RSUM, RINV = small[:, 40:44], small[:, 44:45], small[:, 45:46], small[:, 46:47], small[:, 47:48]
    c_phase = const.at

    XS = at("XS", A_R3, [P, NB + 1, D])
    r = Region(A_R4, A_W)
    SQJ = r("SQJ", [P, D])
    ROWS = r("ROWS", [P, P])
    DEXP = r("DEXP", [8, 2, HP])
    DSM = r("DSM", [8, 2])

    r = Region(A_R3, A_R5)
    CT = r("CT", [P, 2, TOK])
    BTOK = r("BTOK", [P, 2, 9, P])
    CBT = r("CBT", [P, 2, 9, P])
    m_at = r.at
    M = r("M", [P, 2, 9, P])
    BT = at("BT", m_at, [P, 2, TOK])
    ACSROW = r("ACSROW", [HEADS_B, TOK])
    XR = r("XR", [P, PADW])
    ACC = r("ACC", [P, CONVW])
    rows_at = r.at
    XC = r("XC", [P, TOK])
    XD = r("XD", [P, 9, P])
    XW = r("XW", [P, 9, P])
    YT = XW
    ST = r("ST", [P, 9, P])
    rows_end = r.at
    r = Region(c_phase, end - base)
    MASKT = r("MASKT", [P, P])
    CST = r("CST", [P, 6, XBC_TILES])
    SEL = r("SEL", [HEADS_B, 2, P])
    DECB = r("DECB", [P, HEADS_B, 9])
    DECR = r("DECR", [HEADS_B, HEADS_B, 9])
    TOKQ = r("TOKQ", [P, 4, 9, HEADS_B])
    FS = r("FS", [P, 2, P])
    FSO = r("FSO", [P, 2, P])
    SI = r("SI", [P, P])
    ZS = r("ZS", [P, TOK])
    CSO = r("CSO", [6 * XBC_TILES, P])
    r = Region(rows_at, rows_end)
    RW = [r(f"DTROW{i}", [HEADS_B, TOK]) for i in range(4)]
    r = Region(A_R5, A_W)
    RW += [r(f"DTROW{i}", [HEADS_B, TOK]) for i in range(4, 8)]
    YB = at("YB", A_R5, [P, 8, TOK])

    V = at("V", A_R3, [P, 8, 9 * P])
    YA = at("YA", A_R3, [P, 8, 9 * P])
    r = Region(A_R4, A_R5)
    VG = r("VG", [P, TOK])
    GVB = r("GVB", [P, A_GROUPS, 2 * P])
    vs_at = r.at
    SQV = r("SQV", [P, 9, 2 * P])
    VS = at("VS", vs_at, [P, 9, P])
    WS = r("WS", [P, A_GROUPS, P])
    WT = r("WT", [P, A_GROUPS, P])
    BSB = r("BSB", [P, A_GROUPS, P])
    UG = r("UG", [P, TOK])
    ZG = r("ZG", [P, TOK])
    r = Region(c_phase, end - base)
    TMP = r("TMP", [P, TOK])
    RSY = r("RSY", [P, 2, TOK])
    GSM = r("GSM", [P, 4, 16])

    YAH = at("YAH", A_R4, [P, 8, TOK], f32r)
    YAL = at("YAL", A_R5, [P, 8, TOK], f32r)
    O0 = at("O0", A_R3, [P, 8, TOK])
    XS2 = at("XS2", A_R4, [P, NB + 1, D])
    RSO = RSY[:, 0, :]
    SQA = RSY[:, 1, :]
    O1 = at("O1", A_R5, [P, 8, TOK])
    YO = at("YO", A_R4, [P, 2, 9, P])

    Y1 = at("Y1", A_R5, [P, 8, TOK])
    r = Region(A_R3 + BIG, A_R5)
    QT = r("QT", [P, TOK])
    KALL = r("KALL", [P, KEYS])
    VTOK = r("VTOK", [P, 11, P])
    NFB = r("NFB", [P, KEYS])
    SB = r("SB", [P, SEQ])
    PT = r("PT", [P, NB, P])
    KTOK = r("KTOK", [P, NB, P])
    VRAW = r("VRAW", [P, TOK])
    r = Region(A_R4, A_R5)
    FW = [r(f"FROW{i}", [HEADS_C, TOK]) for i in range(6)]
    r = Region(A_R5 + 4 * TOK * 4, A_W)
    LROW = r("LROW", [HEADS_C, KEYS])
    ONEROW = r("ONEROW", [HEADS_C, KEYS])
    LT = r("LT", [P, 9, HEADS_C])
    CLT = r("CLT", [P, 2, HEADS_C])
    r = Region(c_phase, end - base)
    NRM = r("NRM", [P, 5, CH])
    NFROW = r("NFROW", [HEADS_C, KEYS])
    SEL8 = r("SEL8", [HEADS_C, P])
    MASKD = r("MASKD", [P, P])
    KC = r("KC", [P, 2, P])
    KSAM = KC[0:DEC, 0, :]

    PB = [ctx.enter_context(nc.psum_tensor(f"PB{i}", [P, 512], f32)) for i in range(8)]

    w_even = w_in_even[0].rearrange("(k p) e -> p k e", p=P)
    w_oe = w_out_even[0].rearrange("(s k p) e -> s p k e", s=2, p=P)
    w_odd = w_in_odd[0].rearrange("(k p) e -> p k e", p=P)
    w_oo = w_out_odd[0].rearrange("(k p) e -> p k e", p=P)
    xp = x_prompt[0].rearrange("(b p) d -> p b d", p=P)
    yp = y_prompt[0].rearrange("(b p) d -> p b d", p=P)

    STEPS = 12
    V_, Z_, Q_, K_ = range(4)
    NORM_SLOT = (0, 1, 2, 3, 4, 0)

    def norm_chunk(n):
        c = n % 3
        if n < 3:
            return [(slice(0, CH), QT[:, c * CH:(c + 1) * CH])]
        if c < 2:
            return [(slice(0, CH), KALL[:, c * CH:(c + 1) * CH])]
        return [(slice(0, SEQ - 2 * CH), KALL[:, 2 * CH:SEQ]), (slice(SEQ - 2 * CH, CH), KALL[:, SEQ + PAST:KEYS])]

    def wait(eng, name, value):
        if not isinstance(value, int) or value > 0:
            eng.wait_ge(S(name), value)

    block = ctx.enter_context(nc.Block())


    @block.sync
    def _(sp):
        def load_w(w, src, cols=P):
            if not isinstance(w[2], int) or w[0] + w[1] * w[2] >= 2:
                sp.wait_ge(S("w_low"), times(w, 1, -1))
            sp.dma_start(WRAW[:, slot(w), :, 0:cols], src).then_inc(S(f"w_raw{slot(w)}"), 16)

        def even(col, n=P):
            return w_even[:, :, bass.ds(col, n)]

        for i, (src, rows) in enumerate([
                (norm_pre[0].rearrange("(k p) -> k p", p=P), (PRE0, 8)),
                (norm_post[0].rearrange("(k p) -> k p", p=P), (POST0, 8)),
                (norm_pre[1].rearrange("(k p) -> k p", p=P), (PRE1, 8)),
                (norm_post[1].rearrange("(k p) -> k p", p=P), (POST1, 8)),
                (ssd_norm_g[0].rearrange("(k p) -> k p", p=P), (GSSD, 8)),
                (conv_b[0].rearrange("(k p) -> k p", p=P), (CONVB, XBC_TILES)),
                (gq[0:1, :], (GQ, 1)), (gk[0:1, :], (GK, 1)),
                (state_conv[0, 0].rearrange("r (k p) -> (r k) p", p=P), (CTX, 36))]):
            sp.dma_start(ROWS[rows[0]:rows[0] + rows[1], :], src).then_inc(S("rows_in"), 16)
        sp.dma_start(DSM[:, :], ssd_d[0].rearrange("(t j) -> t j", j=2)).then_inc(S("rows_in"), 16)
        for b in range(NB):
            sp.dma_start(XS[:, b, :], xp[:, b, :]).then_inc(S(f"x_in{b}"), 16)
            if b == 1:
                load_w(tile_no(W_BC, 1, 0), even(XBC0 + 8 * P))
        sp.dma_start(XS[0:DEC, NB, :], x_sample[0]).then_inc(S(f"x_in{NB}"), 16)
        sp.dma_start(CONVW_SB[:, :, :], conv_w[0].rearrange("(t p) k -> p t k", p=P)).then_inc(S("par_in"), 16)
        sp.dma_start(DTB[0:HEADS_B, :], dt_bias[0].unsqueeze(1)).then_inc(S("par_in"), 16)
        sp.dma_start(AL[0:HEADS_B, :], a_log[0].unsqueeze(1)).then_inc(S("par_in"), 16)
        sp.dma_start(BF[0:HEADS_C, :], b_forget[0].unsqueeze(1)).then_inc(S("par_in"), 16)
        for j in range(1, 4):
            load_w(tile_no(W_BC, 1, j), even(XBC0 + (8 + j) * P))
        load_w(tile_no(W_DT, 1, 0), even(DT0, HEADS_B), HEADS_B)

        def states_out(t):
            sp.wait_ge(S("fs_out"), t + 1)
            for j, dst in enumerate((ssd_prompt, ssd_sample)):
                sp.dma_start(dst[0, 0].rearrange("(t h) p n -> t (h p) n", h=2)[t], FSO[:, j, :]) \
                    .then_inc(S("ssd_stored"), 16)

        def pair_loads(t):
            load_w(tile_no(W_XZ, 2, t), even(XBC0 + P * t))
            load_w(tile_no(W_XZ + 1, 2, t), even(3 * D + P * t))
            if not isinstance(t, int) or t > 0:
                sp.wait_ge(S("si_used"), t)
            sp.dma_start(SI[:, :], state_ssd[0, 0].rearrange("(t h) p n -> t (h p) n", h=2)[t]) \
                .then_inc(S("si_in"), 16)

        pair_loads(0)
        with sp.Fori(1, 8) as t:
            pair_loads(t)
            states_out(t - 1)
        load_w(tile_no(W_V, 1, 0), even(D))
        load_w(tile_no(W_V, 1, 1), even(D + P))
        states_out(7)
        sp.wait_ge(S("cso"), 1)
        for j, dst in enumerate((conv_prompt, conv_sample)):
            for q in range(3):
                sp.dma_start(dst[0, 0, q].rearrange("(t p) -> t p", p=P),
                             CSO[(3 * j + q) * XBC_TILES:(3 * j + q + 1) * XBC_TILES, :]).then_inc(S("conv_stored"), 16)
        sp.wait_ge(S("yb"), 8)
        sp.wait_ge(S("y_turn"), 24)
        sp.dma_start(GVB[:, :, :].rearrange("p g k -> p (g k)"),
                     gmlp_gv[0:1].rearrange("a g k -> a (g k)").broadcast_to([P, D])).then_inc(S("gv_in"), 16)
        sp.dma_start(BSB[:, :, :].rearrange("p g k -> p (g k)"),
                     gmlp_bs[0:1].rearrange("a g k -> a (g k)").broadcast_to([P, A_GROUPS * P])).then_inc(S("gv_in"), 16)
        sp.dma_start(WS[:, :, :], gmlp_ws[0].rearrange("g i j -> i g j")).then_inc(S("gv_in"), 16)
        with sp.Fori(1, 4) as i:
            for j in range(2):
                load_w(tile_no(W_V + j, 2, i), even(D + P * j + 2 * P * i))
        load_w(tile_no(W_UZ, 1, 0), even(0))
        load_w(tile_no(W_UZ, 1, 1), even(2 * D))
        sp.wait_ge(S("v_normed"), 4)
        sp.dma_start(gv_sample[0, 0].rearrange("t (k f) -> t k f", f=P), V[0:DEC, :, NB * P:]) \
            .then_inc(S("gv_stored"), 16)
        with sp.Fori(1, 8) as t:
            load_w(tile_no(W_UZ, 2, t), even(P * t))
            load_w(tile_no(W_UZ + 1, 2, t), even(2 * D + P * t))
        with sp.Fori(0, 8) as n:
            load_w(tile_no(W_OE, 2, n), w_oe[1][:, :, bass.ds(P * n, P)])
            load_w(tile_no(W_OE + 1, 2, n), w_oe[0][:, :, bass.ds(P * (n + 1) - P, P)])

        def qkvz(h, j):
            col = D * (2, 3, 0, 1)[j]
            load_w(tile_no(W_QKVZ + j, 4, h), w_odd[:, :, bass.ds(col + P * h, P)])

        load_w(tile_no(W_F, 1, 0), w_odd[:, :, 4 * D:4 * D + HEADS_C], HEADS_C)
        qkvz(0, 0)
        sp.wait_ge(S("p_chunk"), 3 * W_F)
        for b in range(NB):
            sp.dma_start(XS2[:, b, :], xp[:, b, :]).then_inc(S(f"x_in{b}"), 16)
        sp.dma_start(XS2[0:DEC, NB, :], x_sample[0]).then_inc(S(f"x_in{NB}"), 16)
        sp.wait_ge(S("x_turn"), 8)
        sp.dma_start(CLT[:, :, :], cache_logf[0, 0].rearrange("(b p) h -> p b h", p=P)).then_inc(S("clf_in"), 16)
        qkvz(0, 1)
        sp.wait_ge(S("lt"), 1)
        sp.dma_start(logf_prompt[0, 0].rearrange("(b p) h -> p b h", p=P), LT[:, 0:NB, :]).then_inc(S("lf_stored"), 16)
        sp.dma_start(logf_sample[0, 0], LT[0:DEC, NB, :]).then_inc(S("lf_stored"), 16)

        def out_odd_w(i, j):
            load_w(tile_no(W_OO + j, 2, i), w_oo[:, :, bass.ds(P * j + 2 * P * i, P)])

        def head_cols(h):
            return bass.ds(P * (h + 3) - 3 * P, P)

        def turn_moves(t, attend=True, project=True, last=False):
            p = t + 1
            if project:
                qkvz(p, Q_)
                qkvz(p, K_)
            if attend:
                sp.wait_ge(S("vt_read"), 3 * t + 3)
                sp.dma_start(v_prompt[0, 0].rearrange("(b p) h d -> p b (h d)", p=P)[:, :, head_cols(t)],
                             VTOK[:, 0:NB, :]).then_inc(S("v_stored"), 16)
                sp.dma_start(v_sample[0, 0].rearrange("t h d -> t (h d)")[:, head_cols(t)],
                             VTOK[0:DEC, NB + 2, :]).then_inc(S("v_stored"), 16)
                sp.wait_ge(S("k_tok"), 3 * t + 3)
                sp.dma_start(k_prompt[0, 0].rearrange("(b p) h d -> p b (h d)", p=P)[:, :, head_cols(t)],
                             KTOK[:, :, :]).then_inc(S("k_stored"), 16)
                sp.dma_start(k_sample[0, 0].rearrange("t h d -> t (h d)")[:, head_cols(t)], KSAM) \
                    .then_inc(S("k_stored"), 16)
            if not project:
                return
            out_odd_w(0, 0) if last else qkvz(p + 1, V_)
            if attend:
                sp.wait_ge(S("k_stored"), 32 * t + 32)
            else:
                sp.wait_ge(S("lt"), 1)
            sp.dma_start(KC[:, :, :], cache_k[0, 0].rearrange("(b p) h d -> p b (h d)", p=P)[:, :, head_cols(p)]) \
                .then_inc(S("kc_in"), 16)
            out_odd_w(0, 1) if last else qkvz(p + 1, Z_)
            if attend:
                sp.wait_ge(S("pv"), 9 * t + 9)
            sp.dma_start(VTOK[:, NB:NB + 2, :],
                         cache_v[0, 0].rearrange("(b p) h d -> p b (h d)", p=P)[:, :, head_cols(p)]) \
                .then_inc(S("vc_in"), 16)

        turn_moves(-1, attend=False)
        with sp.Fori(0, 6) as t:
            turn_moves(t)
        turn_moves(6, last=True)
        turn_moves(7, project=False)
        with sp.Fori(1, 4) as i:
            for j in range(2):
                out_odd_w(i, j)
        for k in range(8):
            sp.wait_ge(S("y_tok"), 3 * k + 3)
            sp.dma_start(yp[:, :, k * P:(k + 1) * P], YO[:, k % 2, 0:NB, :]).then_inc(S(f"y_stored{k % 2}"), 16)
            sp.dma_start(y_sample[0][:, k * P:(k + 1) * P], YO[0:DEC, k % 2, NB, :]).then_inc(S(f"y_stored{k % 2}"), 16)
        for name, n in (("ssd_stored", 16), ("conv_stored", 6), ("gv_stored", 1), ("lf_stored", 2),
                        ("k_stored", 16), ("v_stored", 16), ("y_stored0", 8), ("y_stored1", 8)):
            sp.wait_ge(S(name), 16 * n)

    @block.gpsimd
    def _(pool):
        order = Order(pool, S("pool_order"))

        def split_low(w):
            pool.wait_ge(S("w_high"), times(w, 1, 1))
            if not isinstance(w[2], int) or w[0] + w[1] * w[2] >= 2:
                pool.wait_ge(S("p_chunk"), times(w, 3, -3))
            pool.tensor_tensor(WL[:, slot(w), :, :], WRAW[:, slot(w), :, :], WH[:, slot(w), :, :].bitcast(f32),
                               ALU.subtract).then_inc(S("w_low"), 1)

        def split_lows(ws):
            for w in ws:
                split_low(w)

        order(pool.memset(IDENT[:, :], 0.0))
        order.fence()
        order(pool.affine_select(out=IDENT[:, :], in_=IDENT[:, :], compare_op=ALU.not_equal, fill=1.0, base=0,
                                 pattern=[[-1, P]], channel_multiplier=1))
        order(pool.memset(MASKT[:, :], 0.0))
        order.fence()
        pool.affine_select(out=MASKT[:, :], in_=MASKT[:, :], compare_op=ALU.is_ge, fill=NEG, base=0,
                           pattern=[[1, P]], channel_multiplier=-1).then_inc(S("masks"), 1)
        for w in range(W_XZ):
            split_low(tile_no(w, 1, 0))
        with pool.Fori(0, 8) as t:
            split_lows([tile_no(W_XZ + j, 2, t) for j in range(2)])
        with pool.Fori(0, 4) as i:
            split_lows([tile_no(W_V + j, 2, i) for j in range(2)])
        with pool.Fori(0, 8) as t:
            split_lows([tile_no(W_UZ + j, 2, t) for j in range(2)])
        with pool.Fori(0, 8) as n:
            split_lows([tile_no(W_OE + j, 2, n) for j in range(2)])
        split_low(tile_no(W_F, 1, 0))
        pool.wait_ge(S("h1_lo"), 8)
        order(pool.memset(MASKD[:, :], 0.0))
        order.fence()
        pool.affine_select(out=MASKD[:, :], in_=MASKD[:, :], compare_op=ALU.is_ge, fill=NEGBIG, base=0,
                           pattern=[[-1, P]], channel_multiplier=1).then_inc(S("masks"), 1)
        split_low(tile_no(W_QKVZ + V_, 4, 0))
        split_low(tile_no(W_QKVZ + Z_, 4, 0))

        def turn_parts(p):
            def squares(n):
                pool.wait_ge(S(f"c_read{n % 3}"), times(tile_no(W_QKVZ - 8 + (Q_ if n < 3 else K_), 4, p), 1, 1))
                if n == 0:
                    wait(pool, "n_done", 2 * p)
                if n == 5:
                    pool.wait_ge(S("n_done"), 2 * p + 1)
                for cols, src in norm_chunk(n):
                    last = pool.tensor_tensor(NRM[:, NORM_SLOT[n], cols], src, src, ALU.mult)
                last.then_inc(S("n_sq"), 1)

            split_low(tile_no(W_QKVZ + Q_, 4, p))
            split_low(tile_no(W_QKVZ + K_, 4, p))
            for n in range(3):
                squares(n)
            split_low(tile_no(W_QKVZ + 4 + V_, 4, p))
            for n in range(3, 6):
                squares(n)
            split_low(tile_no(W_QKVZ + 4 + Z_, 4, p))

        turn_parts(0)
        with pool.Fori(1, 8) as p:
            turn_parts(p)
        with pool.Fori(1, 4) as i:
            split_lows([tile_no(W_OO + j, 2, i) for j in range(2)])

    def sample_rows(b):
        return DEC if b == NB else P

    def span(b, n=1):
        return slice(b * P, b * P + (DEC if b == NB else n * P))

    def groups_before(b):
        return b if b < 4 else (4 + 2 * (b - 4) if b < NB else 12)

    @block.tensor
    def _(pe):
        def mm(out, lhsT, rhs, start=True, stop=True):
            return pe.matmul(out, lhsT, rhs, start=start, stop=stop)

        def turn(out, in_):
            n = in_.shape[0]
            return pe.transpose(out, in_, IDENT[0:n, 0:n])

        def key_wait(rows):
            if rows <= DEC:
                pe.wait_ge(S("masks"), 1)

        def project_chunk(w, u, c, hi, lo, start=True, stop=True, ready=None, ks=range(KT)):
            if c == 0:
                pe.wait_ge(S("w_low"), times(w, 1, 1))
            if start and not (isinstance(u[2], int) and u[0] + u[1] * u[2] == 0):
                pe.wait_ge(S(f"c_read{c}"), times(u, 1, 0))
            cols = slice(c * CH, (c + 1) * CH)
            for k in ks:
                if ready:
                    pe.wait_ge(S(ready), k + 1)
                wh, wl = WH[:, slot(w), k, :], WL[:, slot(w), k, :]
                mm(PB[c][:, 0:CH], wh, hi[:, k, cols], start=start and k == 0, stop=False)
                mm(PB[c][:, 0:CH], wh, lo[:, k, cols], start=False, stop=False)
                last = mm(PB[c][:, 0:CH], wl, hi[:, k, cols], start=False, stop=stop and k == KT - 1)
            if ks[-1] == KT - 1:
                last.then_inc(S("p_chunk"), 1)

        def project(w, u, hi, lo, start=True, stop=True, ready=None):
            for c in range(3):
                project_chunk(w, u, c, hi, lo, start, stop, ready if c == 0 else None)

        pe.wait_ge(S("masks"), 1)
        pe.wait_ge(S("rows_in"), 160)
        turn(PB[3][:, 0:N_ROWS], ROWS[0:N_ROWS, :])
        pe.wait_ge(S("dexp"), 1)
        turn(PB[3][:, P:P + 8], DEXP[:, :, :].rearrange("t j p -> t (j p)")).then_inc(S("rows_turn"), 1)
        pe.wait_ge(S("cols"), 1)
        for q, (b0, nb, rows) in enumerate(QUADS):
            pe.wait_ge(S("xn"), b0 + nb)
            for k in range(KT):
                i = q * KT + k
                if i >= 4:
                    pe.wait_ge(S("h_lo"), i - 3)
                for j in range(nb):
                    last = turn(PB[3 + i % 4][:, j * P:j * P + rows], XS[0:rows, b0 + j, k * P:(k + 1) * P])
                last.then_inc(S("x_t"), 1)
        pe.wait_ge(S("h_lo"), 24)
        for w in range(W_XZ):
            project(tile_no(w, 1, 0), tile_no(w, 1, 0), HH, HL)

        pe.wait_ge(S("conv_act"), 4)
        n = 0
        for g in range(GROUPS_B):
            for b0, nb, rows in QUADS:
                for what in range(2):
                    if n >= 3:
                        pe.wait_ge(S("cb_read"), n - 2)
                    bank = PB[5 + n % 3]
                    for j in range(nb):
                        cols = slice((b0 + j) * P, (b0 + j) * P + rows)
                        if what == 0:
                            last = mm(bank[0:rows, j * P:j * P + rows], BT[:, g, cols], CT[:, g, cols])
                        else:
                            last = turn(bank[0:rows, j * P:(j + 1) * P], BT[:, g, cols])
                    last.then_inc(S("cb_mm"), 1)
                    n += 1

        pe.wait_ge(S("dt_rows"), 1)
        for i, row in enumerate((RW[0], RW[2], RW[3], ACSROW)):
            for b in range(NB + 1):
                out = PB[3] if i < 3 else PB[4]
                o = (i * 9 if i < 3 else 0) + b
                turn(out[0:sample_rows(b), o * HEADS_B:(o + 1) * HEADS_B], row[:, span(b)])
        mm(PB[4][:, 256:256 + 9 * HEADS_B], ONES[0:HEADS_B, :], DECR[:, :, :].rearrange("k h b -> k (h b)")) \
            .then_inc(S("dt_turn"), 1)

        def pair_front(g, t):
            pe.wait_ge(S("conv_act"), 5 + t)
            if isinstance(t, int) and t == 0:
                pe.wait_ge(S("tokq"), 1)
                pe.wait_ge(S("cb_read"), 12)
            else:
                pe.wait_ge(S("yf"), 3 * t)
            for q, (b0, nb, rows) in enumerate(QUADS):
                for j in range(nb):
                    last = turn(PB[3 + q][0:rows, j * P:(j + 1) * P], XC[:, (b0 + j) * P:(b0 + j) * P + rows])
                last.then_inc(S("xc_turn"), 1)
            pe.wait_ge(S("sel"), t + 1)

            def decay_rows(n):
                j, q = ((0, 0), (0, 1), (1, 0), (1, 1), (0, 2), (1, 2))[n]
                if n >= 2:
                    pe.wait_ge(S("seg"), 6 * t + n - 1)
                b0, nb, rows = QUADS[q]
                width = nb * rows
                mm(PB[6 + n % 2][:, 0:width], SEL[:, j, :], ACSROW[:, b0 * P:b0 * P + width]).then_inc(S("bc"), 1)

            decay_rows(0)
            decay_rows(1)
            for q, (b0, nb, rows) in enumerate(QUADS):
                pe.wait_ge(S("xw"), 3 * t + q + 1)
                if q == 2:
                    pe.wait_ge(S("si_in"), 16 * t + 16)
                    turn(PB[5][:, P:2 * P], SI[:, :]).then_inc(S("si_used"), 1)
                for j in range(nb):
                    last = mm(PB[3 + q][:, j * P:(j + 1) * P], BTOK[0:rows, g, b0 + j, :], XW[0:rows, b0 + j, :])
                last.then_inc(S("ds"), 1)
            for n in range(2, 6):
                decay_rows(n)
            pe.wait_ge(S("st"), t + 1)
            turn(PB[5][:, 2 * P:3 * P], FS[:, 0, :])
            turn(PB[5][:, 3 * P:4 * P], FS[:, 1, :]).then_inc(S("fs_turn"), 1)

        def pair_back(g, t):
            pe.wait_ge(S("m"), 6 * t + 6)
            pe.wait_ge(S("fs_out"), t + 1)
            for q, (b0, nb, rows) in enumerate(QUADS):
                intra, state = PB[(3, 5, 7)[q]], PB[(4, 6, 7)[q]]
                off = P if q == 2 else 0
                for j in range(nb):
                    b = b0 + j
                    for i in range(2):
                        mm(intra[0:rows, j * P + i * HP:j * P + (i + 1) * HP], M[0:rows, i, b, 0:rows],
                           XD[0:rows, b, i * HP:(i + 1) * HP])
                    last = mm(state[0:rows, off + j * P:off + (j + 1) * P], CT[:, g, b * P:b * P + rows], ST[:, b, :])
                last.then_inc(S("y_mm"), 1)
            for q, (b0, nb, rows) in enumerate(QUADS):
                if q < 2:
                    pe.wait_ge(S("yt"), 3 * t + (1 if q == 0 else 3))
                for j in range(nb):
                    last = turn(PB[3 + q][:, j * P:j * P + rows], YT[0:rows, b0 + j, :])
                last.then_inc(S("y_turn"), 1)

        for g in range(GROUPS_B):
            t0 = 4 * g
            xz = [tile_no(W_XZ + j, 2, t0) for j in range(2)]
            project(xz[0], xz[0], HH, HL)
            project(xz[1], xz[1], HH, HL)
            pair_front(g, t0)
            with pe.Fori(t0 + 1, t0 + 4) as t:
                xz = [tile_no(W_XZ + j, 2, t) for j in range(2)]
                project(xz[0], xz[0], HH, HL)
                pair_back(g, t - 1)
                project(xz[1], xz[1], HH, HL)
                pair_front(g, t)
            pair_back(g, t0 + 3)

        pe.wait_ge(S("yf"), 24)
        turn(PB[3][0:6 * XBC_TILES, 0:P], CST[:, :, :].rearrange("p r t -> p (r t)")).then_inc(S("cst_turn"), 1)

        with pe.Fori(0, 4) as i:
            vt = [tile_no(W_V + j, 2, i) for j in range(2)]
            project(vt[0], vt[0], HH, HL)
            project(vt[1], vt[1], HH, HL)
            pe.wait_ge(S("v_tok"), 6 * i)
            pe.wait_ge(S("cso"), 1)
            for j, src in enumerate((VG, UG)):
                pe.wait_ge(S("c_read2"), times(vt[j], 1, 1))
                for q, (b0, nb, rows) in enumerate(QUADS):
                    if j == 1 and q == 2:
                        pe.wait_ge(S("v_tok"), 6 * i + 1)
                    key_wait(rows)
                    for n in range(nb):
                        last = turn(PB[(3, 4, 5, 6, 7, 3)[3 * j + q]][0:rows, n * P:(n + 1) * P],
                                    src[:, (b0 + n) * P:(b0 + n) * P + rows])
                    last.then_inc(S("v_turn"), 1)
        pe.wait_ge(S("v_tok"), 24)
        for n in range(6):
            g, c = n // 3, n % 3
            pe.wait_ge(S("y_sq"), 4 + 4 * g)
            if n == 5:
                pe.wait_ge(S("gs_ms"), 1)
            mm(PB[(3, 4, 5, 6, 7, 3)[n]][:, 0:CH], ONES[:, :], RSY[:, g, c * CH:(c + 1) * CH]).then_inc(S("gs_mm"), 1)
        pe.wait_ge(S("gv_in"), 48)
        pe.wait_ge(S("gs_ms"), 4)
        for g in range(A_GROUPS):
            last = turn(PB[6][:, g * P:(g + 1) * P], WS[:, g, :])
        last.then_inc(S("ws_turn"), 1)
        pe.wait_ge(S("wt"), 1)
        with pe.Fori(0, 4) as i:
            for j in range(2):
                uz = [tile_no(W_UZ + 2 * j + n, 4, i) for n in range(2)]
                project(uz[0], uz[0], HH, HL)
                project(uz[1], uz[1], HH, HL)
                pe.wait_ge(S("vs"), 2 * i + j + 1)
                for q, (b0, nb, rows) in enumerate(QUADS):
                    if j > 0:
                        pe.wait_ge(S("s_read"), 6 * i + 3 * j - 3 + q + 1)
                    else:
                        pe.wait_ge(S("s_read"), 6 * i)
                    for n in range(nb):
                        last = mm(PB[3 + q][:, n * P:n * P + rows], VS[:, b0 + n, :], WT[:, i, 0:rows])
                    last.then_inc(S("s_mm"), 1)

        def out_sums(name, at_count):
            pe.wait_ge(S(name), at_count)
            for c in range(3):
                mm(PB[3 + c][:, 0:CH], ONES[:, :], SQA[:, c * CH:(c + 1) * CH]).then_inc(S("ss_mm"), 1)

        def out_even(n, first):
            pe_u = tile_no(W_OE, 1, n)
            project(tile_no(W_OE, 2, n), pe_u, HH, HL, stop=False, ready="yb_lo" if first else None)
            project(tile_no(W_OE + 1, 2, n), pe_u, YAH, YAL, start=False, ready="ya_lo" if first else None)

        out_even(0, True)
        with pe.Fori(1, 8) as n:
            out_even(n, False)
        pe.wait_ge(S("s_read"), 24)
        out_sums("o_sq", 8)
        for k in range(8):
            if k < 2:
                pe.wait_ge(S("ss_ms"), 3)
            else:
                pe.wait_ge(S("x1"), k - 1)
            for q, (b0, nb, rows) in enumerate(QUADS):
                bank = ((3, 4, 5), (6, 7, 0))[k % 2][q]
                for j in range(nb):
                    if k == 0:
                        pe.wait_ge(S(f"x_in{b0 + j}"), 32)
                    last = turn(PB[bank][:, j * P:j * P + rows], XS2[0:rows, b0 + j, k * P:(k + 1) * P])
            last.then_inc(S("x_turn"), 1)
        pe.wait_ge(S("x1"), 8)
        out_sums("x1_sq", 8)

        project(tile_no(W_F, 1, 0), tile_no(W_F - 8, 1, 0), HH, HL, ready="h1_lo")
        pe.wait_ge(S("clf_in"), 16)
        pe.wait_ge(S("ss_ms"), 6)
        for b in range(2):
            last = turn(PB[3][0:HEADS_C, b * P:(b + 1) * P], CLT[:, b, :])
        last.then_inc(S("clf_turn"), 1)
        pe.wait_ge(S("lrow"), 1)
        for b in range(NB + 1):
            cols = slice(SEQ + PAST, KEYS) if b == NB else span(b)
            last = turn(PB[4][0:sample_rows(b), b * HEADS_C:(b + 1) * HEADS_C], LROW[:, cols])
        last.then_inc(S("lt_turn"), 1)

        pe.wait_ge(S("masks"), 2)

        def norm_sum(h, n, bank):
            pe.wait_ge(S("n_sq"), 6 * h + n + 1)
            mm(PB[bank][:, 0:CH], ONES[:, :], NRM[:, NORM_SLOT[n], :]).then_inc(S("n_ss"), 1)

        def turn_quad(src, q, bank, sem):
            b0, nb, rows = QUADS[q]
            c0 = SEQ + PAST if q == 2 and src is KALL else b0 * P
            for j in range(nb):
                last = turn(PB[bank][0:rows, j * P:(j + 1) * P], src[:, c0 + j * P:c0 + j * P + rows])
            last.then_inc(S(sem), 1)

        def nf_rows(h, c, bank):
            cols = slice(c * 512, min(KEYS, c * 512 + 512))
            mm(PB[bank][:, 0:cols.stop - cols.start], SEL8[:, :], NFROW[:, cols]).then_inc(S("nf_mm"), 1)

        def scores(h, b):
            rows = sample_rows(b)
            if b == 0:
                pe.wait_ge(S("nf"), 3 * h + 2)
                pe.wait_ge(S("n_done"), 2 * h + 1)
            else:
                pe.wait_ge(S("sm"), 9 * h + b)
            if b == 2:
                pe.wait_ge(S("n_done"), 2 * h + 2)
            if b == 4:
                pe.wait_ge(S("k_tok"), 3 * h + 2)
            if b == NB:
                pe.wait_ge(S("kc_done"), h + 1)
            q = QT[:, b * P:b * P + rows]
            key0, keys = (SEQ, PAST + DEC) if b == NB else (0, (b + 1) * P)
            for i, c0 in enumerate(range(0, keys, 512)):
                c1 = min(c0 + 512, keys)
                mm(PB[3 + i][0:rows, 0:c1 - c0], q, KALL[:, key0 + c0:key0 + c1], stop=c1 < keys)
            mm(PB[3 + i][0:rows, keys - rows - c0:keys - c0], IDENT[0:rows, 0:rows],
               MASKD[0:rows, 0:rows], start=False).then_inc(S("sc_mm"), 1)

        def key_blocks(b):
            return [(j, j, P) for j in range(b + 1)] if b < NB else [(0, 8, P), (1, 9, P), (2, 10, DEC)]

        def turn_probs(h, b):
            rows, blocks = sample_rows(b), key_blocks(b)
            pe.wait_ge(S("pn"), 9 * h + b + 1)
            if b == 0:
                pe.wait_ge(S("nf"), 3 * h + 3)
            if b == 4:
                pe.wait_ge(S("k_tok"), 3 * h + 3)
            wait(pe, "pt_read", 13 * h + groups_before(b))
            for g in range(0, len(blocks), 4):
                for j, _, keys in blocks[g:g + 4]:
                    turned = P if keys == P else rows
                    last = turn(PB[5 + g // 4][0:keys, (j % 4) * P:(j % 4) * P + turned],
                                SB[0:turned, j * P:j * P + keys])
                last.then_inc(S("p_turn"), 1)

        def values(h, b):
            rows, blocks = sample_rows(b), key_blocks(b)
            if b % 4 == 0:
                pe.wait_ge(S("vt_read"), 3 * h + b // 4 + 1)
            if b == NB:
                pe.wait_ge(S("vc_in"), 16 * h + 16)
            wait(pe, "y_read", 9 * h + b)
            pe.wait_ge(S("pt_read"), 13 * h + groups_before(b) + (len(blocks) + 3) // 4)
            for i, (j, src, keys) in enumerate(blocks):
                last = mm(PB[7][:, 0:rows], VTOK[0:keys, src, :], PT[0:keys, j, 0:rows],
                          start=i == 0, stop=i == len(blocks) - 1)
            last.then_inc(S("pv"), 1)

        def turn_steps(t, attend=True, project=True):
            p = t + 1
            for i in range(STEPS):
                if project:
                    project_chunk(tile_no(W_QKVZ + i // 3, 4, p), tile_no(W_QKVZ - 8 + i // 3, 4, p), i % 3, HH, HL)
                elif i >= 9:
                    project_chunk(tile_no(W_OO, 2, 0), tile_no(W_OO - 8, 2, 0), i - 9, HH, HL, ready="y1_lo", ks=range(7))
                if attend and i == 0:
                    pe.wait_ge(S("n_ms"), 6 * t + 5)
                    norm_sum(t, 5, 4)
                    pe.wait_ge(S("vt_read"), 3 * t + 1)
                    turn_quad(VRAW, 1, 6, "vt_turn")
                if attend and i == 1:
                    pe.wait_ge(S("n_ms"), 6 * t + 6)
                    key_wait(DEC)
                    turn_quad(VRAW, 2, 4, "vt_turn")
                if attend and i == 2:
                    pe.wait_ge(S("n_done"), 2 * t + 2)
                    pe.wait_ge(S("vt_read"), 3 * t + 2)
                    turn_quad(KALL, 0, 6, "kt_turn")
                    pe.wait_ge(S("vt_read"), 3 * t + 3)
                    turn_quad(KALL, 1, 4, "kt_turn")
                if attend and i == 3:
                    pe.wait_ge(S("k_tok"), 3 * t + 1)
                    key_wait(DEC)
                    turn_quad(KALL, 2, 6, "kt_turn")
                if project and i == 8:
                    wait(pe, "sm", 9 * t + 8)
                    norm_sum(p, 0, 4)
                if project and i == 9:
                    pe.wait_ge(S("n_ms"), 6 * p + 1)
                    norm_sum(p, 1, 4)
                    wait(pe, "pt_read", 13 * t + 12)
                    norm_sum(p, 2, 6)
                if project and i == 10:
                    pe.wait_ge(S("n_ms"), 6 * p + 2)
                    norm_sum(p, 3, 4)
                    pe.wait_ge(S("n_ms"), 6 * p + 3)
                    pe.wait_ge(S("kc_in"), 16 * p + 16)
                    for b in range(2):
                        last = turn(PB[6][:, b * P:(b + 1) * P], KC[:, b, :])
                    last.then_inc(S("kc_turn"), 1)
                    wait(pe, "sm", 9 * t + 9)
                    pe.wait_ge(S("sel8"), p + 1)
                    nf_rows(p, 0, 3)
                if project and i == 11:
                    pe.wait_ge(S("n_ms"), 6 * p + 4)
                    norm_sum(p, 4, 4)
                    pe.wait_ge(S("kc_done"), p + 1)
                    turn_quad(VRAW, 0, 6, "vt_turn")
                    pe.wait_ge(S("nf"), 3 * p + 1)
                    nf_rows(p, 1, 3)
                    wait(pe, "pt_read", 13 * t + 13)
                    nf_rows(p, 2, 5)
                if attend and 2 <= i <= NB + 2:
                    values(t, i - 2)
                if attend and 1 <= i <= NB + 1:
                    turn_probs(t, i - 1)
                if attend and i <= NB:
                    scores(t, i)

        turn_steps(-1, attend=False)
        with pe.Fori(0, 7) as t:
            turn_steps(t)
        turn_steps(7, project=False)

        def out_odd(i, j):
            project(tile_no(W_OO + j, 2, i), tile_no(W_OO - 8 + j, 2, i), HH, HL)

        for c in range(3):
            project_chunk(tile_no(W_OO, 2, 0), tile_no(W_OO - 8, 2, 0), c, HH, HL, start=False, ready="y1_lo", ks=[7])
        out_odd(0, 1)
        with pe.Fori(1, 4) as i:
            out_odd(i, 0)
            out_odd(i, 1)
        out_sums("o_sq", 16)
        pe.wait_ge(S("ss_ms"), 9)
        for k in range(8):
            pe.wait_ge(S("x2"), k + 1)
            for q, (b0, nb, rows) in enumerate(QUADS):
                if k >= 2:
                    pe.wait_ge(S("y_tok"), 3 * (k - 2) + q + 1)
                bank, off = ((3, 4, 5), (6, 7, 0))[k % 2][q], 0
                for j in range(nb):
                    last = turn(PB[bank][0:rows, off + j * P:off + (j + 1) * P],
                                O1[:, k, (b0 + j) * P:(b0 + j) * P + rows])
                last.then_inc(S("o_turn"), 1)

    @block.scalar
    def _(act):
        def copy(out, in_, scale=1.0):
            return act.activation(out, in_, ACT.Copy, scale=scale)

        order = Order(act, S("act_order"))

        def split_high(w):
            act.wait_ge(S(f"w_raw{slot(w)}"), loads_of_slot(w))
            if not isinstance(w[2], int) or w[0] + w[1] * w[2] >= 2:
                act.wait_ge(S("p_chunk"), times(w, 3, -3))
            copy(WH[:, slot(w), :, :], WRAW[:, slot(w), :, :]).then_inc(S("w_high"), 1)

        def read_chunks(w, outs, func=ACT.Copy, rows=P):
            for c in range(3):
                act.wait_ge(S("p_chunk"), times(w, 3, c + 1))
                for i, (cols, out) in enumerate(outs[c]):
                    last = act.activation(out, PB[c][0:rows, cols], func)
                last.then_inc(S(f"c_read{c}"), 1)

        def whole(t, rows=P):
            return [[(slice(0, CH), t[0:rows, c * CH:(c + 1) * CH])] for c in range(3)]

        def parted(t, prompt0, sample0):
            two = SEQ - 2 * CH
            return [[(slice(0, CH), t[:, prompt0:prompt0 + CH])],
                    [(slice(0, CH), t[:, prompt0 + CH:prompt0 + 2 * CH])],
                    [(slice(0, two), t[:, prompt0 + 2 * CH:prompt0 + SEQ]),
                     (slice(two, CH), t[:, sample0:sample0 + DEC])]]

        act.wait_ge(S("rows_turn"), 1)
        order(copy(COLS[:, :], PB[3][:, 0:N_ROWS]))
        copy(DCOL[:, :], PB[3][:, P:P + 8]).then_inc(S("cols"), 1)
        order.fence()
        for b in range(NB + 2):
            if b <= NB:
                rows = sample_rows(b)
                act.wait_ge(S(f"x_in{b}"), 16)
                if b > 0:
                    act.wait_ge(S("x_ss"), b)
                act.activation(SQJ[0:rows, :], XS[0:rows, b, :], ACT.Square, accum_out=SS[0:rows, b:b + 1]) \
                    .then_inc(S("x_ss"), 1)
            if b == 0:
                continue
            b -= 1
            rows = sample_rows(b)
            act.wait_ge(S("x_ms"), b + 1)
            act.activation(RT[0:rows, b:b + 1], MS[0:rows, b:b + 1], ACT.Sqrt).then_inc(S("x_rt"), 1)
        for w in range(2):
            split_high(tile_no(w, 1, 0))
        for q, (b0, nb, rows) in enumerate(QUADS):
            for k in range(KT):
                i = q * KT + k
                act.wait_ge(S("x_t"), i + 1)
                act.activation(HH[:, k, b0 * P:b0 * P + nb * rows], PB[3 + i % 4][:, 0:nb * rows], ACT.Copy,
                               scale=COLS[:, PRE0 + k:PRE0 + k + 1]).then_inc(S("h_hi"), 1)

        def conv_silu(n, out):
            act.wait_ge(S("conv"), n + 1)
            order(act.activation(out[:, 0:SEQ], ACC[:, 0:SEQ], ACT.Silu))
            act.activation(out[:, SEQ:TOK], ACC[:, SEQ + 3:CONVW], ACT.Silu).then_inc(S("conv_act"), 1)

        for j in range(4):
            w = tile_no(W_BC, 1, j)
            if j > 0:
                act.wait_ge(S("conv"), j)
            read_chunks(w, parted(XR, 3, SAMP))
            split_high(tile_no(W_BC, 1, j + 2))
            conv_silu(j, (BT, CT)[j // 2][:, j % 2, :])
        w = tile_no(W_DT, 1, 0)
        read_chunks(w, whole(RW[4], HEADS_B), rows=HEADS_B)
        split_high(tile_no(W_DT + 2, 1, 0))
        n = 0
        for g in range(GROUPS_B):
            for b0, nb, rows in QUADS:
                for what in range(2):
                    act.wait_ge(S("cb_mm"), n + 1)
                    width = rows if what == 0 else P
                    dst = (CBT, BTOK)[what][0:rows, g, b0:b0 + nb, 0:width]
                    src = PB[5 + n % 3][0:rows, 0:nb * P].rearrange("p (b c) -> p b c", c=P)[:, :, 0:width]
                    copy(dst, src).then_inc(S("cb_read"), 1)
                    n += 1

        def log1p_exp_steps(rows, neg, e, w1, lg, name, first):
            act.wait_ge(S(name), first)
            act.activation(e, neg, ACT.Exp).then_inc(S(name + "_a"), 1)
            act.wait_ge(S(name), first + 1)
            act.activation(lg, w1, ACT.Ln).then_inc(S(name + "_a"), 1)

        log1p_exp_steps(HEADS_B, RW[5][:, :], RW[6][:, :], RW[1][:, :], RW[2][:, :], "dtc", 1)
        act.wait_ge(S("par_in"), 64)
        act.activation(EAL[0:HEADS_B, :], AL[0:HEADS_B, :], ACT.Exp).then_inc(S("dtc_a"), 1)
        act.wait_ge(S("dtc"), 3)
        order(act.activation(RW[5][:, :], RW[5][:, :], ACT.Exp))
        act.activation(RW[3][:, :], ACSROW[:, :], ACT.Exp).then_inc(S("dtc_a"), 1)
        act.wait_ge(S("dt_turn"), 1)
        b3 = PB[3][:, 0:3 * 9 * HEADS_B].rearrange("p (q b h) -> p q b h", q=3, h=HEADS_B)
        b4 = PB[4][:, 0:9 * HEADS_B].rearrange("p (b h) -> p b h", h=HEADS_B)
        order(copy(TOKQ[:, 0:3, 0:NB, :], b3[:, :, 0:NB, :]))
        order(copy(TOKQ[0:DEC, 0:3, NB, :], b3[0:DEC, :, NB, :]))
        order(copy(TOKQ[:, 3, 0:NB, :], b4[:, 0:NB, :]))
        order(copy(TOKQ[0:DEC, 3, NB, :], b4[0:DEC, NB, :]))
        copy(DECB[:, :, :].rearrange("p h b -> p (h b)"), PB[4][:, 256:256 + 9 * HEADS_B]).then_inc(S("tokq"), 1)

        def read_x(t):
            act.wait_ge(S("conv"), 4 + t)
            read_chunks(tile_no(W_XZ, 2, t), parted(XR, 3, SAMP))
            split_high(tile_no(W_XZ + 2, 2, t))

        def read_gate(t):
            if isinstance(t, int) and t == 0:
                act.wait_ge(S("dt_rows"), 1)
                act.wait_ge(S("dt_turn"), 1)
            else:
                act.wait_ge(S("yb"), t)
            conv_silu(4 + t, XC)
            read_chunks(tile_no(W_XZ + 1, 2, t), whole(ZS), ACT.Silu)
            split_high(tile_no(W_XZ + 3, 2, t))

        def front(t):
            for n, (j, q) in enumerate(((0, 0), (0, 1), (1, 0), (1, 1), (0, 2), (1, 2))):
                b0, nb, rows = QUADS[q]
                act.wait_ge(S("seg"), 6 * t + n + 1)
                m = M[0:rows, j, b0:b0 + nb, 0:rows]
                act.activation(m, m, ACT.Exp).then_inc(S("mexp"), 1)
            act.wait_ge(S("fs_turn"), t + 1)
            if not isinstance(t, int) or t > 0:
                act.wait_ge(S("ssd_stored"), 32 * t)
            copy(FSO[:, :, :].rearrange("p j n -> p (j n)"), PB[5][:, 2 * P:4 * P]).then_inc(S("fs_out"), 1)

        read_x(0)
        read_gate(0)
        front(0)
        with order.loop(1, 8, 1) as t:
            read_x(t)
            read_gate(t)
            front(t)
        act.wait_ge(S("cst_turn"), 1)
        copy(CSO[:, :], PB[3][0:6 * XBC_TILES, 0:P]).then_inc(S("cso"), 1)
        act.wait_ge(S("yb"), 8)
        act.wait_ge(S("y_turn"), 24)

        def roots(src, name, at_count, done):
            act.wait_ge(S(name), at_count)
            act.activation(src, src, ACT.Sqrt).then_inc(S(done), 1)

        def inverse_root(x, done):
            order(act.activation(x, x, ACT.Ln))
            order.fence()
            act.activation(x, x, ACT.Exp, scale=-0.5).then_inc(S(done), 1)

        with order.loop(0, 4, 0) as i:
            act.wait_ge(S("v_turn"), 6 * i)
            for j, out in enumerate((VG, UG)):
                w = tile_no(W_V + j, 2, i)
                read_chunks(w, whole(out), ACT.Gelu)
                split_high(tile_no(W_V + j + 2, 2, i))
            roots(GSM[:, 2, 0:9], "v_ms", i + 1, "v_rt")
        act.wait_ge(S("gs_ms"), 6)
        inverse_root(RSY[:, :, :], "gs_rt")
        with order.loop(0, 8, 0) as t:
            act.wait_ge(S("ya"), t)
            read_chunks(tile_no(W_UZ, 2, t), whole(UG), ACT.Gelu)
            split_high(tile_no(W_UZ + 2, 2, t))
            read_chunks(tile_no(W_UZ + 1, 2, t), whole(ZG), ACT.Silu)
            split_high(tile_no(W_UZ + 3, 2, t))
        for k in range(8):
            act.wait_ge(S("yb_x"), k + 1)
            copy(HH[:, k, :], HX[:, k, :]).then_inc(S("hi"), 1)
        act.wait_ge(S("ya"), 8)
        for k in range(8):
            copy(YAH[:, k, :], YA[:, k, 0:TOK]).then_inc(S("ya_hi"), 1)
        with order.loop(0, 8, 0) as n:
            w0, w1 = tile_no(W_OE, 2, n), tile_no(W_OE + 1, 2, n)
            split_high(tile_no(W_OE + 2, 2, n))
            read_chunks(w1, whole(O0[:, n, :]))
            split_high(tile_no(W_OE + 3, 2, n))
        act.wait_ge(S("ss_ms"), 3)
        inverse_root(RSO, "ss_rt")
        for k in range(8):
            act.wait_ge(S("x1"), k + 1)
            if k > 0:
                act.wait_ge(S("x1_sq"), k)
            act.activation(TMP[:, :], O0[:, k, :], ACT.Square).then_inc(S("x1_s"), 1)
        act.wait_ge(S("ss_ms"), 6)
        inverse_root(RSO, "ss_rt")
        for k in range(8):
            act.wait_ge(S("h1_x"), k + 1)
            copy(HH[:, k, :], HX[:, k, :]).then_inc(S("hi"), 1)

        read_chunks(tile_no(W_F, 1, 0), whole(FW[0], HEADS_C), rows=HEADS_C)
        split_high(tile_no(W_F + 2, 1, 0))
        log1p_exp_steps(HEADS_C, FW[2][:, :], FW[3][:, :], FW[4][:, :], FW[5][:, :], "fc", 1)

        def turn_steps(t, attend=True, project=True):
            p = t + 1
            two = SEQ - 2 * CH

            def read(i):
                j, c = i // 3, i % 3
                w = tile_no(W_QKVZ + j, 4, p)
                act.wait_ge(S("p_chunk"), times(w, 3, c + 1))
                cols = slice(c * CH, (c + 1) * CH)
                if j == V_:
                    wait(act, "vt_turn", 3 * p + c - 2)
                    last = copy(VRAW[:, cols], PB[c][:, 0:CH])
                elif j == Z_:
                    last = copy(Y1[:, p, cols], PB[c][:, 0:CH])
                elif j == Q_:
                    wait(act, "sc_mm", 9 * p + 3 * c - 6)
                    last = copy(QT[:, cols], PB[c][:, 0:CH])
                else:
                    wait(act, "sc_mm", 9 * p)
                    for part, key in norm_chunk(3 + c):
                        last = copy(key, PB[c][:, part])
                last.then_inc(S(f"c_read{c}"), 1)
                if i == 5:
                    act.wait_ge(S("c_read2"), times(tile_no(W_QKVZ - 8 + Z_, 4, p), 1, 1))
                if c == 2:
                    split_high(tile_no(W_QKVZ + 2 + j, 4, p))
                if i == 5:
                    act.activation(Y1[:, p, :], Y1[:, p, :], ACT.Silu).then_inc(S("zs"), 1)

            def read_turned(dst, bank, rows, n, name):
                copy(dst, PB[bank][0:rows, 0:n * P].rearrange("p (b d) -> p b d", d=P)).then_inc(S(name), 1)

            def nf_read(c, bank):
                act.wait_ge(S("nf_mm"), 3 * p + c + 1)
                c0, c1 = c * 512, min(KEYS, c * 512 + 512)
                copy(NFB[:, c0:c1], PB[bank][:, 0:c1 - c0]).then_inc(S("nf"), 1)

            def probs_read(b):
                blocks = b + 1 if b < NB else 3
                for g in range(0, blocks, 4):
                    nb = min(4, blocks - g)
                    act.wait_ge(S("p_turn"), 13 * t + groups_before(b) + g // 4 + 1)
                    if g == 0:
                        wait(act, "pv", 9 * t + b)
                    bank = PB[5 + g // 4]
                    if b < NB:
                        last = copy(PT[:, g:g + nb, :], bank[:, 0:nb * P].rearrange("p (b l) -> p b l", l=P))
                    else:
                        src = bank[:, 0:3 * P].rearrange("p (b l) -> p b l", l=P)
                        copy(PT[:, 0:2, 0:DEC], src[:, 0:2, 0:DEC])
                        last = copy(PT[0:DEC, 2, 0:DEC], src[0:DEC, 2, 0:DEC])
                    last.then_inc(S("pt_read"), 1)

            for i in range(STEPS):
                if project:
                    read(i)
                if attend and i == 0:
                    act.wait_ge(S("vt_turn"), 3 * t + 2)
                    read_turned(VTOK[:, 4:8, :], 6, P, 4, "vt_read")
                if attend and i == 1:
                    act.wait_ge(S("vt_turn"), 3 * t + 3)
                    read_turned(VTOK[0:DEC, NB + 2:NB + 3, :], 4, DEC, 1, "vt_read")
                    act.wait_ge(S("n_ms"), 6 * t + 6)
                    inverse_root(NRM[:, 0:5:4, :], "n_rt")
                if attend and i == 2:
                    wait(act, "k_stored", 32 * t)
                    for q, bank in ((0, 6), (1, 4)):
                        act.wait_ge(S("kt_turn"), 3 * t + q + 1)
                        read_turned(KTOK[:, 4 * q:4 * q + 4, :], bank, P, 4, "k_tok")
                if attend and i == 3:
                    act.wait_ge(S("kt_turn"), 3 * t + 3)
                    copy(KSAM, PB[6][0:DEC, 0:P]).then_inc(S("k_tok"), 1)
                if attend and 1 <= i <= NB + 1:
                    probs_read(i - 1)
                if project and i == 10:
                    act.wait_ge(S("kc_turn"), p + 1)
                    copy(KALL[:, SEQ:SEQ + PAST], PB[6][:, 0:PAST]).then_inc(S("kc_done"), 1)
                    nf_read(0, 3)
                if project and i == 11:
                    act.wait_ge(S("vt_turn"), 3 * p + 1)
                    wait(act, "pv", 9 * p)
                    wait(act, "v_stored", 32 * p)
                    read_turned(VTOK[:, 0:4, :], 6, P, 4, "vt_read")
                    nf_read(1, 3)
                    nf_read(2, 5)
                if project and i == 10:
                    act.wait_ge(S("n_ms"), 6 * p + 4)
                    inverse_root(NRM[:, 0:4, :], "n_rt")
                if attend and i <= NB:
                    act.wait_ge(S("sm"), 9 * t + i + 1)
                    rows = sample_rows(i)
                    width = PAST + DEC if i == NB else (i + 1) * P
                    act.activation(SB[0:rows, 0:width], SB[0:rows, 0:width], ACT.Exp, scale=SCALE,
                                   bias=NBIAS[0:rows, :], accum_out=RSUM[0:rows, :]).then_inc(S("ex"), 1)
                if not project and 1 <= i < 8:
                    act.wait_ge(S("p_chunk"), 3 * W_OO)
                    copy(HH[:, i - 1, :], Y1[:, i - 1, :]).then_inc(S("hi"), 1)

        act.wait_ge(S("lt"), 1)
        act.wait_ge(S("lf_stored"), 32)
        turn_steps(-1, attend=False)
        with order.loop(0, 7, 2) as t:
            turn_steps(t)
        turn_steps(7, project=False)
        act.wait_ge(S("y_read"), 72)
        copy(HH[:, 7, :], Y1[:, 7, :]).then_inc(S("hi"), 1)

        def out_odd(i, j, more):
            n = tile_no(W_OO + j, 2, i)
            k = 2 * i + j
            read_chunks(n, whole(O1[:, k, :]))
            if more:
                split_high(tile_no(W_OO + j + 2, 2, i))

        act.wait_ge(S("y1_lo"), 8)
        with act.Fori(0, 3) as i:
            out_odd(i, 0, True)
            out_odd(i, 1, True)
        out_odd(3, 0, False)
        out_odd(3, 1, False)
        act.wait_ge(S("ss_ms"), 9)
        inverse_root(RSO, "ss_rt")
        for k in range(8):
            for q, (b0, nb, rows) in enumerate(QUADS):
                bank, off = ((3, 4, 5), (6, 7, 0))[k % 2][q], 0
                act.wait_ge(S("o_turn"), 3 * k + q + 1)
                if q == 0 and k >= 2:
                    act.wait_ge(S(f"y_stored{k % 2}"), 32 * (k // 2))
                copy(YO[0:rows, k % 2, b0:b0 + nb, :],
                     PB[bank][0:rows, off:off + nb * P].rearrange("p (b d) -> p b d", d=P)).then_inc(S("y_tok"), 1)

    @block.vector
    def _(dve):
        order = Order(dve, S("dve_order"))

        def tt(out, a, b, op):
            return dve.tensor_tensor(out, a, b, op)

        def ts(out, a, s1, s2, op0, op1=ALU.bypass):
            return dve.tensor_scalar(out, a, s1, s2, op0, op1) if s2 is not None else \
                dve.tensor_scalar(out, a, s1, None, op0)

        def stt(out, a, s, b, op0, op1):
            return dve.scalar_tensor_tensor(out=out, in0=a, scalar=s, in1=b, op0=op0, op1=op1)

        order(dve.memset(ONES[:, :], 1.0))
        dve.wait_ge(S("rows_in"), 160)
        dve.tensor_copy(DEXP[:, :, :], DSM[:, :].unsqueeze(2).broadcast_to([8, 2, HP])).then_inc(S("dexp"), 1)
        for b in range(NB + 2):
            if b <= NB:
                rows = sample_rows(b)
                dve.wait_ge(S("x_ss"), b + 1)
                ts(MS[0:rows, b:b + 1], SS[0:rows, b:b + 1], 1.0 / D, EPS, ALU.mult, ALU.add).then_inc(S("x_ms"), 1)
            if b == 0:
                continue
            b -= 1
            rows = sample_rows(b)
            dve.wait_ge(S("x_rt"), b + 1)
            order(dve.reciprocal(RR[0:rows, b:b + 1], RT[0:rows, b:b + 1]))
            order.fence()
            ts(XS[0:rows, b, :], XS[0:rows, b, :], RR[0:rows, b:b + 1], None, ALU.mult).then_inc(S("xn"), 1)
        for q, (b0, nb, rows) in enumerate(QUADS):
            for k in range(KT):
                i = q * KT + k
                cols = slice(b0 * P, b0 * P + nb * rows)
                dve.wait_ge(S("h_hi"), i + 1)
                stt(HL[:, k, cols], PB[3 + i % 4][:, 0:nb * rows], COLS[:, PRE0 + k:PRE0 + k + 1],
                    HH[:, k, cols].bitcast(f32), ALU.mult, ALU.subtract).then_inc(S("h_lo"), 1)

        def conv(n, tile, w):
            dve.wait_ge(S("c_read2"), times(w, 1, 1))
            if not isinstance(n, int) or n > 0:
                dve.wait_ge(S("conv_act"), n)
            past = COLS[:, CTX:CTX + 36].rearrange("p (r t) -> p r t", t=XBC_TILES)
            order(dve.tensor_copy(XR[:, 3 + SEQ:SAMP], past[:, :, tile]))
            order(dve.tensor_copy(CST[:, 0:3, tile], XR[:, SEQ:SEQ + 3]))
            order(dve.tensor_copy(CST[:, 3:6, tile], XR[:, SAMP + DEC - 3:SAMP + DEC]))
            order.fence()
            taps = CONVW_SB[:, tile, :]
            order(ts(ACC[:, :], XR[:, 0:CONVW], taps[:, 0:1], COLS[:, CONVB:CONVB + XBC_TILES][:, bass.ds(tile, 1)],
                     ALU.mult, ALU.add))
            for k in range(1, TAPS):
                order.fence()
                ins = stt(ACC[:, :], XR[:, k:k + CONVW], taps[:, k:k + 1], ACC[:, :], ALU.mult, ALU.add)
                if k < TAPS - 1:
                    order(ins)
            ins.then_inc(S("conv"), 1)

        dve.wait_ge(S("par_in"), 64)
        dve.wait_ge(S("p_chunk"), 1)
        order(dve.memset(XR[:, 0:3], 0.0))
        for j in range(4):
            conv(j, 8 + j, tile_no(W_BC, 1, j))

        def log1p_exp(raw, bias, x, neg, e, w1, lg, c, name, first):
            order(ts(x, raw, bias, None, ALU.add))
            order.fence()
            order(ts(neg, x, -1.0, None, ALU.mult))
            order.fence()
            tt(neg, x, neg, ALU.min).then_inc(S(name), 1)
            dve.wait_ge(S(name + "_a"), 1)
            ts(w1, e, 1.0, None, ALU.add).then_inc(S(name), 1)
            dve.wait_ge(S(name), 2)
            order(ts(c, w1, -1.0, None, ALU.add))
            order(dve.reciprocal(neg, w1))
            order.fence()
            order(tt(c, e, c, ALU.subtract))
            order.fence()
            order(tt(c, c, neg, ALU.mult))
            order.fence()
            dve.wait_ge(S(name + "_a"), 2)
            order(tt(lg, lg, c, ALU.add))
            order.fence()

        dve.wait_ge(S("c_read2"), W_DT + 1)
        log1p_exp(RW[4][:, :], DTB[0:HEADS_B, :], RW[0][:, :], RW[5][:, :], RW[6][:, :], RW[1][:, :], RW[2][:, :],
                  RW[7][:, :], "dtc", 1)
        order(stt(RW[0][:, :], RW[0][:, :], 0.0, RW[2][:, :], ALU.max, ALU.add))
        order.fence()
        dve.wait_ge(S("dtc_a"), 3)
        order(ts(RW[6][:, :], RW[0][:, :], EAL[0:HEADS_B, :], -1.0, ALU.mult, ALU.mult))
        order(dve.memset(RW[4][:, :], 1.0))
        order.fence()
        order(dve.memset(RW[4][:, 0:TOK:P], 0.0))
        order.fence()
        order(dve.tensor_tensor_scan(ACSROW[:, :], RW[4][:, :], RW[6][:, :], 0.0, ALU.mult, ALU.add))
        order.fence()
        ends = ACSROW[:, P - 1:SEQ:P]
        order(tt(RW[5][:, 0:SEQ].rearrange("h (b l) -> h b l", l=P), ends.unsqueeze(2).broadcast_to([HEADS_B, NB, P]),
                 ACSROW[:, 0:SEQ].rearrange("h (b l) -> h b l", l=P), ALU.subtract))
        tt(RW[5][:, SEQ:TOK], ACSROW[:, TOK - 1:TOK].broadcast_to([HEADS_B, DEC]), ACSROW[:, SEQ:TOK], ALU.subtract) \
            .then_inc(S("dtc"), 1)
        dve.wait_ge(S("dtc_a"), 4)
        order(tt(RW[2][:, :], RW[5][:, :], RW[0][:, :], ALU.mult))
        one = IDENT[0:HEADS_B, 0:HEADS_B].unsqueeze(2)
        order(tt(DECR[:, :, 0:NB], one.broadcast_to([HEADS_B, HEADS_B, NB]),
                 RW[3][:, P - 1:SEQ:P].unsqueeze(1).broadcast_to([HEADS_B, HEADS_B, NB]), ALU.mult))
        tt(DECR[:, :, NB:NB + 1], one,
           RW[3][:, TOK - 1:TOK].unsqueeze(1).broadcast_to([HEADS_B, HEADS_B, 1]), ALU.mult).then_inc(S("dt_rows"), 1)

        def heads_of(q, t, b0, nb, rows):
            return TOKQ[0:rows, q, b0:b0 + nb, bass.ds(2 * t, 2)].unsqueeze(3).broadcast_to([rows, nb, 2, HP])

        def front(g, t):
            if not isinstance(t, int) or t > 0:
                dve.wait_ge(S("bc"), 6 * t)
            if isinstance(t, int) and t == 0:
                dve.wait_ge(S("tokq"), 1)
            order(ts(SEL[:, 0, :], ONES[0:HEADS_B, :], IDENT[0:HEADS_B, bass.ds(2 * t, 1)], None, ALU.mult))
            ts(SEL[:, 1, :], ONES[0:HEADS_B, :], IDENT[0:HEADS_B, bass.ds(2 * t + 1, 1)], None, ALU.mult) \
                .then_inc(S("sel"), 1)
            for q, (b0, nb, rows) in enumerate(QUADS):
                dve.wait_ge(S("xc_turn"), 3 * t + q + 1)
                src = PB[3 + q][0:rows, 0:nb * P].rearrange("p (b j d) -> p b j d", j=2, d=HP)
                for i, dst in enumerate((XD, XW)):
                    last = tt(dst[0:rows, b0:b0 + nb, :].rearrange("p b (j d) -> p b j d", j=2), src,
                              heads_of(i, t, b0, nb, rows), ALU.mult)
                last.then_inc(S("xw"), 1)

            def decays(n):
                j, q = ((0, 0), (0, 1), (1, 0), (1, 1), (0, 2), (1, 2))[n]
                b0, nb, rows = QUADS[q]
                dve.wait_ge(S("bc"), 6 * t + n + 1)
                for i in range(nb):
                    last = stt(M[0:rows, j, b0 + i, 0:rows], PB[6 + n % 2][0:rows, i * P:i * P + rows],
                               TOKQ[0:rows, 3, b0 + i, bass.ds(2 * t + j, 1)], MASKT[0:rows, 0:rows],
                               ALU.subtract, ALU.min)
                last.then_inc(S("seg"), 1)

            decays(0)
            decays(1)
            dve.wait_ge(S("ds"), 3 * t + 3)
            if not isinstance(t, int) or t > 0:
                dve.wait_ge(S("fs_turn"), t)
            order(dve.memset(ST[:, 0, :], 0.0))
            order(dve.tensor_copy(ST[:, 1, :], PB[3][:, 0:P]))
            dve.wait_ge(S("si_used"), t + 1)
            order(dve.tensor_copy(ST[:, NB, :], PB[5][:, P:2 * P]))
            for b in range(1, NB + 1):
                order.fence()
                dst = ST[:, b + 1, :] if b < NB - 1 else FS[:, b - NB + 1, :]
                new = PB[3 + b // 4][:, (b % 4) * P:(b % 4 + 1) * P]
                for i in range(2):
                    cols = slice(i * HP, (i + 1) * HP)
                    ins = stt(dst[:, cols], ST[:, b, cols], DECB[:, bass.ds(2 * t + i, 1), b:b + 1].rearrange("p a b -> p (a b)"),
                              new[:, cols], ALU.mult, ALU.add)
                    if b < NB or i == 0:
                        order(ins)
            ins.then_inc(S("st"), 1)
            for n in range(2, 6):
                decays(n)
            for n, (j, q) in enumerate(((0, 0), (0, 1), (1, 0), (1, 1), (0, 2), (1, 2))):
                b0, nb, rows = QUADS[q]
                dve.wait_ge(S("mexp"), 6 * t + n + 1)
                m = M[0:rows, j, b0:b0 + nb, 0:rows]
                tt(m, m, CBT[0:rows, g, b0:b0 + nb, 0:rows], ALU.mult).then_inc(S("m"), 1)

        def back(t):
            for q, (b0, nb, rows) in enumerate(QUADS):
                intra, state = PB[(3, 5, 7)[q]], PB[(4, 6, 7)[q]]
                off = P if q == 2 else 0
                dve.wait_ge(S("y_mm"), 3 * t + q + 1)
                yt = YT[0:rows, b0:b0 + nb, :]
                order(tt(yt.rearrange("p b (j d) -> p b j d", j=2),
                         state[0:rows, off:off + nb * P].rearrange("p (b j d) -> p b j d", j=2, d=HP),
                         heads_of(2, t, b0, nb, rows), ALU.mult))
                order.fence()
                tt(yt, yt, intra[0:rows, 0:nb * P].rearrange("p (b d) -> p b d", d=P), ALU.add).then_inc(S("yt"), 1)
            for q, (b0, nb, rows) in enumerate(QUADS):
                cols = slice(b0 * P, b0 * P + nb * rows)
                dve.wait_ge(S("y_turn"), 3 * t + q + 1)
                stt(YB[:, t, cols], XC[:, cols], DCOL[:, bass.ds(t, 1)], PB[3 + q][:, 0:nb * rows], ALU.mult, ALU.add) \
                    .then_inc(S("yf"), 1)
            dve.wait_ge(S("yf"), 3 * t + 3)
            dve.wait_ge(S("c_read2"), times(tile_no(W_XZ + 1, 2, t), 1, 1))
            tt(YB[:, t, :], YB[:, t, :], ZS[:, :], ALU.mult).then_inc(S("yb"), 1)

        PAIR = 28
        for g in range(GROUPS_B):
            t0 = 4 * g
            conv(4 + t0, t0, tile_no(W_XZ, 2, t0))
            front(g, t0)
            with order.loop(t0 + 1, t0 + 4, PAIR) as t:
                back(t - 1)
                conv(4 + t, t, tile_no(W_XZ, 2, t))
                front(g, t)
            back(t0 + 3)

        dve.wait_ge(S("cso"), 1)
        dve.wait_ge(S("ssd_stored"), 256)
        dve.wait_ge(S("conv_stored"), 96)
        dve.wait_ge(S("yb"), 8)
        order(dve.memset(V[:, :, NB * P:], 0.0))
        order(dve.memset(RSY[:, :, :], 0.0))
        order.fence()
        dve.wait_ge(S("gv_in"), 48)
        for g in range(GROUPS_B):
            with order.loop(2 * g, 2 * g + 2, 9) as i:
                for j in range(2):
                    for q, (b0, nb, rows) in enumerate(QUADS):
                        bank = (3, 4, 5, 6, 7, 3)[3 * j + q]
                        dve.wait_ge(S("v_turn"), 6 * i + 3 * j + q + 1)
                        dve.tensor_copy(V[0:rows, 2 * i + j, b0 * P:(b0 + nb) * P], PB[bank][0:rows, 0:nb * P]) \
                            .then_inc(S("v_tok"), 1)
                dve.wait_ge(S("v_tok"), 6 * i + 6)
                vj = [V[:, 2 * i + j, :].rearrange("p (b f) -> p b f", f=P) for j in range(2)]
                for j in range(2):
                    order(tt(SQV[:, :, j * P:(j + 1) * P], vj[j], vj[j], ALU.mult))
                order.fence()
                order(dve.tensor_reduce(GSM[:, 0, 0:9], SQV[:, :, :], AX.X, ALU.add))
                order.fence()
                ts(GSM[:, 2, 0:9], GSM[:, 0, 0:9], 1.0 / (2 * P), EPS, ALU.mult, ALU.add).then_inc(S("v_ms"), 1)
                for j in range(2):
                    yb = YB[:, 2 * i + j, :]
                    order(tt(TMP[:, :], yb, yb, ALU.mult))
                    order.fence()
                    tt(RSY[:, g, :], RSY[:, g, :], TMP[:, :], ALU.add).then_inc(S("y_sq"), 1)
                    dve.wait_ge(S("y_sq"), 2 * i + j + 1)
                dve.wait_ge(S("v_rt"), i + 1)
                order(dve.reciprocal(GSM[:, 3, 0:9], GSM[:, 2, 0:9]))
                order.fence()
                for j in range(2):
                    order(tt(vj[j], vj[j], GSM[:, 3, 0:9].unsqueeze(2).broadcast_to([P, 9, P]), ALU.mult))
                order.fence()
                order(tt(vj[0], vj[0], GVB[:, i, 0:P].unsqueeze(1).broadcast_to([P, 9, P]), ALU.mult))
                order.fence()
                tt(vj[1], vj[1], GVB[:, i, P:2 * P].unsqueeze(1).broadcast_to([P, 9, P]), ALU.mult) \
                    .then_inc(S("v_normed"), 1)
        for n in range(6):
            g, c = n // 3, n % 3
            dve.wait_ge(S("gs_mm"), 3 * g + 3 if n < 5 else 6)
            dve.wait_ge(S("gs_mm"), n + 1)
            ts(RSY[:, g, c * CH:(c + 1) * CH], PB[(3, 4, 5, 6, 7, 3)[n]][:, 0:CH], 1.0 / 512, EPS, ALU.mult, ALU.add) \
                .then_inc(S("gs_ms"), 1)
        dve.wait_ge(S("ws_turn"), 1)
        order(dve.tensor_copy(WT[:, :, :].rearrange("p g i -> p (g i)"), PB[6][:, :]))
        order.fence()
        dve.memset(WT[P // 2:P, :, 0:P // 2], 0.0).then_inc(S("wt"), 1)
        dve.wait_ge(S("gs_rt"), 1)
        dve.wait_ge(S("gv_stored"), 16)
        with order.loop(0, 4, 2) as i:
            for j in range(2):
                t = 2 * i + j
                if j == 0:
                    dve.wait_ge(S("s_mm"), 6 * i)
                else:
                    dve.wait_ge(S("s_mm"), 6 * i + 3)
                dve.tensor_copy(VS[:, :, :], V[:, t, :].rearrange("p (b f) -> p b f", f=P)).then_inc(S("vs"), 1)
                dve.wait_ge(S("c_read2"), 31 + 4 * i + 2 * j)
                order(tt(UG[:, :], UG[:, :], ZG[:, :], ALU.mult))
                order.fence()
                for q, (b0, nb, rows) in enumerate(QUADS):
                    dve.wait_ge(S("s_mm"), 6 * i + 3 * j + q + 1)
                    tt(ZG[:, b0 * P:b0 * P + nb * rows].rearrange("p (b l) -> p b l", l=rows),
                       PB[3 + q][:, 0:nb * rows].rearrange("p (b l) -> p b l", l=rows),
                       BSB[:, i, 0:rows].unsqueeze(1).broadcast_to([P, nb, rows]), ALU.add).then_inc(S("s_read"), 1)
                dve.wait_ge(S("s_read"), 6 * i + 3 * j + 3)
                dve.wait_ge(S("vs"), t + 1)
                tt(YA[:, t, 0:TOK], ZG[:, :], UG[:, :], ALU.mult).then_inc(S("ya"), 1)

        dve.wait_ge(S("p_chunk"), 3 * W_OE)
        for k in range(9):
            if k < 8:
                stt(HX[:, k, :], YB[:, k, :], COLS[:, GSSD + k:GSSD + k + 1], RSY[:, k // 4, :], ALU.mult, ALU.mult) \
                    .then_inc(S("yb_x"), 1)
            if k > 0:
                dve.wait_ge(S("hi"), k)
                tt(HL[:, k - 1, :], HX[:, k - 1, :], HH[:, k - 1, :].bitcast(f32), ALU.subtract).then_inc(S("yb_lo"), 1)
        for k in range(8):
            dve.wait_ge(S("ya_hi"), k + 1)
            tt(YAL[:, k, :], YA[:, k, 0:TOK], YAH[:, k, :].bitcast(f32), ALU.subtract).then_inc(S("ya_lo"), 1)

        def add_squares(tile, last, sem):
            order(tt(TMP[:, :], tile, tile, ALU.mult))
            order.fence()
            tt(SQA, SQA, TMP[:, :], ALU.add).then_inc(S(sem), 1)

        dve.wait_ge(S("yb_lo"), 8)
        order(dve.memset(SQA, 0.0))
        order.fence()
        with order.loop(0, 8, 1) as n:
            dve.wait_ge(S("c_read2"), times(tile_no(W_OE, 1, n), 1, 1))
            if True:
                dve.wait_ge(S("o_sq"), n)
            add_squares(O0[:, n, :], None, "o_sq")

        def rstd(first):
            for c in range(3):
                dve.wait_ge(S("ss_mm"), first + c + 1)
                ts(RSO[:, c * CH:(c + 1) * CH], PB[3 + c][:, 0:CH], 1.0 / D, EPS, ALU.mult, ALU.add) \
                    .then_inc(S("ss_ms"), 1)
            dve.wait_ge(S("ss_rt"), first // 3 + 1)

        rstd(0)
        order(dve.memset(SQA, 0.0))
        order.fence()
        for k in range(9):
            if k < 8:
                order(stt(O0[:, k, :], O0[:, k, :], COLS[:, POST0 + k:POST0 + k + 1], RSO, ALU.mult, ALU.mult))
                order.fence()
                dve.wait_ge(S("x_turn"), k + 1)
                for q, (b0, nb, rows) in enumerate(QUADS):
                    bank = ((3, 4, 5), (6, 7, 0))[k % 2][q]
                    cols = slice(b0 * P, b0 * P + nb * rows)
                    last = tt(O0[:, k, cols], O0[:, k, cols], PB[bank][:, 0:nb * rows], ALU.add)
                last.then_inc(S("x1"), 1)
            if k > 0:
                dve.wait_ge(S("x1_s"), k)
                if k > 1:
                    dve.wait_ge(S("x1_sq"), k - 1)
                tt(SQA, SQA, TMP[:, :], ALU.add).then_inc(S("x1_sq"), 1)
        rstd(3)
        for k in range(9):
            if k < 8:
                stt(HX[:, k, :], O0[:, k, :], COLS[:, PRE1 + k:PRE1 + k + 1], RSO, ALU.mult, ALU.mult) \
                    .then_inc(S("h1_x"), 1)
            if k > 0:
                dve.wait_ge(S("hi"), 8 + k)
                tt(HL[:, k - 1, :], HX[:, k - 1, :], HH[:, k - 1, :].bitcast(f32), ALU.subtract).then_inc(S("h1_lo"), 1)

        dve.wait_ge(S("c_read2"), W_F - 8 + 1)
        log1p_exp(FW[0][:, :], BF[0:HEADS_C, :], FW[1][:, :], FW[2][:, :], FW[3][:, :], FW[4][:, :], FW[5][:, :],
                  FW[0][:, :], "fc", 1)
        order(ts(FW[1][:, :], FW[1][:, :], 0.0, None, ALU.min))
        order.fence()
        order(tt(LROW[:, 0:SEQ], FW[1][:, 0:SEQ], FW[5][:, 0:SEQ], ALU.subtract))
        order(tt(LROW[:, SEQ + PAST:KEYS], FW[1][:, SEQ:TOK], FW[5][:, SEQ:TOK], ALU.subtract))
        dve.wait_ge(S("clf_turn"), 1)
        dve.tensor_copy(LROW[:, SEQ:SEQ + PAST], PB[3][0:HEADS_C, 0:PAST]).then_inc(S("lrow"), 1)
        order(dve.memset(ONEROW[:, :], 1.0))
        order.fence()
        order(dve.memset(ONEROW[:, 0:KEYS:SEQ], 0.0))
        order.fence()
        dve.wait_ge(S("lrow"), 1)
        order(dve.tensor_tensor_scan(NFROW[:, :], ONEROW[:, :], LROW[:, :], 0.0, ALU.mult, ALU.add))
        order.fence()
        order(ts(NFROW[:, :], NFROW[:, :], -1.0 / SCALE, None, ALU.mult))
        dve.wait_ge(S("lt_turn"), 1)
        order(dve.tensor_copy(LT[:, 0:NB, :], PB[4][:, 0:NB * HEADS_C].rearrange("p (b h) -> p b h", h=HEADS_C)))
        dve.tensor_copy(LT[0:DEC, NB, :], PB[4][0:DEC, NB * HEADS_C:(NB + 1) * HEADS_C]).then_inc(S("lt"), 1)
        order.fence()
        dve.wait_ge(S("masks"), 2)
        dve.wait_ge(S("lf_stored"), 32)

        def turn_steps(t, attend=True, project=True):
            p = t + 1

            def mean_square(h, n, bank):
                dve.wait_ge(S("n_ss"), 6 * h + n + 1)
                ts(NRM[:, NORM_SLOT[n], :], PB[bank][:, 0:CH], 1.0 / P, EPS, ALU.mult, ALU.add).then_inc(S("n_ms"), 1)

            def norms(h, chunks, count):
                dve.wait_ge(S("n_rt"), 2 * h + count)
                for n in chunks:
                    gain = GQ if n < 3 else GK
                    for cols, x in norm_chunk(n):
                        last = stt(x, x, COLS[:, gain:gain + 1], NRM[:, NORM_SLOT[n], cols], ALU.mult, ALU.mult)
                last.then_inc(S("n_done"), 1)

            for i in range(STEPS):
                if attend and 2 <= i <= NB + 2:
                    b = i - 2
                    rows = sample_rows(b)
                    if b == 0:
                        dve.wait_ge(S("zs"), t + 1)
                    dve.wait_ge(S("pv"), 9 * t + b + 1)
                    y = Y1[:, t, b * P:b * P + rows]
                    tt(y, PB[7][:, 0:rows], y, ALU.mult).then_inc(S("y_read"), 1)
                if attend and i <= NB:
                    rows = sample_rows(i)
                    if i == 0:
                        dve.wait_ge(S("nf"), 3 * t + 3)
                    dve.wait_ge(S("sc_mm"), 9 * t + i + 1)
                    wait(dve, "p_turn", 13 * t + groups_before(i))
                    key0, width = (SEQ, PAST + DEC) if i == NB else (0, (i + 1) * P)
                    n = (width + 511) // 512
                    order(dve.memset(MX[0:rows, n:n + 1], -3.0e38))
                    for k in range(n):
                        c0, c1 = k * 512, min(width, k * 512 + 512)
                        order(dve.tensor_tensor_reduce(SB[0:rows, c0:c1], PB[3 + k][0:rows, 0:c1 - c0],
                                                       NFB[0:rows, key0 + c0:key0 + c1], 1.0, -3.0e38,
                                                       ALU.add, ALU.max, MX[0:rows, k:k + 1]))
                    order.fence()
                    order(dve.tensor_reduce(MXR[0:rows, :], MX[0:rows, 0:n + 1], AX.X, ALU.max))
                    order.fence()
                    ts(NBIAS[0:rows, :], MXR[0:rows, :], -SCALE, None, ALU.mult).then_inc(S("sm"), 1)
                if attend and i == 0:
                    mean_square(t, 5, 4)
                if attend and i == 1:
                    norms(t, (4, 5), 2)
                if project and i == 8:
                    mean_square(p, 0, 4)
                if project and i == 9:
                    mean_square(p, 1, 4)
                    mean_square(p, 2, 6)
                    wait(dve, "nf_mm", 3 * p)
                    ts(SEL8[:, :], ONES[0:HEADS_C, :], IDENT[0:HEADS_C, bass.ds(p, 1)], None, ALU.mult) \
                        .then_inc(S("sel8"), 1)
                if project and i == 10:
                    mean_square(p, 3, 4)
                if project and i == 11:
                    norms(p, (0, 1, 2, 3), 1)
                    mean_square(p, 4, 4)
                if attend and i <= NB:
                    dve.wait_ge(S("ex"), 9 * t + i + 1)
                    order(dve.reciprocal(RINV[0:rows, :], RSUM[0:rows, :]))
                    order.fence()
                    ts(SB[0:rows, 0:width], SB[0:rows, 0:width], RINV[0:rows, :], None, ALU.mult).then_inc(S("pn"), 1)
                if not project and 2 <= i < 9:
                    low_of_y(i - 2)

        def low_of_y(k):
            dve.wait_ge(S("hi"), 16 + k + 1)
            tt(HL[:, k, :], Y1[:, k, :], HH[:, k, :].bitcast(f32), ALU.subtract).then_inc(S("y1_lo"), 1)

        turn_steps(-1, attend=False)
        with order.loop(0, 7, 40) as t:
            turn_steps(t)
        turn_steps(7, project=False)
        low_of_y(7)
        order(dve.memset(SQA, 0.0))
        order.fence()
        with order.loop(0, 8, 1) as n:
            dve.wait_ge(S("c_read2"), times(tile_no(W_OO - 8, 1, n), 1, 1))
            dve.wait_ge(S("o_sq"), 8 + n)
            add_squares(O1[:, n, :], None, "o_sq")
        rstd(6)
        for k in range(8):
            order(stt(O1[:, k, :], O1[:, k, :], COLS[:, POST1 + k:POST1 + k + 1], RSO, ALU.mult, ALU.mult))
            order.fence()
            tt(O1[:, k, :], O1[:, k, :], O0[:, k, :], ALU.add).then_inc(S("x2"), 1)

    ctx.close()


_INS = ["x_prompt", "x_sample", "cache_fox_k", "cache_fox_v", "cache_fox_logf", "state_ssd", "state_conv",
        "norm_pre", "norm_post", "w_in_even", "w_out_even", "gmlp_ws", "gmlp_bs", "gmlp_gv",
        "ssd_conv_w", "ssd_conv_b", "ssd_dt_bias", "ssd_a_log", "ssd_d", "ssd_norm_g",
        "w_in_odd", "fox_b_forget", "w_out_odd", "fox_gq", "fox_gk"]
_OUTS = [(1, 1024, 1024), (1, 32, 1024),
         (1, 1, 1024, 8, 128), (1, 1, 1024, 8, 128), (1, 1, 1024, 8),
         (1, 1, 16, 64, 128), (1, 1, 3, 1536),
         (1, 1, 32, 8, 128), (1, 1, 32, 8, 128), (1, 1, 32, 8),
         (1, 1, 16, 64, 128), (1, 1, 3, 1536), (1, 1, 32, 1024)]


def kernel(**inputs):
    import numpy as _np
    import concourse.bacc as _bacc
    from concourse import mybir as _mybir
    from concourse.bass_utils import run_bass_kernel_spmd as _run

    nc = _bacc.Bacc("TRN2", target_bir_lowering=False, num_devices=1)
    arrays, args = {}, []
    for name in _INS:
        a = _np.ascontiguousarray(inputs[name])
        arrays[f"in_{name}_dram"] = a
        args.append(nc.dram_tensor(f"in_{name}_dram", a.shape, _mybir.dt.from_np(a.dtype), kind="ExternalInput").ap())
    for i, shape in enumerate(_OUTS):
        args.append(nc.dram_tensor(f"out_{i}_dram", shape, _mybir.dt.float32, kind="ExternalOutput").ap())
    hybrid_trunk(nc, *args)
    r = _run(nc, [arrays], core_ids=[0])
    return tuple(r.results[0][f"out_{i}_dram"] for i in range(len(_OUTS)))
```

```python
import concourse.bass as bass
from concourse import mybir
from contextlib import ExitStack, contextmanager

f32 = mybir.dt.float32
f32r = mybir.dt.float32r
bf16 = mybir.dt.bfloat16
ALU = mybir.AluOpType
ACT = mybir.ActivationFunctionType
AX = mybir.AxisListType

P = 128
D = 1024
KT = D // P
SEQ, DEC = 1024, 32
TOK = SEQ + DEC
NB = SEQ // P
CH = TOK // 3
PAST = 256
EPS = 1e-6
EVEN_IN, XBC0, DT0 = 5648, 4096, 5632
XBC_TILES = 12
HEADS_B, GROUPS_B, HP = 16, 2, 64
A_GROUPS = 4
HEADS_C = 8
SCALE = float(P) ** -0.5
TAPS = 4
PADW = 3 + SEQ + 3 + DEC
CONVW = PADW - 3
SAMP = 3 + SEQ + 3
KEYS = SEQ + PAST + DEC
NEG = -30000.0
NEGBIG = -1e30
LN_EXP_SET = 6

W_DT, W_BC, W_XZ, W_V, W_UZ, W_OE, W_F, W_QKVZ, W_OO = 0, 1, 5, 21, 29, 45, 61, 62, 94

PRE0, POST0, PRE1, POST1, GSSD, CONVB, GQ, GK, CTX = 0, 8, 16, 24, 32, 40, 52, 53, 54
N_ROWS = CTX + 36
QUADS = [(0, 4, P), (4, 4, P), (8, 1, DEC)]


def tile_no(first, per, t):
    return first, per, t


def times(w, k, add):
    first, per, t = w
    return first * k + add + per * k * t


def loads_of_slot(w):
    first, per, t = w
    if per == 1:
        assert isinstance(t, int)
        first, t = first + t, 0
    return 16 * (first // 2 + 1) + 16 * (per // 2) * t


def slot(w):
    first, per, t = w
    return (first + (t if per == 1 else 0)) % 2


class Order:

    def __init__(self, eng, sem):
        self.eng, self.sem, self.base, self.n = eng, sem, 0, 0

    def __call__(self, ins):
        ins.then_inc(self.sem, 1)
        self.n += 1
        return ins

    def fence(self):
        self.eng.wait_ge(self.sem, self.base + self.n)

    @contextmanager
    def loop(self, start, end, per):
        before = self.base + self.n
        with self.eng.Fori(start, end) as t:
            self.base, self.n = before - per * start + per * t, 0
            yield t
            assert self.n == per, f"the loop's body counts {self.n}, not {per}"
        self.base, self.n = before + per * (end - start), 0


def hybrid_trunk(nc, x_prompt, x_sample, cache_k, cache_v, cache_logf, state_ssd, state_conv,
                 norm_pre, norm_post, w_in_even, w_out_even, gmlp_ws, gmlp_bs, gmlp_gv,
                 conv_w, conv_b, dt_bias, a_log, ssd_d, ssd_norm_g,
                 w_in_odd, b_forget, w_out_odd, gq, gk,
                 y_prompt, y_sample, k_prompt, v_prompt, logf_prompt, ssd_prompt, conv_prompt,
                 k_sample, v_sample, logf_sample, ssd_sample, conv_sample, gv_sample):
    ctx = ExitStack()
    ctx.enter_context(nc.allow_non_contiguous_dma(reason="small parameter vectors"))
    sems = {}

    def S(name):
        if name not in sems:
            sems[name] = ctx.enter_context(nc.semaphore(name))
        return sems[name]

    base = (nc.sbuf_base + 63) // 64 * 64
    end = nc.sbuf_usable_end
    BIG = KT * TOK * 4
    A_H, A_R3 = 0, 2 * BIG
    A_R4 = A_R3 + 8 * 9 * P * 4
    A_R5 = A_R4 + BIG
    A_W = A_R5 + BIG
    A_C = A_W + 6 * 4096

    def at(name, offset, shape, dt=f32):
        size = 2 if dt == bf16 else 4
        for s in shape[1:]:
            size *= s
        assert base + offset + size <= end, (name, base + offset + size - end)
        return nc.alloc_sbuf_tensor_at(name, shape, dt, offset=base + offset)

    class Region:
        def __init__(self, offset, limit):
            self.at, self.limit = offset, limit

        def __call__(self, name, shape, dt=f32):
            t = at(name, self.at, shape, dt)
            size = 2 if dt == bf16 else 4
            for s in shape[1:]:
                size *= s
            self.at += (size + 31) // 32 * 32
            assert self.at <= self.limit, (name, self.at - self.limit)
            return t

    HH = at("HH", A_H, [P, KT, TOK], f32r)
    HL = at("HL", A_H + BIG, [P, KT, TOK], f32r)
    HX = at("HX", A_H + BIG, [P, KT, TOK])
    WRAW = at("WRAW", A_W, [P, 2, KT, P])
    WH = at("WH", A_W + 8192, [P, 2, KT, P], f32r)
    WL = at("WL", A_W + 16384, [P, 2, KT, P], f32r)

    const = Region(A_C, end - base)
    IDENT = const("IDENT", [P, P])
    ONES = const("ONES", [P, P])
    COLS = const("COLS", [P, N_ROWS])
    CONVW_SB = const("CONVW", [P, XBC_TILES, TAPS])
    DCOL = const("DCOL", [P, 8])
    small = const("small", [P, 64])
    SS, MS, RT, RR = small[:, 0:9], small[:, 9:18], small[:, 18:27], small[:, 27:36]
    DTB, AL, EAL, BF = small[:, 36:37], small[:, 37:38], small[:, 38:39], small[:, 39:40]
    MX, MXR, NBIAS = small[:, 40:44], small[:, 44:45], small[:, 45:46]
    RSUM, RINV = small[:, 46:47], small[:, 47:48]
    c_phase = const.at

    XS = at("XS", A_R3, [P, NB + 1, D])
    r = Region(A_R4, A_W)
    SQJ = r("SQJ", [P, D])
    ROWS = r("ROWS", [P, P])
    DEXP = r("DEXP", [8, 2, HP])
    DSM = r("DSM", [8, 2])

    r = Region(A_R3, A_R5)
    CT = r("CT", [P, 2, TOK])
    BTOK = r("BTOK", [P, 2, 9, P])
    CBT = r("CBT", [P, 2, 9, P])
    m_at = r.at
    M = r("M", [P, 2, 9, P])
    BT = at("BT", m_at, [P, 2, TOK])
    acs_at = r.at
    ACSROW = r("ACSROW", [HEADS_B, TOK])
    XR = r("XR", [P, PADW])
    ACC = r("ACC", [P, CONVW])
    rows_at = r.at
    XC = r("XC", [P, TOK])
    XD = r("XD", [P, 9, P])
    XW = r("XW", [P, 9, P])
    YF = XD[:, :, :].rearrange("p b d -> p (b d)")[:, 0:TOK]
    YT = XW
    ST = r("ST", [P, 9, P])
    rows_end = r.at
    r = Region(c_phase, end - base)
    MASKT = r("MASKT", [P, P])
    CST = r("CST", [P, 6, XBC_TILES])
    DECB = r("DECB", [P, HEADS_B, 9])
    DECR = r("DECR", [HEADS_B, HEADS_B, 9])
    TOKQ = r("TOKQ", [P, 4, 9, HEADS_B])
    FS = r("FS", [P, 2, P])
    FSO = r("FSO", [P, 2, P])
    SI = r("SI", [P, P])
    CSO = r("CSO", [6 * XBC_TILES, P])
    ACSB = (at("ACSB0", acs_at, [P, TOK]), r("ACSB1", [P, TOK]))
    r = Region(rows_at, rows_end)
    RW = [r(f"DTROW{i}", [HEADS_B, TOK]) for i in range(4)]
    r = Region(A_R5 + 4 * TOK * 4, A_W)
    RW += [r(f"DTROW{i}", [HEADS_B, TOK]) for i in range(4, 8)]
    YB = at("YB", A_R5, [P, 8, TOK])

    V = at("V", A_R3, [P, 8, 9 * P])
    YA = at("YA", A_R3, [P, 8, 9 * P])
    r = Region(A_R4, A_R5)
    VG = r("VG", [P, TOK])
    GVB = r("GVB", [P, A_GROUPS, 2 * P])
    VS = at("VS", r.at, [P, 9, P])
    SQV = r("SQV", [P, 9, 2 * P])
    WS = r("WS", [P, A_GROUPS, P])
    WT = r("WT", [P, A_GROUPS, P])
    BSB = r("BSB", [P, A_GROUPS, P])
    UG = r("UG", [P, TOK])
    ZG = r("ZG", [P, TOK])
    r = Region(c_phase, end - base)
    TMP = r("TMP", [P, TOK])
    RSY = r("RSY", [P, 2, TOK])
    GSM = r("GSM", [P, 4, 16])

    YAH = at("YAH", A_R4, [P, 8, TOK], f32r)
    YAL = at("YAL", A_R5, [P, 8, TOK], f32r)
    O0 = at("O0", A_R3, [P, 8, TOK])
    XS2 = at("XS2", A_H, [P, NB + 1, D])
    RSO = RSY[:, 0, :]
    SQA = RSY[:, 1, :]
    X1SQ = (TMP, SQA)
    O1 = at("O1", A_R5, [P, 8, TOK])
    YO = at("YO", A_R4, [P, 3, 9, P])

    Y1 = at("Y1", A_R5, [P, 8, TOK])
    r = Region(A_R3 + BIG, A_R5)
    QT = r("QT", [P, TOK])
    KALL = r("KALL", [P, KEYS])
    VTOK = r("VTOK", [P, 11, P])
    NFB = r("NFB", [P, KEYS])
    SB = r("SB", [P, SEQ])
    PT = r("PT", [P, NB, P])
    KTOK = r("KTOK", [P, NB, P])
    VRAW = r("VRAW", [P, TOK])
    r = Region(A_R4, A_R5)
    FW = [r(f"FROW{i}", [HEADS_C, TOK]) for i in range(6)]
    r = Region(A_R5 + 4 * TOK * 4, A_W)
    LROW = r("LROW", [HEADS_C, KEYS])
    ONEROW = r("ONEROW", [HEADS_C, KEYS])
    LT = r("LT", [P, 9, HEADS_C])
    CLT = r("CLT", [P, 2, HEADS_C])
    r = Region(c_phase, end - base)
    NRM = r("NRM", [P, 5, CH])
    NRML = at("NRML", c_phase, [P, 5, CH], f32r)
    nf_at = r.at
    NFROW = r("NFROW", [HEADS_C, KEYS])
    NRMH = at("NRMH", nf_at, [P, 3, CH], f32r)
    ONESR = r("ONESR", [P, P], f32r)
    MASKD = r("MASKD", [P, P], bf16)
    IDENTB = r("IDENTB", [P, P], bf16)
    KC = r("KC", [P, 2, P])
    KSAM = KC[0:DEC, 0, :]

    acs_rows = nc.dram_tensor("acs_rows", [HEADS_B, TOK], f32, kind="Internal").ap()
    nf_rows = nc.dram_tensor("nf_rows", [HEADS_C, KEYS], f32, kind="Internal").ap()

    PB = [ctx.enter_context(nc.psum_tensor(f"PB{i}", [P, 512], f32)) for i in range(8)]

    w_even = w_in_even[0].rearrange("(k p) e -> p k e", p=P)
    w_oe = w_out_even[0].rearrange("(s k p) e -> s p k e", s=2, p=P)
    w_odd = w_in_odd[0].rearrange("(k p) e -> p k e", p=P)
    w_oo = w_out_odd[0].rearrange("(k p) e -> p k e", p=P)
    xp = x_prompt[0].rearrange("(b p) d -> p b d", p=P)
    yp = y_prompt[0].rearrange("(b p) d -> p b d", p=P)

    STEPS = 12
    V_, Z_, Q_, K_ = range(4)
    NORM_SLOT = (0, 1, 2, 3, 4, 0)

    def norm_chunk(n):
        c = n % 3
        if n < 3:
            return [(slice(0, CH), QT[:, c * CH:(c + 1) * CH])]
        if c < 2:
            return [(slice(0, CH), KALL[:, c * CH:(c + 1) * CH])]
        return [(slice(0, SEQ - 2 * CH), KALL[:, 2 * CH:SEQ]), (slice(SEQ - 2 * CH, CH), KALL[:, SEQ + PAST:KEYS])]

    def wait(eng, name, value):
        if not isinstance(value, int) or value > 0:
            eng.wait_ge(S(name), value)

    PAIR_STEPS = 6
    DECAYS = ((0, 0), (0, 1), (1, 0), (1, 1), (0, 2), (1, 2))
    DECAYS_OF_STEP = ((0, 1), (2, 3), (4, 5))

    block = ctx.enter_context(nc.Block())


    @block.sync
    def _(sp):
        def load_w(w, src, cols=P):
            if not isinstance(w[2], int) or w[0] + w[1] * w[2] >= 2:
                sp.wait_ge(S("w_low"), times(w, 1, -1))
            sp.dma_start(WRAW[:, slot(w), :, 0:cols], src).then_inc(S(f"w_raw{slot(w)}"), 16)

        def even(col, n=P):
            return w_even[:, :, bass.ds(col, n)]

        for b in range(NB):
            sp.dma_start(XS[:, b, :], xp[:, b, :]).then_inc(S(f"x_in{b}"), 16)
            if b == 2:
                for src, (row, n) in (
                        (norm_pre[0].rearrange("(k p) -> k p", p=P), (PRE0, 8)),
                        (norm_post[0].rearrange("(k p) -> k p", p=P), (POST0, 8)),
                        (norm_pre[1].rearrange("(k p) -> k p", p=P), (PRE1, 8)),
                        (norm_post[1].rearrange("(k p) -> k p", p=P), (POST1, 8)),
                        (ssd_norm_g[0].rearrange("(k p) -> k p", p=P), (GSSD, 8)),
                        (conv_b[0].rearrange("(k p) -> k p", p=P), (CONVB, XBC_TILES)),
                        (gq[0:1, :], (GQ, 1)), (gk[0:1, :], (GK, 1)),
                        (state_conv[0, 0].rearrange("r (k p) -> (r k) p", p=P), (CTX, 36))):
                    sp.dma_start(ROWS[row:row + n, :], src).then_inc(S("rows_in"), 16)
                sp.dma_start(DSM[:, :], ssd_d[0].rearrange("(t j) -> t j", j=2)).then_inc(S("rows_in"), 16)
            if b == 3:
                load_w(tile_no(W_DT, 1, 0), even(DT0, HEADS_B), HEADS_B)
        sp.dma_start(XS[0:DEC, NB, :], x_sample[0]).then_inc(S(f"x_in{NB}"), 16)
        sp.dma_start(CONVW_SB[:, :, :], conv_w[0].rearrange("(t p) k -> p t k", p=P)).then_inc(S("par_in"), 16)
        sp.dma_start(DTB[0:HEADS_B, :], dt_bias[0].unsqueeze(1)).then_inc(S("par_in"), 16)
        sp.dma_start(AL[0:HEADS_B, :], a_log[0].unsqueeze(1)).then_inc(S("par_in"), 16)
        sp.dma_start(BF[0:HEADS_C, :], b_forget[0].unsqueeze(1)).then_inc(S("par_in"), 16)
        for j in range(4):
            load_w(tile_no(W_BC, 1, j), even(XBC0 + (8 + j) * P))

        def states_out(t):
            sp.wait_ge(S("fs_out"), t + 1)
            for j, dst in enumerate((ssd_prompt, ssd_sample)):
                sp.dma_start(dst[0, 0].rearrange("(t h) p n -> t (h p) n", h=2)[t], FSO[:, j, :]) \
                    .then_inc(S("ssd_stored"), 16)

        def state_in(t):
            if not isinstance(t, int) or t > 0:
                sp.wait_ge(S("si_used"), t)
            sp.dma_start(SI[:, :], state_ssd[0, 0].rearrange("(t h) p n -> t (h p) n", h=2)[t]) \
                .then_inc(S("si_in"), 16)

        def decays_in(t):
            if not isinstance(t, int) or t > 0:
                sp.wait_ge(S("seg"), 6 * t)
            for j in range(2):
                row = acs_rows.rearrange("(t h) c -> t h c", h=2)[t, j:j + 1]
                sp.dma_start(ACSB[j][:, :], row.broadcast_to([P, TOK])).then_inc(S("acs_in"), 16)

        def pair_moves(t, states=True):
            load_w(tile_no(W_XZ, 2, t), even(XBC0 + P * t))
            load_w(tile_no(W_XZ + 1, 2, t), even(3 * D + P * t))
            state_in(t - 1)
            decays_in(t - 1)
            if states:
                states_out(t - 2)

        load_w(tile_no(W_XZ, 2, 0), even(XBC0))
        load_w(tile_no(W_XZ + 1, 2, 0), even(3 * D))
        sp.wait_ge(S("dtc"), 3)
        sp.dma_start(acs_rows, ACSROW[:, :]).then_inc(S("acs_stored"), 16)
        sp.wait_ge(S("acs_stored"), 16)
        sp.wait_ge(S("dt_turn"), 1)
        pair_moves(1, states=False)
        with sp.Fori(2, 8) as t:
            pair_moves(t)
        load_w(tile_no(W_V, 1, 0), even(D))
        load_w(tile_no(W_V, 1, 1), even(D + P))
        state_in(7)
        decays_in(7)
        states_out(6)
        states_out(7)
        sp.wait_ge(S("cso"), 1)
        for j, dst in enumerate((conv_prompt, conv_sample)):
            for q in range(3):
                row = (3 * j + q) * XBC_TILES
                sp.dma_start(dst[0, 0, q].rearrange("(t p) -> t p", p=P), CSO[row:row + XBC_TILES, :]) \
                    .then_inc(S("conv_stored"), 16)
        sp.wait_ge(S("yb"), 8)
        sp.wait_ge(S("y_turn"), 24)
        sp.dma_start(GVB[:, :, :].rearrange("p g k -> p (g k)"),
                     gmlp_gv[0:1].rearrange("a g k -> a (g k)").broadcast_to([P, D])).then_inc(S("gv_in"), 16)
        sp.dma_start(BSB[:, :, :].rearrange("p g k -> p (g k)"),
                     gmlp_bs[0:1].rearrange("a g k -> a (g k)").broadcast_to([P, A_GROUPS * P])) \
            .then_inc(S("gv_in"), 16)
        sp.dma_start(WS[:, :, :], gmlp_ws[0].rearrange("g i j -> i g j")).then_inc(S("gv_in"), 16)
        with sp.Fori(1, 4) as i:
            for j in range(2):
                load_w(tile_no(W_V + j, 2, i), even(D + P * j + 2 * P * i))
        load_w(tile_no(W_UZ, 1, 0), even(0))
        load_w(tile_no(W_UZ, 1, 1), even(2 * D))
        sp.wait_ge(S("v_normed"), 4)
        sp.dma_start(gv_sample[0, 0].rearrange("t (k f) -> t k f", f=P), V[0:DEC, :, NB * P:]) \
            .then_inc(S("gv_stored"), 16)
        with sp.Fori(1, 8) as t:
            load_w(tile_no(W_UZ, 2, t), even(P * t))
            load_w(tile_no(W_UZ + 1, 2, t), even(2 * D + P * t))
        with sp.Fori(0, 8) as n:
            load_w(tile_no(W_OE, 2, n), w_oe[1][:, :, bass.ds(P * n, P)])
            load_w(tile_no(W_OE + 1, 2, n), w_oe[0][:, :, bass.ds(P * (n + 1) - P, P)])

        def qkvz(h, j):
            col = D * (2, 3, 0, 1)[j]
            load_w(tile_no(W_QKVZ + j, 4, h), w_odd[:, :, bass.ds(col + P * h, P)])

        load_w(tile_no(W_F, 1, 0), w_odd[:, :, 4 * D:4 * D + HEADS_C], HEADS_C)
        qkvz(0, 0)
        sp.wait_ge(S("p_chunk"), 3 * (W_F - 1))
        for b in range(NB):
            sp.dma_start(XS2[:, b, :], xp[:, b, :]).then_inc(S(f"x_in{b}"), 16)
        sp.dma_start(XS2[0:DEC, NB, :], x_sample[0]).then_inc(S(f"x_in{NB}"), 16)
        sp.wait_ge(S("p_chunk"), 3 * W_F)
        sp.dma_start(CLT[:, :, :], cache_logf[0, 0].rearrange("(b p) h -> p b h", p=P)).then_inc(S("clf_in"), 16)
        qkvz(0, 1)

        def out_odd_w(i, j):
            load_w(tile_no(W_OO + j, 2, i), w_oo[:, :, bass.ds(P * j + 2 * P * i, P)])

        def head_cols(h):
            return bass.ds(P * (h + 3) - 3 * P, P)

        def turn_moves(t, attend=True, project=True, last=False):
            p = t + 1
            if project:
                qkvz(p, Q_)
                qkvz(p, K_)
            if attend:
                sp.wait_ge(S("vt_read"), 3 * t + 3)
                sp.dma_start(v_prompt[0, 0].rearrange("(b p) h d -> p b (h d)", p=P)[:, :, head_cols(t)],
                             VTOK[:, 0:NB, :]).then_inc(S("v_stored"), 16)
                sp.dma_start(v_sample[0, 0].rearrange("t h d -> t (h d)")[:, head_cols(t)],
                             VTOK[0:DEC, NB + 2, :]).then_inc(S("v_stored"), 16)
                sp.wait_ge(S("k_tok"), 3 * t + 3)
                sp.dma_start(k_prompt[0, 0].rearrange("(b p) h d -> p b (h d)", p=P)[:, :, head_cols(t)],
                             KTOK[:, :, :]).then_inc(S("k_stored"), 16)
                sp.dma_start(k_sample[0, 0].rearrange("t h d -> t (h d)")[:, head_cols(t)], KSAM) \
                    .then_inc(S("k_stored"), 16)
            if not project:
                return
            out_odd_w(0, 0) if last else qkvz(p + 1, V_)
            if attend:
                sp.wait_ge(S("k_stored"), 32 * t + 32)
            else:
                sp.wait_ge(S("lt"), 1)
                sp.dma_start(logf_prompt[0, 0].rearrange("(b p) h -> p b h", p=P), LT[:, 0:NB, :]) \
                    .then_inc(S("lf_stored"), 16)
                sp.dma_start(logf_sample[0, 0], LT[0:DEC, NB, :]).then_inc(S("lf_stored"), 16)
            sp.dma_start(KC[:, :, :], cache_k[0, 0].rearrange("(b p) h d -> p b (h d)", p=P)[:, :, head_cols(p)]) \
                .then_inc(S("kc_in"), 16)
            out_odd_w(0, 1) if last else qkvz(p + 1, Z_)
            if attend:
                sp.wait_ge(S("sm"), 9 * t + 9)
            else:
                sp.wait_ge(S("nfrow"), 1)
                sp.dma_start(nf_rows[:, :], NFROW[:, :]).then_inc(S("nf_stored"), 16)
                sp.wait_ge(S("nf_stored"), 16)
            sp.dma_start(NFB[:, :], nf_rows[bass.ds(p, 1), :].broadcast_to([P, KEYS])).then_inc(S("nf"), 16)
            if attend:
                sp.wait_ge(S("pv"), 9 * t + 9)
            sp.dma_start(VTOK[:, NB:NB + 2, :],
                         cache_v[0, 0].rearrange("(b p) h d -> p b (h d)", p=P)[:, :, head_cols(p)]) \
                .then_inc(S("vc_in"), 16)

        turn_moves(-1, attend=False)
        with sp.Fori(0, 6) as t:
            turn_moves(t)
        turn_moves(6, last=True)
        turn_moves(7, project=False)
        with sp.Fori(1, 4) as i:
            for j in range(2):
                out_odd_w(i, j)
        for k in range(8):
            if k < 7:
                sp.wait_ge(S("y_tok"), 3 * k + 3)
            else:
                sp.wait_ge(S("y_last"), 3)
            sp.dma_start(yp[:, :, k * P:(k + 1) * P], YO[:, k % 3, 0:NB, :]).then_inc(S(f"y_stored{k % 3}"), 16)
            sp.dma_start(y_sample[0][:, k * P:(k + 1) * P], YO[0:DEC, k % 3, NB, :]) \
                .then_inc(S(f"y_stored{k % 3}"), 16)
        for name, n in (("ssd_stored", 16), ("conv_stored", 6), ("gv_stored", 1), ("lf_stored", 2),
                        ("k_stored", 16), ("v_stored", 16), ("y_stored0", 6), ("y_stored1", 6), ("y_stored2", 4)):
            sp.wait_ge(S(name), 16 * n)

    @block.gpsimd
    def _(pool):
        order = Order(pool, S("pool_order"))

        def split_low(w):
            pool.wait_ge(S("w_high"), times(w, 1, 1))
            if not isinstance(w[2], int) or w[0] + w[1] * w[2] >= 2:
                pool.wait_ge(S("p_chunk"), times(w, 3, -3))
            pool.tensor_tensor(WL[:, slot(w), :, :], WRAW[:, slot(w), :, :], WH[:, slot(w), :, :].bitcast(f32),
                               ALU.subtract).then_inc(S("w_low"), 1)

        def split_lows(ws):
            for w in ws:
                split_low(w)

        pool.memset(WRAW[:, 0, :, HEADS_B:], 0.0).then_inc(S("w_clear"), 1)
        order(pool.memset(IDENT[:, :], 0.0))
        order.fence()
        order(pool.affine_select(out=IDENT[:, :], in_=IDENT[:, :], compare_op=ALU.not_equal, fill=1.0, base=0,
                                 pattern=[[-1, P]], channel_multiplier=1))
        order(pool.memset(MASKT[:, :], 0.0))
        order.fence()
        pool.affine_select(out=MASKT[:, :], in_=MASKT[:, :], compare_op=ALU.is_ge, fill=NEG, base=0,
                           pattern=[[1, P]], channel_multiplier=-1).then_inc(S("masks"), 1)
        for w in range(W_XZ + 4):
            split_low(tile_no(w, 1, 0))

        def pair_parts(t, g, project=True):
            u = t - 1
            for n, (j, q) in enumerate(DECAYS):
                b0, nb, rows = QUADS[q]
                pool.wait_ge(S("mexp"), 6 * u + n + 1)
                m = M[0:rows, j, b0:b0 + nb, 0:rows]
                pool.tensor_tensor(m, m, CBT[0:rows, g, b0:b0 + nb, 0:rows], ALU.mult).then_inc(S("m"), 1)
            if project:
                split_low(tile_no(W_XZ + 2, 2, t))
            pool.wait_ge(S("yf"), 3 * u + 3)
            pool.wait_ge(S("c_read2"), times(tile_no(W_XZ + 1, 2, u), 1, 1))
            pool.tensor_tensor(YB[:, u, :], YB[:, u, :], YF, ALU.mult).then_inc(S("yb"), 1)
            if project:
                split_low(tile_no(W_XZ + 3, 2, t))

        with pool.Fori(1, 5) as t:
            pair_parts(t, 0)
        with pool.Fori(5, 8) as t:
            pair_parts(t, 1)
        pair_parts(8, 1, project=False)
        with pool.Fori(1, 4) as i:
            split_lows([tile_no(W_V + j, 2, i) for j in range(2)])
        with pool.Fori(0, 8) as t:
            split_lows([tile_no(W_UZ + j, 2, t) for j in range(2)])

        def low_halves(src, hi, lo):
            for n in range(1, 3 * KT, 2):
                k, cols = n % KT, slice(n // KT * CH, (n // KT + 1) * CH)
                pool.wait_ge(S(hi), n + 1)
                pool.tensor_tensor(HL[:, k, cols], src[:, k, cols], HH[:, k, cols].bitcast(f32), ALU.subtract) \
                    .then_inc(S(lo), 1)

        split_low(tile_no(W_OE, 1, 0))
        split_low(tile_no(W_OE + 1, 1, 0))
        low_halves(YB, "yb_hi", "yb_lo_odd")
        with pool.Fori(1, 8) as n:
            split_lows([tile_no(W_OE + j, 2, n) for j in range(2)])
        split_low(tile_no(W_F, 1, 0))
        low_halves(HX, "h1_hi", "h1_lo_odd")
        pool.wait_ge(S("h1_lo"), 12)
        order(pool.tensor_copy(IDENTB[:, :], IDENT[:, :]))
        order(pool.memset(MASKD[:, :], 0.0))
        order.fence()
        pool.affine_select(out=MASKD[:, :], in_=MASKD[:, :], compare_op=ALU.is_ge, fill=NEGBIG, base=0,
                           pattern=[[-1, P]], channel_multiplier=1).then_inc(S("masks"), 1)
        split_low(tile_no(W_QKVZ + V_, 4, 0))
        split_low(tile_no(W_QKVZ + Z_, 4, 0))

        def turn_parts(p):
            def squares(n):
                pool.wait_ge(S(f"c_read{n % 3}"), times(tile_no(W_QKVZ - 8 + (Q_ if n < 3 else K_), 4, p), 1, 1))
                if n == 0:
                    wait(pool, "n_done", 2 * p)
                if n == 5:
                    pool.wait_ge(S("n_done"), 2 * p + 1)
                for cols, src in norm_chunk(n):
                    last = pool.tensor_tensor(NRM[:, NORM_SLOT[n], cols], src, src, ALU.mult)
                last.then_inc(S("n_sq"), 1)

            split_low(tile_no(W_QKVZ + Q_, 4, p))
            split_low(tile_no(W_QKVZ + K_, 4, p))
            for n in range(3):
                squares(n)
            split_low(tile_no(W_QKVZ + 4 + V_, 4, p))
            for n in range(3, 6):
                squares(n)
            split_low(tile_no(W_QKVZ + 4 + Z_, 4, p))

        turn_parts(0)
        with pool.Fori(1, 8) as p:
            turn_parts(p)
        for k in range(7):
            pool.wait_ge(S("y1_hi"), k + 1)
            pool.tensor_tensor(HL[:, k, :], Y1[:, k, :], HH[:, k, :].bitcast(f32), ALU.subtract) \
                .then_inc(S("y1_lo"), 1)
        with pool.Fori(1, 4) as i:
            split_lows([tile_no(W_OO + j, 2, i) for j in range(2)])
        for k in range(0, 8, 2):
            pool.wait_ge(S("o1_n"), k // 2 + 1)
            pool.tensor_tensor(O1[:, k, :], O1[:, k, :], O0[:, k, :], ALU.add).then_inc(S("x2_even"), 1)

    def sample_rows(b):
        return DEC if b == NB else P

    def span(b, n=1):
        return slice(b * P, b * P + (DEC if b == NB else n * P))

    def groups_before(b):
        return b if b < 4 else (4 + 2 * (b - 4) if b < NB else 12)

    @block.tensor
    def _(pe):
        def mm(out, lhsT, rhs, start=True, stop=True):
            return pe.matmul(out, lhsT, rhs, start=start, stop=stop)

        def turn(out, in_):
            n = in_.shape[0]
            return pe.transpose(out, in_, IDENT[0:n, 0:n])

        def key_wait(rows):
            if rows <= DEC:
                pe.wait_ge(S("masks"), 1)

        def project_chunk(w, u, c, hi, lo, start=True, stop=True, ready=None, ks=range(KT)):
            if c == 0:
                pe.wait_ge(S("w_low"), times(w, 1, 1))
            if start and not (isinstance(u[2], int) and u[0] + u[1] * u[2] == 0):
                pe.wait_ge(S(f"c_read{c}"), times(u, 1, 0))
            cols = slice(c * CH, (c + 1) * CH)
            for k in ks:
                if ready and len(ready) == 2:
                    pe.wait_ge(S(ready[k % 2]), c * 4 + k // 2 + 1)
                elif ready and (c == 0 or len(ks) < KT):
                    pe.wait_ge(S(ready[0]), k + 1)
                wh, wl = WH[:, slot(w), k, :], WL[:, slot(w), k, :]
                mm(PB[c][:, 0:CH], wh, hi[:, k, cols], start=start and k == 0, stop=False)
                mm(PB[c][:, 0:CH], wh, lo[:, k, cols], start=False, stop=False)
                last = mm(PB[c][:, 0:CH], wl, hi[:, k, cols], start=False, stop=stop and k == KT - 1)
            if ks[-1] == KT - 1:
                last.then_inc(S("p_chunk"), 1)

        def project(w, u, hi, lo, start=True, stop=True, ready=None):
            for c in range(3):
                project_chunk(w, u, c, hi, lo, start, stop, ready)

        pe.wait_ge(S("masks"), 1)
        pe.wait_ge(S("rows_in"), 160)
        turn(PB[3][:, 0:N_ROWS], ROWS[0:N_ROWS, :])
        pe.wait_ge(S("dexp"), 1)
        turn(PB[3][:, P:P + 8], DEXP[:, :, :].rearrange("t j p -> t (j p)")).then_inc(S("rows_turn"), 1)
        pe.wait_ge(S("cols"), 1)
        first = tile_no(0, 1, 0)
        for q, (b0, nb, rows) in enumerate(QUADS):
            pe.wait_ge(S("xn"), b0 + nb)
            for k in range(KT):
                i = q * KT + k
                if i >= 4:
                    pe.wait_ge(S("h_lo"), i - 3)
                for j in range(nb):
                    last = turn(PB[3 + i % 4][:, j * P:j * P + rows], XS[0:rows, b0 + j, k * P:(k + 1) * P])
                last.then_inc(S("x_t"), 1)
                if q == 1:
                    project_chunk(first, first, 0, HH, HL, ks=[k])
        pe.wait_ge(S("h_lo"), 24)
        for c in (1, 2):
            project_chunk(first, first, c, HH, HL)
        for w in range(1, W_XZ):
            project(tile_no(w, 1, 0), tile_no(w, 1, 0), HH, HL)

        pe.wait_ge(S("dt_rows"), 1)
        for i, row in enumerate((RW[0], RW[2], RW[3], ACSROW)):
            for b in range(NB + 1):
                out = PB[3] if i < 3 else PB[4]
                o = (i * 9 if i < 3 else 0) + b
                turn(out[0:sample_rows(b), o * HEADS_B:(o + 1) * HEADS_B], row[:, span(b)])
        mm(PB[4][:, 256:256 + 9 * HEADS_B], ONES[0:HEADS_B, :], DECR[:, :, :].rearrange("k h b -> k (h b)")) \
            .then_inc(S("dt_turn"), 1)

        project(tile_no(W_XZ, 1, 0), tile_no(W_XZ, 1, 0), HH, HL)

        pe.wait_ge(S("conv_act"), 4)
        n = 0
        for g in range(GROUPS_B):
            for b0, nb, rows in QUADS:
                for what in range(2):
                    if n >= 3:
                        pe.wait_ge(S("cb_read"), n - 2)
                    bank = PB[5 + n % 3]
                    for j in range(nb):
                        cols = slice((b0 + j) * P, (b0 + j) * P + rows)
                        if what == 0:
                            last = mm(bank[0:rows, j * P:j * P + rows], BT[:, g, cols], CT[:, g, cols])
                        else:
                            last = turn(bank[0:rows, j * P:(j + 1) * P], BT[:, g, cols])
                    last.then_inc(S("cb_mm"), 1)
                    n += 1

        def pair_steps(t, g, project=True):
            u = t - 1
            for i in range(PAIR_STEPS):
                if project:
                    w = tile_no(W_XZ + i // 3, 2, t)
                    project_chunk(w, w, i % 3, HH, HL)
                elif i in (1, 3, 5):
                    project_chunk(tile_no(W_V, 1, 0), tile_no(W_V, 1, 0), i // 2, HH, HL)
                if i == 0:
                    pe.wait_ge(S("conv_act"), 5 + u)
                    wait(pe, "yf", 3 * u)
                    for q, (b0, nb, rows) in enumerate(QUADS):
                        for j in range(nb):
                            last = turn(PB[3 + q][0:rows, j * P:(j + 1) * P], XC[:, (b0 + j) * P:(b0 + j) * P + rows])
                        last.then_inc(S("xc_turn"), 1)
                if i == 1:
                    for q, (b0, nb, rows) in enumerate(QUADS):
                        pe.wait_ge(S("xw"), 3 * u + q + 1)
                        if q == 2:
                            pe.wait_ge(S("si_in"), 16 * u + 16)
                            turn(PB[5][:, P:2 * P], SI[:, :]).then_inc(S("si_used"), 1)
                        for j in range(nb):
                            last = mm(PB[3 + q][:, j * P:(j + 1) * P], BTOK[0:rows, g, b0 + j, :], XW[0:rows, b0 + j, :])
                        last.then_inc(S("ds"), 1)
                if i == 3:
                    pe.wait_ge(S("st"), u + 1)
                    turn(PB[5][:, 2 * P:3 * P], FS[:, 0, :])
                    turn(PB[5][:, 3 * P:4 * P], FS[:, 1, :]).then_inc(S("fs_turn"), 1)
                for q in {3: (0,), 4: (1, 2)}.get(i, ()):
                    b0, nb, rows = QUADS[q]
                    pe.wait_ge(S("m"), 6 * u + (3, 4, 6)[q])
                    if q == 2:
                        pe.wait_ge(S("fs_out"), u + 1)
                    intra, state = PB[(3, 6, 5)[q]], PB[(4, 7, 5)[q]]
                    off = P if q == 2 else 0
                    for j in range(nb):
                        b = b0 + j
                        mm(state[0:rows, off + j * P:off + (j + 1) * P], CT[:, g, b * P:b * P + rows], ST[:, b, :])
                        for k in range(2):
                            last = mm(intra[0:rows, j * P + k * HP:j * P + (k + 1) * HP], M[0:rows, k, b, 0:rows],
                                      XD[0:rows, b, k * HP:(k + 1) * HP])
                    last.then_inc(S("y_mm"), 1)
                if i == 5:
                    for q, (b0, nb, rows) in enumerate(QUADS):
                        if q < 2:
                            pe.wait_ge(S("yt"), 3 * u + (1, 3)[q])
                        for j in range(nb):
                            last = turn(PB[3 + q][:, j * P:j * P + rows], YT[0:rows, b0 + j, :])
                        last.then_inc(S("y_turn"), 1)

        project(tile_no(W_XZ + 1, 1, 0), tile_no(W_XZ + 1, 1, 0), HH, HL)
        pe.wait_ge(S("tokq"), 1)
        pe.wait_ge(S("cb_read"), 12)
        with pe.Fori(1, 5) as t:
            pair_steps(t, 0)
        with pe.Fori(5, 8) as t:
            pair_steps(t, 1)
        pair_steps(8, 1, project=False)

        pe.wait_ge(S("yf"), 24)
        turn(PB[3][0:6 * XBC_TILES, 0:P], CST[:, :, :].rearrange("p r t -> p (r t)")).then_inc(S("cst_turn"), 1)

        def v_group(i):
            vt = [tile_no(W_V + j, 2, i) for j in range(2)]
            if not isinstance(i, int):
                project(vt[0], vt[0], HH, HL)
            project(vt[1], vt[1], HH, HL)
            wait(pe, "v_tok", 6 * i)
            pe.wait_ge(S("cso"), 1)
            for j, src in enumerate((VG, UG)):
                pe.wait_ge(S("c_read2"), times(vt[j], 1, 1))
                for q, (b0, nb, rows) in enumerate(QUADS):
                    if j == 1 and q == 2:
                        pe.wait_ge(S("v_tok"), 6 * i + 1)
                    key_wait(rows)
                    for n in range(nb):
                        last = turn(PB[(3, 4, 5, 6, 7, 3)[3 * j + q]][0:rows, n * P:(n + 1) * P],
                                    src[:, (b0 + n) * P:(b0 + n) * P + rows])
                    last.then_inc(S("v_turn"), 1)

        v_group(0)
        with pe.Fori(1, 4) as i:
            v_group(i)
        project(tile_no(W_UZ, 1, 0), tile_no(W_UZ, 1, 0), HH, HL)
        pe.wait_ge(S("gv_in"), 48)
        pe.wait_ge(S("v_tok"), 24)
        for g in range(A_GROUPS):
            last = turn(PB[6][:, g * P:(g + 1) * P], WS[:, g, :])
        last.then_inc(S("ws_turn"), 1)
        project(tile_no(W_UZ + 1, 1, 0), tile_no(W_UZ + 1, 1, 0), HH, HL)

        def spatial(i, j):
            pe.wait_ge(S("vs"), 2 * i + j + 1)
            for q, (b0, nb, rows) in enumerate(QUADS):
                if j > 0:
                    pe.wait_ge(S("s_read"), 6 * i + 3 * j - 3 + q + 1)
                else:
                    pe.wait_ge(S("s_read"), 6 * i)
                for n in range(nb):
                    last = mm(PB[3 + q][:, n * P:n * P + rows], VS[:, b0 + n, :], WT[:, i, 0:rows])
                last.then_inc(S("s_mm"), 1)

        def project_uz(i, j):
            for n in range(2):
                uz = tile_no(W_UZ + 2 * j + n, 4, i)
                project(uz, uz, HH, HL)

        pe.wait_ge(S("wt"), 1)
        spatial(0, 0)
        project_uz(0, 1)
        pe.wait_ge(S("s_read"), 3)
        for n in range(6):
            g, c = n // 3, n % 3
            pe.wait_ge(S("y_sq"), 4 + 4 * g)
            if n == 5:
                pe.wait_ge(S("gs_ms"), 1)
            mm(PB[(3, 4, 5, 6, 7, 3)[n]][:, 0:CH], ONES[:, :], RSY[:, g, c * CH:(c + 1) * CH]).then_inc(S("gs_mm"), 1)
        pe.wait_ge(S("gs_ms"), 6)
        spatial(0, 1)
        with pe.Fori(1, 4) as i:
            for j in range(2):
                project_uz(i, j)
                spatial(i, j)

        def out_sums(name, at_count):
            for c in range(3):
                pe.wait_ge(S(name), at_count - 2 + c)
                mm(PB[3 + c][:, 0:CH], ONES[:, :], SQA[:, c * CH:(c + 1) * CH]).then_inc(S("ss_mm"), 1)

        def out_even(n, first):
            u = tile_no(W_OE, 1, n)
            project(tile_no(W_OE, 2, n), u, HH, HL, stop=False, ready=("yb_lo", "yb_lo_odd") if first else None)
            project(tile_no(W_OE + 1, 2, n), u, YAH, YAL, start=False, ready=("ya_lo",) if first else None)

        out_even(0, True)
        with pe.Fori(1, 8) as n:
            out_even(n, False)
        pe.wait_ge(S("s_read"), 24)
        out_sums("o_sq", 24)
        for c in range(3):
            pe.wait_ge(S(f"c_read{c}"), W_OE + 8)
        for k in range(9):
            if k < 8:
                if k < 2:
                    pe.wait_ge(S("ss_ms"), 3)
                for q, (b0, nb, rows) in enumerate(QUADS):
                    if q == 0 and k >= 2:
                        pe.wait_ge(S("x1"), k - 1)
                    if q == 2 and k >= 1:
                        pe.wait_ge(S("x1"), k)
                    bank = ((3, 4, 5), (6, 7, 5))[k % 2][q]
                    for j in range(nb):
                        if k == 0:
                            pe.wait_ge(S(f"x_in{b0 + j}"), 32)
                        last = turn(PB[bank][:, j * P:j * P + rows], XS2[0:rows, b0 + j, k * P:(k + 1) * P])
                last.then_inc(S("x_turn"), 1)
            if k > 0:
                pe.wait_ge(S("x1_s"), k)
                for c in range(3):
                    last = mm(PB[c][:, 0:CH], ONES[:, :], X1SQ[k % 2][:, c * CH:(c + 1) * CH],
                              start=k == 1, stop=k == 8)
                last.then_inc(S("x1_sums"), 1)

        project(tile_no(W_F, 1, 0), tile_no(W_F - 8, 1, 0), HH, HL, ready=("h1_lo", "h1_lo_odd"))
        pe.wait_ge(S("clf_in"), 16)
        pe.wait_ge(S("ss_ms"), 6)
        for b in range(2):
            last = turn(PB[3][0:HEADS_C, b * P:(b + 1) * P], CLT[:, b, :])
        last.then_inc(S("clf_turn"), 1)

        def turn_lrow():
            pe.wait_ge(S("lrow"), 1)
            for b in range(NB + 1):
                cols = slice(SEQ + PAST, KEYS) if b == NB else span(b)
                last = turn(PB[4][0:sample_rows(b), b * HEADS_C:(b + 1) * HEADS_C], LROW[:, cols])
            last.then_inc(S("lt_turn"), 1)

        pe.wait_ge(S("masks"), 2)

        def norm_sum(h, n, bank):
            pe.wait_ge(S("n_lo"), 6 * h + n + 1)
            mm(PB[bank][:, 0:CH], ONESR[:, :], NRMH[:, n % 3, :], stop=False)
            mm(PB[bank][:, 0:CH], ONESR[:, :], NRML[:, NORM_SLOT[n], :], start=False).then_inc(S("n_ss"), 1)

        def turn_quad(src, q, bank, sem):
            b0, nb, rows = QUADS[q]
            c0 = SEQ + PAST if q == 2 and src is KALL else b0 * P
            for j in range(nb):
                last = turn(PB[bank][0:rows, j * P:(j + 1) * P], src[:, c0 + j * P:c0 + j * P + rows])
            last.then_inc(S(sem), 1)

        def scores(h, b):
            rows = sample_rows(b)
            if b == 0:
                wait(pe, "sm", 9 * h)
                pe.wait_ge(S("n_done"), 2 * h + 1)
            else:
                pe.wait_ge(S("sm"), 9 * h + b)
            if b == 2:
                pe.wait_ge(S("n_done"), 2 * h + 2)
            if b == 4:
                pe.wait_ge(S("k_tok"), 3 * h + 2)
            if b == NB:
                pe.wait_ge(S("kc_done"), h + 1)
            q = QT[:, b * P:b * P + rows]
            key0, keys = (SEQ, PAST + DEC) if b == NB else (0, (b + 1) * P)
            for i, c0 in enumerate(range(0, keys, 512)):
                c1 = min(c0 + 512, keys)
                mm(PB[3 + i][0:rows, 0:c1 - c0], q, KALL[:, key0 + c0:key0 + c1], stop=c1 < keys)
            mm(PB[3 + i][0:rows, keys - rows - c0:keys - c0], IDENTB[0:rows, 0:rows],
               MASKD[0:rows, 0:rows], start=False).then_inc(S("sc_mm"), 1)

        def key_blocks(b):
            return [(j, j, P) for j in range(b + 1)] if b < NB else [(0, 8, P), (1, 9, P), (2, 10, DEC)]

        def turn_probs(h, b):
            rows, blocks = sample_rows(b), key_blocks(b)
            pe.wait_ge(S("pn"), 9 * h + b + 1)
            if b == 4:
                pe.wait_ge(S("k_tok"), 3 * h + 3)
            wait(pe, "pt_read", 13 * h + groups_before(b))
            for g in range(0, len(blocks), 4):
                for j, _, keys in blocks[g:g + 4]:
                    turned = P if keys == P else rows
                    last = turn(PB[5 + g // 4][0:keys, (j % 4) * P:(j % 4) * P + turned],
                                SB[0:turned, j * P:j * P + keys])
                last.then_inc(S("p_turn"), 1)

        def values(h, b):
            rows, blocks = sample_rows(b), key_blocks(b)
            if b % 4 == 0:
                pe.wait_ge(S("vt_read"), 3 * h + b // 4 + 1)
            if b == NB:
                pe.wait_ge(S("vc_in"), 16 * h + 16)
            wait(pe, "y_read", 9 * h + b)
            pe.wait_ge(S("pt_read"), 13 * h + groups_before(b) + (len(blocks) + 3) // 4)
            for i, (j, src, keys) in enumerate(blocks):
                last = mm(PB[7][:, 0:rows], VTOK[0:keys, src, :], PT[0:keys, j, 0:rows],
                          start=i == 0, stop=i == len(blocks) - 1)
            last.then_inc(S("pv"), 1)

        def add_last_head(c):
            pe.wait_ge(S("last_lo"), c + 1)
            project_chunk(tile_no(W_OO, 2, 0), tile_no(W_OO - 8, 2, 0), c, HH, HL, start=False, ks=[7])

        def turn_steps(t, attend=True, project=True):
            p = t + 1
            for i in range(STEPS):
                if project:
                    j = i // 3
                    project_chunk(tile_no(W_QKVZ + j, 4, p), tile_no(W_QKVZ - 8 + j, 4, p), i % 3, HH, HL)
                elif 2 <= i < 9:
                    for c in range(3):
                        project_chunk(tile_no(W_OO, 2, 0), tile_no(W_OO - 8, 2, 0), c, HH, HL,
                                      start=i == 2, stop=False, ready=("y1_lo",), ks=[i - 2])
                elif i == 10:
                    add_last_head(0)
                    add_last_head(1)
                if not attend and i == 4:
                    turn_lrow()
                if not attend and i == 8:
                    pe.wait_ge(S("lt"), 1)
                if attend and i == 0:
                    pe.wait_ge(S("n_ms"), 6 * t + 5)
                    norm_sum(t, 5, 4)
                    pe.wait_ge(S("vt_read"), 3 * t + 1)
                    turn_quad(VRAW, 1, 6, "vt_turn")
                if attend and i == 1:
                    pe.wait_ge(S("n_ms"), 6 * t + 6)
                    key_wait(DEC)
                    turn_quad(VRAW, 2, 4, "vt_turn")
                if attend and i == 2:
                    pe.wait_ge(S("n_done"), 2 * t + 2)
                    pe.wait_ge(S("vt_read"), 3 * t + 2)
                    turn_quad(KALL, 0, 6, "kt_turn")
                    pe.wait_ge(S("vt_read"), 3 * t + 3)
                    turn_quad(KALL, 1, 4, "kt_turn")
                if attend and i == 3:
                    pe.wait_ge(S("k_tok"), 3 * t + 1)
                    key_wait(DEC)
                    turn_quad(KALL, 2, 6, "kt_turn")
                if project and i == 8:
                    wait(pe, "sm", 9 * t + 8)
                    norm_sum(p, 0, 4)
                if project and i == 9:
                    pe.wait_ge(S("n_ms"), 6 * p + 1)
                    norm_sum(p, 1, 4)
                    wait(pe, "pt_read", 13 * t + 12)
                    norm_sum(p, 2, 6)
                if project and i == 10:
                    pe.wait_ge(S("n_ms"), 6 * p + 3)
                    pe.wait_ge(S("kc_in"), 16 * p + 16)
                    for b in range(2):
                        last = turn(PB[6][:, b * P:(b + 1) * P], KC[:, b, :])
                    last.then_inc(S("kc_turn"), 1)
                if project and i == 11:
                    pe.wait_ge(S("n_ms"), 6 * p + 4)
                    norm_sum(p, 4, 4)
                    pe.wait_ge(S("kc_done"), p + 1)
                    turn_quad(VRAW, 0, 6, "vt_turn")
                if attend and 2 <= i <= NB + 2:
                    values(t, i - 2)
                if attend and 1 <= i <= NB + 1:
                    turn_probs(t, i - 1)
                if attend and i <= NB:
                    scores(t, i)
                if project and i == 10:
                    pe.wait_ge(S("n_ms"), 6 * p + 2)
                    norm_sum(p, 3, 4)

        turn_steps(-1, attend=False)
        with pe.Fori(0, 7) as t:
            turn_steps(t)
        turn_steps(7, project=False)

        def out_odd(i, j):
            project(tile_no(W_OO + j, 2, i), tile_no(W_OO - 8 + j, 2, i), HH, HL)

        add_last_head(2)
        out_odd(0, 1)
        with pe.Fori(1, 4) as i:
            out_odd(i, 0)
            out_odd(i, 1)
        out_sums("o_sq", 48)
        pe.wait_ge(S("ss_ms"), 9)
        for k in range(8):
            pe.wait_ge(S(("x2_even", "x2_odd")[k % 2]), k // 2 + 1)
            for q, (b0, nb, rows) in enumerate(QUADS):
                if k >= 2:
                    pe.wait_ge(S("y_tok"), 3 * (k - 2) + q + 1)
                bank = ((3, 4, 5), (6, 7, 0))[k % 2][q]
                for j in range(nb):
                    last = turn(PB[bank][0:rows, j * P:(j + 1) * P],
                                O1[:, k, (b0 + j) * P:(b0 + j) * P + rows])
                last.then_inc(S("o_turn"), 1)

    @block.scalar
    def _(act):
        def copy(out, in_, scale=1.0):
            return act.activation(out, in_, ACT.Copy, scale=scale)

        order = Order(act, S("act_order"))

        def load_ln_exp():
            act.add_instruction(mybir.InstLoadActFuncSet(name=nc.get_next_instruction_name(),
                                                         act_func_set_id=LN_EXP_SET, ins=[], outs=[]))

        def split_high(w):
            act.wait_ge(S(f"w_raw{slot(w)}"), loads_of_slot(w))
            if not isinstance(w[2], int) or w[0] + w[1] * w[2] >= 2:
                act.wait_ge(S("p_chunk"), times(w, 3, -3))
            copy(WH[:, slot(w), :, :], WRAW[:, slot(w), :, :]).then_inc(S("w_high"), 1)

        def read_chunks(w, outs, func=ACT.Copy, rows=P):
            for c in range(3):
                act.wait_ge(S("p_chunk"), times(w, 3, c + 1))
                for cols, out in outs[c]:
                    last = act.activation(out, PB[c][0:rows, cols], func)
                last.then_inc(S(f"c_read{c}"), 1)

        def whole(t, rows=P):
            return [[(slice(0, CH), t[0:rows, c * CH:(c + 1) * CH])] for c in range(3)]

        def parted(t, prompt0, sample0):
            two = SEQ - 2 * CH
            return [[(slice(0, CH), t[:, prompt0:prompt0 + CH])],
                    [(slice(0, CH), t[:, prompt0 + CH:prompt0 + 2 * CH])],
                    [(slice(0, two), t[:, prompt0 + 2 * CH:prompt0 + SEQ]),
                     (slice(two, CH), t[:, sample0:sample0 + DEC])]]

        for b in range(NB + 2):
            if b <= NB:
                rows = sample_rows(b)
                act.wait_ge(S(f"x_in{b}"), 16)
                if b > 0:
                    act.wait_ge(S("x_ss"), b)
                act.activation(SQJ[0:rows, :], XS[0:rows, b, :], ACT.Square, accum_out=SS[0:rows, b:b + 1]) \
                    .then_inc(S("x_ss"), 1)
            if b == 0:
                continue
            b -= 1
            rows = sample_rows(b)
            act.wait_ge(S("x_ms"), b + 1)
            act.activation(RT[0:rows, b:b + 1], MS[0:rows, b:b + 1], ACT.Sqrt).then_inc(S("x_rt"), 1)
            if b == 2:
                act.wait_ge(S("rows_turn"), 1)
                order(copy(COLS[:, :], PB[3][:, 0:N_ROWS]))
                copy(DCOL[:, :], PB[3][:, P:P + 8]).then_inc(S("cols"), 1)
        order.fence()
        act.wait_ge(S("w_clear"), 1)
        for w in range(2):
            split_high(tile_no(w, 1, 0))
        for q, (b0, nb, rows) in enumerate(QUADS):
            for k in range(KT):
                i = q * KT + k
                act.wait_ge(S("x_t"), i + 1)
                act.activation(HH[:, k, b0 * P:b0 * P + nb * rows], PB[3 + i % 4][:, 0:nb * rows], ACT.Copy,
                               scale=COLS[:, PRE0 + k:PRE0 + k + 1]).then_inc(S("h_hi"), 1)

        def conv_silu(n, out):
            act.wait_ge(S("conv"), n + 1)
            order(act.activation(out[:, 0:SEQ], ACC[:, 0:SEQ], ACT.Silu))
            act.activation(out[:, SEQ:TOK], ACC[:, SEQ + 3:CONVW], ACT.Silu).then_inc(S("conv_act"), 1)

        def log1p_exp_steps(neg, e, w1, lg, name):
            act.wait_ge(S(name), 1)
            act.activation(e, neg, ACT.Exp).then_inc(S(name + "_a"), 1)
            act.wait_ge(S(name), 2)
            order(act.activation(lg, w1, ACT.Ln))
            order.fence()
            act.activation(neg, lg, ACT.Exp, scale=-1.0).then_inc(S(name + "_a"), 1)

        read_chunks(tile_no(W_DT, 1, 0), whole(RW[4], HEADS_B), rows=HEADS_B)
        split_high(tile_no(W_DT + 2, 1, 0))
        load_ln_exp()
        log1p_exp_steps(RW[5][:, :], RW[6][:, :], RW[1][:, :], RW[2][:, :], "dtc")
        act.wait_ge(S("par_in"), 64)
        act.activation(EAL[0:HEADS_B, :], AL[0:HEADS_B, :], ACT.Exp).then_inc(S("dtc_a"), 1)
        for j in range(4):
            w = tile_no(W_BC, 1, j)
            if j > 0:
                act.wait_ge(S("conv"), j)
            read_chunks(w, parted(XR, 3, SAMP))
            split_high(tile_no(W_BC + 2, 1, j))
            conv_silu(j, (BT, CT)[j // 2][:, j % 2, :])
            if j == 0:
                act.wait_ge(S("dtc"), 3)
                order(act.activation(RW[5][:, :], RW[5][:, :], ACT.Exp))
                act.activation(RW[3][:, :], ACSROW[:, :], ACT.Exp).then_inc(S("dtc_a"), 1)
        act.wait_ge(S("dt_turn"), 1)
        b3 = PB[3][:, 0:3 * 9 * HEADS_B].rearrange("p (q b h) -> p q b h", q=3, h=HEADS_B)
        b4 = PB[4][:, 0:9 * HEADS_B].rearrange("p (b h) -> p b h", h=HEADS_B)
        order(copy(TOKQ[:, 0:3, 0:NB, :], b3[:, :, 0:NB, :]))
        order(copy(TOKQ[0:DEC, 0:3, NB, :], b3[0:DEC, :, NB, :]))
        order(copy(TOKQ[:, 3, 0:NB, :], b4[:, 0:NB, :]))
        order(copy(TOKQ[0:DEC, 3, NB, :], b4[0:DEC, NB, :]))
        copy(DECB[:, :, :].rearrange("p h b -> p (h b)"), PB[4][:, 256:256 + 9 * HEADS_B]).then_inc(S("tokq"), 1)
        act.wait_ge(S("conv"), 4)
        read_chunks(tile_no(W_XZ, 2, 0), parted(XR, 3, SAMP))
        split_high(tile_no(W_XZ + 2, 2, 0))
        n = 0
        for g in range(GROUPS_B):
            for b0, nb, rows in QUADS:
                for what in range(2):
                    act.wait_ge(S("cb_mm"), n + 1)
                    width = rows if what == 0 else P
                    dst = (CBT, BTOK)[what][0:rows, g, b0:b0 + nb, 0:width]
                    src = PB[5 + n % 3][0:rows, 0:nb * P].rearrange("p (b c) -> p b c", c=P)[:, :, 0:width]
                    copy(dst, src).then_inc(S("cb_read"), 1)
                    n += 1
        read_chunks(tile_no(W_XZ + 1, 2, 0), whole(YB[:, 0, :]), ACT.Silu)
        split_high(tile_no(W_XZ + 3, 2, 0))

        def pair_steps(t, project=True):
            u = t - 1
            for i in range(PAIR_STEPS):
                c = i % 3
                w = tile_no(W_XZ + i // 3, 2, t)
                if project:
                    if i == 0:
                        act.wait_ge(S("conv"), 4 + t)
                    act.wait_ge(S("p_chunk"), times(w, 3, c + 1))
                    if i < 3:
                        for cols, out in parted(XR, 3, SAMP)[c]:
                            last = copy(out, PB[c][:, cols])
                    else:
                        last = act.activation(YB[:, t, c * CH:(c + 1) * CH], PB[c][:, 0:CH], ACT.Silu)
                    last.then_inc(S(f"c_read{c}"), 1)
                    if c == 2:
                        split_high(tile_no(W_XZ + 2 + i // 3, 2, t))
                for n in DECAYS_OF_STEP[i] if i < 3 else ():
                    j, q = DECAYS[n]
                    b0, nb, rows = QUADS[q]
                    act.wait_ge(S("seg"), 6 * u + n + 1)
                    m = M[0:rows, j, b0:b0 + nb, 0:rows]
                    act.activation(m, m, ACT.Exp).then_inc(S("mexp"), 1)
                if i == 3:
                    act.wait_ge(S("fs_turn"), u + 1)
                    wait(act, "ssd_stored", 32 * u)
                    copy(FSO[:, :, :].rearrange("p j n -> p (j n)"), PB[5][:, 2 * P:4 * P]).then_inc(S("fs_out"), 1)
                if project and i == 5:
                    act.wait_ge(S("yf"), 3 * t)
                    conv_silu(4 + t, XC)

        conv_silu(4, XC)
        with order.loop(1, 8, 1) as t:
            pair_steps(t)
        pair_steps(8, project=False)
        act.wait_ge(S("cst_turn"), 1)
        copy(CSO[:, :], PB[3][0:6 * XBC_TILES, 0:P]).then_inc(S("cso"), 1)
        act.wait_ge(S("yb"), 8)
        act.wait_ge(S("y_turn"), 24)

        def inverse_root(x, done):
            order(act.activation(x, x, ACT.Ln))
            order.fence()
            act.activation(x, x, ACT.Exp, scale=-0.5).then_inc(S(done), 1)

        with order.loop(0, 4, 0) as i:
            act.wait_ge(S("v_turn"), 6 * i)
            for j, out in enumerate((VG, UG)):
                w = tile_no(W_V + j, 2, i)
                read_chunks(w, whole(out), ACT.Gelu)
                split_high(tile_no(W_V + j + 2, 2, i))
            act.wait_ge(S("v_ms"), i + 1)
            act.activation(GSM[:, 2, 0:9], GSM[:, 2, 0:9], ACT.Sqrt).then_inc(S("v_rt"), 1)

        def inverse_root_chunks(n):
            for c in range(3):
                act.wait_ge(S("ss_ms"), 3 * n + c + 1)
                inverse_root(RSO[:, c * CH:(c + 1) * CH], "ss_rt")

        def read_uz(t):
            read_chunks(tile_no(W_UZ, 2, t), whole(UG), ACT.Gelu)
            split_high(tile_no(W_UZ + 2, 2, t))
            read_chunks(tile_no(W_UZ + 1, 2, t), whole(ZG), ACT.Silu)
            split_high(tile_no(W_UZ + 3, 2, t))

        act.wait_ge(S("v_turn"), 24)
        read_uz(0)
        act.wait_ge(S("ya"), 1)
        read_uz(1)
        load_ln_exp()
        act.wait_ge(S("gs_ms"), 6)
        inverse_root(RSY[:, :, :], "gs_rt")
        with order.loop(2, 8, 0) as t:
            act.wait_ge(S("ya"), t)
            read_uz(t)
        load_ln_exp()

        def high_halves(src, done, name=None):
            for n in range(3 * KT):
                k, cols = n % KT, slice(n // KT * CH, (n // KT + 1) * CH)
                if name:
                    act.wait_ge(S(name), n + 1)
                copy(HH[:, k, cols], src[:, k, cols]).then_inc(S(done), 1)

        act.wait_ge(S("yb_normed"), 8)
        act.wait_ge(S("p_chunk"), 3 * W_OE)
        high_halves(YB, "yb_hi")
        act.wait_ge(S("ya"), 8)
        for k in range(8):
            copy(YAH[:, k, :], YA[:, k, 0:TOK]).then_inc(S("ya_hi"), 1)
        with order.loop(0, 8, 0) as n:
            split_high(tile_no(W_OE + 2, 2, n))
            read_chunks(tile_no(W_OE + 1, 2, n), whole(O0[:, n, :]))
            split_high(tile_no(W_OE + 3, 2, n))
        inverse_root_chunks(0)
        for k in range(8):
            act.wait_ge(S("x1"), k + 1)
            if k > 1:
                act.wait_ge(S("x1_sums"), k - 1)
            act.activation(X1SQ[(k + 1) % 2][:, 0:TOK], O0[:, k, :], ACT.Square).then_inc(S("x1_s"), 1)
        inverse_root_chunks(1)
        high_halves(HX, "h1_hi", "h1_x")

        read_chunks(tile_no(W_F, 1, 0), whole(FW[0], HEADS_C), rows=HEADS_C)
        split_high(tile_no(W_F + 2, 1, 0))
        log1p_exp_steps(FW[2][:, :], FW[3][:, :], FW[4][:, :], FW[5][:, :], "fc")

        def last_head_high(c):
            act.wait_ge(S("y_read"), 63 + (3, 6, 9)[c])
            cols = slice(c * CH, (c + 1) * CH)
            copy(HH[:, 7, cols], Y1[:, 7, cols]).then_inc(S("last_hi"), 1)

        def turn_steps(t, attend=True, project=True):
            p = t + 1

            def read(i):
                j, c = i // 3, i % 3
                w = tile_no(W_QKVZ + j, 4, p)
                act.wait_ge(S("p_chunk"), times(w, 3, c + 1))
                cols = slice(c * CH, (c + 1) * CH)
                if j == V_:
                    wait(act, "vt_turn", 3 * p + c - 2)
                    last = copy(VRAW[:, cols], PB[c][:, 0:CH])
                elif j == Z_:
                    last = copy(Y1[:, p, cols], PB[c][:, 0:CH])
                elif j == Q_:
                    wait(act, "sc_mm", 9 * p + 3 * c - 6)
                    last = copy(QT[:, cols], PB[c][:, 0:CH])
                else:
                    wait(act, "sc_mm", 9 * p)
                    for part, key in norm_chunk(3 + c):
                        last = copy(key, PB[c][:, part])
                last.then_inc(S(f"c_read{c}"), 1)
                if i == 5:
                    act.wait_ge(S("c_read2"), times(tile_no(W_QKVZ - 8 + Z_, 4, p), 1, 1))
                if c == 2:
                    split_high(tile_no(W_QKVZ + 2 + j, 4, p))
                if i == 5:
                    act.activation(Y1[:, p, :], Y1[:, p, :], ACT.Silu).then_inc(S("zs"), 1)
                    load_ln_exp()

            def read_turned(dst, bank, rows, n, name):
                copy(dst, PB[bank][0:rows, 0:n * P].rearrange("p (b d) -> p b d", d=P)).then_inc(S(name), 1)

            def probs_read(b):
                blocks = b + 1 if b < NB else 3
                for g in range(0, blocks, 4):
                    nb = min(4, blocks - g)
                    act.wait_ge(S("p_turn"), 13 * t + groups_before(b) + g // 4 + 1)
                    if g == 0:
                        wait(act, "pv", 9 * t + b)
                    bank = PB[5 + g // 4]
                    if b < NB:
                        last = copy(PT[:, g:g + nb, :], bank[:, 0:nb * P].rearrange("p (b l) -> p b l", l=P))
                    else:
                        src = bank[:, 0:3 * P].rearrange("p (b l) -> p b l", l=P)
                        copy(PT[:, 0:2, 0:DEC], src[:, 0:2, 0:DEC])
                        last = copy(PT[0:DEC, 2, 0:DEC], src[0:DEC, 2, 0:DEC])
                    last.then_inc(S("pt_read"), 1)

            for i in range(STEPS):
                if not attend and i == 6:
                    act.wait_ge(S("lt"), 1)
                if project:
                    read(i)
                if attend and i == 0:
                    act.wait_ge(S("vt_turn"), 3 * t + 2)
                    read_turned(VTOK[:, 4:8, :], 6, P, 4, "vt_read")
                if attend and i == 1:
                    act.wait_ge(S("vt_turn"), 3 * t + 3)
                    read_turned(VTOK[0:DEC, NB + 2:NB + 3, :], 4, DEC, 1, "vt_read")
                    act.wait_ge(S("n_ms"), 6 * t + 6)
                    inverse_root(NRM[:, 0:5:4, :], "n_rt")
                if attend and i == 2:
                    wait(act, "k_stored", 32 * t)
                    for q, bank in ((0, 6), (1, 4)):
                        act.wait_ge(S("kt_turn"), 3 * t + q + 1)
                        read_turned(KTOK[:, 4 * q:4 * q + 4, :], bank, P, 4, "k_tok")
                if attend and i == 3:
                    act.wait_ge(S("kt_turn"), 3 * t + 3)
                    copy(KSAM, PB[6][0:DEC, 0:P]).then_inc(S("k_tok"), 1)
                if attend and 1 <= i <= NB + 1:
                    probs_read(i - 1)
                if project and i == 10:
                    act.wait_ge(S("kc_turn"), p + 1)
                    copy(KALL[:, SEQ:SEQ + PAST], PB[6][:, 0:PAST]).then_inc(S("kc_done"), 1)
                if project and i == 11:
                    act.wait_ge(S("vt_turn"), 3 * p + 1)
                    wait(act, "pv", 9 * p)
                    wait(act, "v_stored", 32 * p)
                    read_turned(VTOK[:, 0:4, :], 6, P, 4, "vt_read")
                if project and i == 10:
                    act.wait_ge(S("n_ms"), 6 * p + 4)
                    inverse_root(NRM[:, 0:4, :], "n_rt")
                if project and i >= 6:
                    n = i - 6
                    if n < 3:
                        act.wait_ge(S("nf_stored"), 16)
                        wait(act, "n_ss", 6 * p + n - 2)
                    else:
                        act.wait_ge(S("n_ss"), 6 * p + n - 2)
                    act.wait_ge(S("n_sq"), 6 * p + n + 1)
                    copy(NRMH[:, n % 3, :], NRM[:, NORM_SLOT[n], :]).then_inc(S("n_hi"), 1)
                if attend and i <= NB:
                    act.wait_ge(S("sm"), 9 * t + i + 1)
                    rows = sample_rows(i)
                    width = PAST + DEC if i == NB else (i + 1) * P
                    act.activation(SB[0:rows, 0:width], SB[0:rows, 0:width], ACT.Exp, scale=SCALE,
                                   bias=NBIAS[0:rows, :], accum_out=RSUM[0:rows, :]).then_inc(S("ex"), 1)
                if not project and i < 7:
                    act.wait_ge(S("p_chunk"), 3 * W_OO)
                    copy(HH[:, i, :], Y1[:, i, :]).then_inc(S("y1_hi"), 1)
                if not project and i in (7, 8):
                    last_head_high(i - 7)

        turn_steps(-1, attend=False)
        act.wait_ge(S("lf_stored"), 32)
        with order.loop(0, 7, 2) as t:
            turn_steps(t)
        turn_steps(7, project=False)
        last_head_high(2)

        def out_odd(i, j, more):
            n = tile_no(W_OO + j, 2, i)
            k = 2 * i + j
            read_chunks(n, whole(O1[:, k, :]))
            if more:
                split_high(tile_no(W_OO + j + 2, 2, i))

        act.wait_ge(S("y1_lo"), 7)
        act.wait_ge(S("last_lo"), 3)
        with act.Fori(0, 3) as i:
            out_odd(i, 0, True)
            out_odd(i, 1, True)
        out_odd(3, 0, False)
        out_odd(3, 1, False)
        inverse_root_chunks(2)
        for k in range(7):
            for q, (b0, nb, rows) in enumerate(QUADS):
                bank = ((3, 4, 5), (6, 7, 0))[k % 2][q]
                act.wait_ge(S("o_turn"), 3 * k + q + 1)
                if q == 0 and k >= 3:
                    act.wait_ge(S(f"y_stored{k % 3}"), 32 * (k // 3))
                copy(YO[0:rows, k % 3, b0:b0 + nb, :],
                     PB[bank][0:rows, 0:nb * P].rearrange("p (b d) -> p b d", d=P)).then_inc(S("y_tok"), 1)

    @block.vector
    def _(dve):
        order = Order(dve, S("dve_order"))

        def tt(out, a, b, op):
            return dve.tensor_tensor(out, a, b, op)

        def ts(out, a, s1, s2, op0, op1=ALU.bypass):
            return dve.tensor_scalar(out, a, s1, s2, op0, op1) if s2 is not None else \
                dve.tensor_scalar(out, a, s1, None, op0)

        def stt(out, a, s, b, op0, op1):
            return dve.scalar_tensor_tensor(out=out, in0=a, scalar=s, in1=b, op0=op0, op1=op1)

        order(dve.memset(ONES[:, :], 1.0))
        for b in range(NB + 2):
            if b <= NB:
                rows = sample_rows(b)
                dve.wait_ge(S("x_ss"), b + 1)
                ts(MS[0:rows, b:b + 1], SS[0:rows, b:b + 1], 1.0 / D, EPS, ALU.mult, ALU.add).then_inc(S("x_ms"), 1)
            if b == 0:
                continue
            b -= 1
            rows = sample_rows(b)
            dve.wait_ge(S("x_rt"), b + 1)
            order(dve.reciprocal(RR[0:rows, b:b + 1], RT[0:rows, b:b + 1]))
            order.fence()
            ts(XS[0:rows, b, :], XS[0:rows, b, :], RR[0:rows, b:b + 1], None, ALU.mult).then_inc(S("xn"), 1)
            if b == 1:
                dve.wait_ge(S("rows_in"), 160)
                dve.tensor_copy(DEXP[:, :, :], DSM[:, :].unsqueeze(2).broadcast_to([8, 2, HP])) \
                    .then_inc(S("dexp"), 1)
        for q, (b0, nb, rows) in enumerate(QUADS):
            for k in range(KT):
                i = q * KT + k
                cols = slice(b0 * P, b0 * P + nb * rows)
                dve.wait_ge(S("h_hi"), i + 1)
                stt(HL[:, k, cols], PB[3 + i % 4][:, 0:nb * rows], COLS[:, PRE0 + k:PRE0 + k + 1],
                    HH[:, k, cols].bitcast(f32), ALU.mult, ALU.subtract).then_inc(S("h_lo"), 1)

        def conv(n, tile, w):
            dve.wait_ge(S("c_read2"), times(w, 1, 1))
            if not isinstance(n, int) or n > 0:
                dve.wait_ge(S("conv_act"), n)
            past = COLS[:, CTX:CTX + 36].rearrange("p (r t) -> p r t", t=XBC_TILES)
            order(dve.tensor_copy(XR[:, 3 + SEQ:SAMP], past[:, :, tile]))
            order(dve.tensor_copy(CST[:, 0:3, tile], XR[:, SEQ:SEQ + 3]))
            order(dve.tensor_copy(CST[:, 3:6, tile], XR[:, SAMP + DEC - 3:SAMP + DEC]))
            order.fence()
            taps = CONVW_SB[:, tile, :]
            order(ts(ACC[:, :], XR[:, 0:CONVW], taps[:, 0:1], COLS[:, CONVB:CONVB + XBC_TILES][:, bass.ds(tile, 1)],
                     ALU.mult, ALU.add))
            for k in range(1, TAPS):
                order.fence()
                ins = stt(ACC[:, :], XR[:, k:k + CONVW], taps[:, k:k + 1], ACC[:, :], ALU.mult, ALU.add)
                if k < TAPS - 1:
                    order(ins)
            ins.then_inc(S("conv"), 1)

        dve.wait_ge(S("par_in"), 64)
        dve.wait_ge(S("p_chunk"), 1)
        order(dve.memset(XR[:, 0:3], 0.0))

        def log1p_exp(raw, bias, x, neg, e, w1, lg, c, name):
            order(ts(x, raw, bias, None, ALU.add))
            order.fence()
            order(ts(neg, x, -1.0, None, ALU.mult))
            order.fence()
            tt(neg, x, neg, ALU.min).then_inc(S(name), 1)
            dve.wait_ge(S(name + "_a"), 1)
            ts(w1, e, 1.0, None, ALU.add).then_inc(S(name), 1)
            dve.wait_ge(S(name), 2)
            order(ts(c, w1, -1.0, None, ALU.add))
            order.fence()
            order(tt(c, e, c, ALU.subtract))
            order.fence()
            dve.wait_ge(S(name + "_a"), 2)
            order(tt(c, c, neg, ALU.mult))
            order.fence()
            order(tt(lg, lg, c, ALU.add))
            order.fence()

        dve.wait_ge(S("c_read2"), W_DT + 1)
        log1p_exp(RW[4][:, :], DTB[0:HEADS_B, :], RW[0][:, :], RW[5][:, :], RW[6][:, :], RW[1][:, :], RW[2][:, :],
                  RW[7][:, :], "dtc")
        conv(0, 8, tile_no(W_BC, 1, 0))
        order(stt(RW[0][:, :], RW[0][:, :], 0.0, RW[2][:, :], ALU.max, ALU.add))
        order.fence()
        dve.wait_ge(S("dtc_a"), 3)
        order(ts(RW[6][:, :], RW[0][:, :], EAL[0:HEADS_B, :], -1.0, ALU.mult, ALU.mult))
        order(dve.memset(RW[4][:, :], 1.0))
        order.fence()
        order(dve.memset(RW[4][:, 0:TOK:P], 0.0))
        order.fence()
        order(dve.tensor_tensor_scan(ACSROW[:, :], RW[4][:, :], RW[6][:, :], 0.0, ALU.mult, ALU.add))
        order.fence()
        ends = ACSROW[:, P - 1:SEQ:P]
        order(tt(RW[5][:, 0:SEQ].rearrange("h (b l) -> h b l", l=P), ends.unsqueeze(2).broadcast_to([HEADS_B, NB, P]),
                 ACSROW[:, 0:SEQ].rearrange("h (b l) -> h b l", l=P), ALU.subtract))
        tt(RW[5][:, SEQ:TOK], ACSROW[:, TOK - 1:TOK].broadcast_to([HEADS_B, DEC]), ACSROW[:, SEQ:TOK], ALU.subtract) \
            .then_inc(S("dtc"), 1)
        dve.wait_ge(S("dtc_a"), 4)
        order(tt(RW[2][:, :], RW[5][:, :], RW[0][:, :], ALU.mult))
        one = IDENT[0:HEADS_B, 0:HEADS_B].unsqueeze(2)
        order(tt(DECR[:, :, 0:NB], one.broadcast_to([HEADS_B, HEADS_B, NB]),
                 RW[3][:, P - 1:SEQ:P].unsqueeze(1).broadcast_to([HEADS_B, HEADS_B, NB]), ALU.mult))
        tt(DECR[:, :, NB:NB + 1], one,
           RW[3][:, TOK - 1:TOK].unsqueeze(1).broadcast_to([HEADS_B, HEADS_B, 1]), ALU.mult).then_inc(S("dt_rows"), 1)

        def heads_of(q, t, b0, nb, rows):
            return TOKQ[0:rows, q, b0:b0 + nb, bass.ds(2 * t, 2)].unsqueeze(3).broadcast_to([rows, nb, 2, HP])

        def decays(u, n):
            j, q = DECAYS[n]
            b0, nb, rows = QUADS[q]
            dve.wait_ge(S("acs_in"), 32 * u + 32)
            for i in range(nb):
                cols = slice((b0 + i) * P, (b0 + i) * P + rows)
                last = stt(M[0:rows, j, b0 + i, 0:rows], ACSB[j][0:rows, cols],
                           TOKQ[0:rows, 3, b0 + i, bass.ds(2 * u + j, 1)], MASKT[0:rows, 0:rows],
                           ALU.subtract, ALU.min)
            last.then_inc(S("seg"), 1)

        def pair_steps(t, project=True):
            u = t - 1
            for i in range(PAIR_STEPS):
                if i == 0:
                    wait(dve, "yb", u)
                    for q, (b0, nb, rows) in enumerate(QUADS):
                        dve.wait_ge(S("xc_turn"), 3 * u + q + 1)
                        src = PB[3 + q][0:rows, 0:nb * P].rearrange("p (b j d) -> p b j d", j=2, d=HP)
                        for k, dst in enumerate((XD, XW)):
                            last = tt(dst[0:rows, b0:b0 + nb, :].rearrange("p b (j d) -> p b j d", j=2), src,
                                      heads_of(k, u, b0, nb, rows), ALU.mult)
                        last.then_inc(S("xw"), 1)
                for n in DECAYS_OF_STEP[i] if i < 2 else ():
                    decays(u, n)
                if i == 1:
                    dve.wait_ge(S("ds"), 3 * u + 3)
                    wait(dve, "fs_turn", u)
                    order(dve.memset(ST[:, 0, :], 0.0))
                    order(dve.tensor_copy(ST[:, 1, :], PB[3][:, 0:P]))
                    dve.wait_ge(S("si_used"), u + 1)
                    order(dve.tensor_copy(ST[:, NB, :], PB[5][:, P:2 * P]))
                    for b in range(1, NB + 1):
                        order.fence()
                        dst = ST[:, b + 1, :] if b < NB - 1 else FS[:, b - NB + 1, :]
                        new = PB[3 + b // 4][:, (b % 4) * P:(b % 4 + 1) * P]
                        for k in range(2):
                            cols = slice(k * HP, (k + 1) * HP)
                            decay = DECB[:, bass.ds(2 * u + k, 1), b:b + 1].rearrange("p a b -> p (a b)")
                            ins = stt(dst[:, cols], ST[:, b, cols], decay, new[:, cols], ALU.mult, ALU.add)
                            if b < NB or k == 0:
                                order(ins)
                    ins.then_inc(S("st"), 1)
                    decays(u, 4)
                    decays(u, 5)
                if project and i == 3:
                    conv(4 + t, t, tile_no(W_XZ, 2, t))
                if i == 4:
                    for q, (b0, nb, rows) in enumerate(QUADS):
                        intra, state = PB[(3, 6, 5)[q]], PB[(4, 7, 5)[q]]
                        off = P if q == 2 else 0
                        dve.wait_ge(S("y_mm"), 3 * u + q + 1)
                        yt = YT[0:rows, b0:b0 + nb, :]
                        order(tt(yt.rearrange("p b (j d) -> p b j d", j=2),
                                 state[0:rows, off:off + nb * P].rearrange("p (b j d) -> p b j d", j=2, d=HP),
                                 heads_of(2, u, b0, nb, rows), ALU.mult))
                        order.fence()
                        tt(yt, yt, intra[0:rows, 0:nb * P].rearrange("p (b d) -> p b d", d=P), ALU.add) \
                            .then_inc(S("yt"), 1)
                if i == 5:
                    for q, (b0, nb, rows) in enumerate(QUADS):
                        cols = slice(b0 * P, b0 * P + nb * rows)
                        dve.wait_ge(S("y_turn"), 3 * u + q + 1)
                        stt(YF[:, cols], XC[:, cols], DCOL[:, bass.ds(u, 1)], PB[3 + q][:, 0:nb * rows],
                            ALU.mult, ALU.add).then_inc(S("yf"), 1)

        for j in range(1, 4):
            conv(j, 8 + j, tile_no(W_BC, 1, j))
        conv(4, 0, tile_no(W_XZ, 2, 0))
        dve.wait_ge(S("tokq"), 1)
        with order.loop(1, 8, 27) as t:
            pair_steps(t)
        pair_steps(8, project=False)

        dve.wait_ge(S("cso"), 1)
        dve.wait_ge(S("ssd_stored"), 256)
        dve.wait_ge(S("conv_stored"), 96)
        dve.wait_ge(S("yb"), 8)
        order(dve.memset(V[:, :, NB * P:], 0.0))
        order(dve.memset(RSY[:, :, :], 0.0))
        order.fence()
        dve.wait_ge(S("gv_in"), 48)
        for g in range(GROUPS_B):
            with order.loop(2 * g, 2 * g + 2, 9) as i:
                for j in range(2):
                    for q, (b0, nb, rows) in enumerate(QUADS):
                        bank = (3, 4, 5, 6, 7, 3)[3 * j + q]
                        dve.wait_ge(S("v_turn"), 6 * i + 3 * j + q + 1)
                        dve.tensor_copy(V[0:rows, 2 * i + j, b0 * P:(b0 + nb) * P], PB[bank][0:rows, 0:nb * P]) \
                            .then_inc(S("v_tok"), 1)
                dve.wait_ge(S("v_tok"), 6 * i + 6)
                vj = [V[:, 2 * i + j, :].rearrange("p (b f) -> p b f", f=P) for j in range(2)]
                for j in range(2):
                    order(tt(SQV[:, :, j * P:(j + 1) * P], vj[j], vj[j], ALU.mult))
                order.fence()
                order(dve.tensor_reduce(GSM[:, 0, 0:9], SQV[:, :, :], AX.X, ALU.add))
                order.fence()
                ts(GSM[:, 2, 0:9], GSM[:, 0, 0:9], 1.0 / (2 * P), EPS, ALU.mult, ALU.add).then_inc(S("v_ms"), 1)
                for j in range(2):
                    yb = YB[:, 2 * i + j, :]
                    order(tt(TMP[:, :], yb, yb, ALU.mult))
                    order.fence()
                    tt(RSY[:, g, :], RSY[:, g, :], TMP[:, :], ALU.add).then_inc(S("y_sq"), 1)
                    dve.wait_ge(S("y_sq"), 2 * i + j + 1)
                dve.wait_ge(S("v_rt"), i + 1)
                order(dve.reciprocal(GSM[:, 3, 0:9], GSM[:, 2, 0:9]))
                order.fence()
                for j in range(2):
                    order(tt(vj[j], vj[j], GSM[:, 3, 0:9].unsqueeze(2).broadcast_to([P, 9, P]), ALU.mult))
                order.fence()
                order(tt(vj[0], vj[0], GVB[:, i, 0:P].unsqueeze(1).broadcast_to([P, 9, P]), ALU.mult))
                order.fence()
                tt(vj[1], vj[1], GVB[:, i, P:2 * P].unsqueeze(1).broadcast_to([P, 9, P]), ALU.mult) \
                    .then_inc(S("v_normed"), 1)
        dve.wait_ge(S("ws_turn"), 1)
        order(dve.tensor_copy(WT[:, :, :].rearrange("p g i -> p (g i)"), PB[6][:, :]))
        order.fence()
        dve.memset(WT[P // 2:P, :, 0:P // 2], 0.0).then_inc(S("wt"), 1)
        dve.wait_ge(S("gv_stored"), 16)

        def gated(i, j):
            t = 2 * i + j
            wait(dve, "s_mm", 6 * i + 3 * j)
            dve.tensor_copy(VS[:, :, :], V[:, t, :].rearrange("p (b f) -> p b f", f=P)).then_inc(S("vs"), 1)
            dve.wait_ge(S("c_read2"), W_UZ + 2 + 4 * i + 2 * j)
            order(tt(UG[:, :], UG[:, :], ZG[:, :], ALU.mult))
            order.fence()
            for q, (b0, nb, rows) in enumerate(QUADS):
                dve.wait_ge(S("s_mm"), 6 * i + 3 * j + q + 1)
                tt(ZG[:, b0 * P:b0 * P + nb * rows].rearrange("p (b l) -> p b l", l=rows),
                   PB[3 + q][:, 0:nb * rows].rearrange("p (b l) -> p b l", l=rows),
                   BSB[:, i, 0:rows].unsqueeze(1).broadcast_to([P, nb, rows]), ALU.add).then_inc(S("s_read"), 1)
            dve.wait_ge(S("s_read"), 6 * i + 3 * j + 3)
            dve.wait_ge(S("vs"), t + 1)
            tt(YA[:, t, 0:TOK], ZG[:, :], UG[:, :], ALU.mult).then_inc(S("ya"), 1)

        def normalise_yb(k, g):
            stt(YB[:, k, :], YB[:, k, :], COLS[:, GSSD:GSSD + 8][:, bass.ds(k, 1)], RSY[:, g, :],
                ALU.mult, ALU.mult).then_inc(S("yb_normed"), 1)

        gated(0, 0)
        for n in range(6):
            g, c = n // 3, n % 3
            dve.wait_ge(S("gs_mm"), 3 * g + 3 if n < 5 else 6)
            ts(RSY[:, g, c * CH:(c + 1) * CH], PB[(3, 4, 5, 6, 7, 3)[n]][:, 0:CH], 1.0 / 512, EPS, ALU.mult, ALU.add) \
                .then_inc(S("gs_ms"), 1)
        gated(0, 1)
        dve.wait_ge(S("gs_rt"), 1)
        normalise_yb(3, 0)
        normalise_yb(7, 1)
        with order.loop(1, 4, 2) as i:
            for j in range(2):
                normalise_yb(4 * j + i - 1, j)
                gated(i, j)

        dve.wait_ge(S("p_chunk"), 3 * W_OE)

        def to_halves(src, normalised, name, hi, lo):
            for n in range(3 * KT + 1):
                if normalised and n < 3 * KT:
                    k, cols = n % KT, slice(n // KT * CH, (n // KT + 1) * CH)
                    normalised(k, cols).then_inc(S(name), 1)
                if n % 2 == 1:
                    k, cols = (n - 1) % KT, slice((n - 1) // KT * CH, ((n - 1) // KT + 1) * CH)
                    dve.wait_ge(S(hi), n)
                    tt(HL[:, k, cols], src[:, k, cols], HH[:, k, cols].bitcast(f32), ALU.subtract) \
                        .then_inc(S(lo), 1)

        to_halves(YB, None, None, "yb_hi", "yb_lo")
        dve.wait_ge(S("yb_lo"), 12)
        dve.wait_ge(S("yb_lo_odd"), 12)
        for k in range(8):
            dve.wait_ge(S("ya_hi"), k + 1)
            tt(YAL[:, k, :], YA[:, k, 0:TOK], YAH[:, k, :].bitcast(f32), ALU.subtract).then_inc(S("ya_lo"), 1)

        def add_squares(tile, u, n):
            for c in range(3):
                cols = slice(c * CH, (c + 1) * CH)
                dve.wait_ge(S(f"c_read{c}"), times(u, 1, 1))
                dve.wait_ge(S("o_sq"), 3 * n)
                order(tt(TMP[:, cols], tile[:, cols], tile[:, cols], ALU.mult))
                order.fence()
                tt(SQA[:, cols], SQA[:, cols], TMP[:, cols], ALU.add).then_inc(S("o_sq"), 1)

        order(dve.memset(SQA, 0.0))
        order.fence()
        with order.loop(0, 8, 3) as n:
            add_squares(O0[:, n, :], tile_no(W_OE, 1, n), n)

        def rstd(n):
            for c in range(3):
                if n == 1:
                    dve.wait_ge(S("x1_sums"), 8)
                else:
                    dve.wait_ge(S("ss_mm"), (n // 2) * 3 + c + 1)
                ts(RSO[:, c * CH:(c + 1) * CH], PB[c if n == 1 else 3 + c][:, 0:CH], 1.0 / D, EPS,
                   ALU.mult, ALU.add).then_inc(S("ss_ms"), 1)
            dve.wait_ge(S("ss_rt"), 3 * n + 3)

        rstd(0)
        for k in range(8):
            order(stt(O0[:, k, :], O0[:, k, :], COLS[:, POST0 + k:POST0 + k + 1], RSO, ALU.mult, ALU.mult))
            order.fence()
            dve.wait_ge(S("x_turn"), k + 1)
            for q, (b0, nb, rows) in enumerate(QUADS):
                bank = ((3, 4, 5), (6, 7, 5))[k % 2][q]
                cols = slice(b0 * P, b0 * P + nb * rows)
                last = tt(O0[:, k, cols], O0[:, k, cols], PB[bank][:, 0:nb * rows], ALU.add)
            last.then_inc(S("x1"), 1)
        rstd(1)
        to_halves(HX, lambda k, cols: stt(HX[:, k, cols], O0[:, k, cols], COLS[:, PRE1 + k:PRE1 + k + 1],
                                      RSO[:, cols], ALU.mult, ALU.mult), "h1_x", "h1_hi", "h1_lo")

        dve.wait_ge(S("c_read2"), W_F - 8 + 1)
        log1p_exp(FW[0][:, :], BF[0:HEADS_C, :], FW[1][:, :], FW[2][:, :], FW[3][:, :], FW[4][:, :], FW[5][:, :],
                  FW[0][:, :], "fc")
        order(ts(FW[1][:, :], FW[1][:, :], 0.0, None, ALU.min))
        order.fence()
        order(tt(LROW[:, 0:SEQ], FW[1][:, 0:SEQ], FW[5][:, 0:SEQ], ALU.subtract))
        order(tt(LROW[:, SEQ + PAST:KEYS], FW[1][:, SEQ:TOK], FW[5][:, SEQ:TOK], ALU.subtract))
        dve.wait_ge(S("clf_turn"), 1)
        dve.tensor_copy(LROW[:, SEQ:SEQ + PAST], PB[3][0:HEADS_C, 0:PAST]).then_inc(S("lrow"), 1)
        order(dve.memset(ONEROW[:, :], 1.0))
        order.fence()
        order(dve.memset(ONEROW[:, 0:KEYS:SEQ], 0.0))
        order.fence()
        dve.wait_ge(S("lrow"), 1)
        order(dve.tensor_tensor_scan(NFROW[:, :], ONEROW[:, :], LROW[:, :], 0.0, ALU.mult, ALU.add))
        order.fence()
        ts(NFROW[:, :], NFROW[:, :], -1.0 / SCALE, None, ALU.mult).then_inc(S("nfrow"), 1)
        dve.wait_ge(S("lt_turn"), 1)
        order(dve.tensor_copy(LT[:, 0:NB, :], PB[4][:, 0:NB * HEADS_C].rearrange("p (b h) -> p b h", h=HEADS_C)))
        dve.tensor_copy(LT[0:DEC, NB, :], PB[4][0:DEC, NB * HEADS_C:(NB + 1) * HEADS_C]).then_inc(S("lt"), 1)
        order.fence()
        dve.wait_ge(S("masks"), 2)
        dve.wait_ge(S("lf_stored"), 32)

        def turn_steps(t, attend=True, project=True):
            p = t + 1

            def mean_square(h, n, bank):
                dve.wait_ge(S("n_ss"), 6 * h + n + 1)
                ts(NRM[:, NORM_SLOT[n], :], PB[bank][:, 0:CH], 1.0 / P, EPS, ALU.mult, ALU.add).then_inc(S("n_ms"), 1)

            def norms(h, chunks, count):
                dve.wait_ge(S("n_rt"), 2 * h + count)
                for n in chunks:
                    gain = GQ if n < 3 else GK
                    for cols, x in norm_chunk(n):
                        last = stt(x, x, COLS[:, gain:gain + 1], NRM[:, NORM_SLOT[n], cols], ALU.mult, ALU.mult)
                last.then_inc(S("n_done"), 1)

            for i in range(STEPS):
                if attend and 2 <= i <= NB + 2:
                    b = i - 2
                    rows = sample_rows(b)
                    if b == 0:
                        dve.wait_ge(S("zs"), t + 1)
                    dve.wait_ge(S("pv"), 9 * t + b + 1)
                    y = Y1[:, t, b * P:b * P + rows]
                    tt(y, PB[7][:, 0:rows], y, ALU.mult).then_inc(S("y_read"), 1)
                if attend and i <= NB:
                    rows = sample_rows(i)
                    if i == 0:
                        dve.wait_ge(S("nf"), 16 * t + 16)
                    dve.wait_ge(S("sc_mm"), 9 * t + i + 1)
                    wait(dve, "p_turn", 13 * t + groups_before(i))
                    key0, width = (SEQ, PAST + DEC) if i == NB else (0, (i + 1) * P)
                    n = (width + 511) // 512
                    order(dve.memset(MX[0:rows, n:n + 1], -3.0e38))
                    for k in range(n):
                        c0, c1 = k * 512, min(width, k * 512 + 512)
                        order(dve.tensor_tensor_reduce(SB[0:rows, c0:c1], PB[3 + k][0:rows, 0:c1 - c0],
                                                       NFB[0:rows, key0 + c0:key0 + c1], 1.0, -3.0e38,
                                                       ALU.add, ALU.max, MX[0:rows, k:k + 1]))
                    order.fence()
                    order(dve.tensor_reduce(MXR[0:rows, :], MX[0:rows, 0:n + 1], AX.X, ALU.max))
                    order.fence()
                    ts(NBIAS[0:rows, :], MXR[0:rows, :], -SCALE, None, ALU.mult).then_inc(S("sm"), 1)
                if attend and i == 0:
                    mean_square(t, 5, 4)
                if attend and i == 1:
                    norms(t, (4, 5), 2)
                if project and i == 8:
                    mean_square(p, 0, 4)
                if project and i == 9:
                    mean_square(p, 1, 4)
                    mean_square(p, 2, 6)
                if project and i == 10:
                    mean_square(p, 3, 4)
                if project and i == 11:
                    norms(p, (0, 1, 2, 3), 1)
                    mean_square(p, 4, 4)
                if project and i >= 6:
                    n = i - 6
                    dve.wait_ge(S("n_hi"), 6 * p + n + 1)
                    tt(NRML[:, NORM_SLOT[n], :], NRM[:, NORM_SLOT[n], :], NRMH[:, n % 3, :].bitcast(f32),
                       ALU.subtract).then_inc(S("n_lo"), 1)
                if attend and i <= NB:
                    dve.wait_ge(S("ex"), 9 * t + i + 1)
                    order(dve.reciprocal(RINV[0:rows, :], RSUM[0:rows, :]))
                    order.fence()
                    ts(SB[0:rows, 0:width], SB[0:rows, 0:width], RINV[0:rows, :], None, ALU.mult).then_inc(S("pn"), 1)
                if not project and i in (8, 9):
                    last_head_low(i - 8)

        def last_head_low(c):
            cols = slice(c * CH, (c + 1) * CH)
            dve.wait_ge(S("last_hi"), c + 1)
            tt(HL[:, 7, cols], Y1[:, 7, cols], HH[:, 7, cols].bitcast(f32), ALU.subtract).then_inc(S("last_lo"), 1)

        dve.tensor_copy(ONESR[:, :], ONES[:, :])
        turn_steps(-1, attend=False)
        with order.loop(0, 7, 40) as t:
            turn_steps(t)
        turn_steps(7, project=False)
        last_head_low(2)
        order(dve.memset(SQA, 0.0))
        order.fence()
        with order.loop(0, 8, 3) as n:
            add_squares(O1[:, n, :], tile_no(W_OO - 8, 1, n), n + 8)
        rstd(2)
        for k in range(8):
            last = stt(O1[:, k, :], O1[:, k, :], COLS[:, POST1 + k:POST1 + k + 1], RSO, ALU.mult, ALU.mult)
            if k % 2 == 0:
                last.then_inc(S("o1_n"), 1)
            else:
                order(last)
                order.fence()
                tt(O1[:, k, :], O1[:, k, :], O0[:, k, :], ALU.add).then_inc(S("x2_odd"), 1)
        dve.wait_ge(S("y_stored1"), 64)
        for q, (b0, nb, rows) in enumerate(QUADS):
            dve.wait_ge(S("o_turn"), 21 + q + 1)
            dve.tensor_copy(YO[0:rows, 1, b0:b0 + nb, :],
                            PB[(6, 7, 0)[q]][0:rows, 0:nb * P].rearrange("p (b d) -> p b d", d=P)) \
                .then_inc(S("y_last"), 1)

    ctx.close()


_INS = ["x_prompt", "x_sample", "cache_fox_k", "cache_fox_v", "cache_fox_logf", "state_ssd", "state_conv",
        "norm_pre", "norm_post", "w_in_even", "w_out_even", "gmlp_ws", "gmlp_bs", "gmlp_gv",
        "ssd_conv_w", "ssd_conv_b", "ssd_dt_bias", "ssd_a_log", "ssd_d", "ssd_norm_g",
        "w_in_odd", "fox_b_forget", "w_out_odd", "fox_gq", "fox_gk"]
_OUTS = [(1, 1024, 1024), (1, 32, 1024),
         (1, 1, 1024, 8, 128), (1, 1, 1024, 8, 128), (1, 1, 1024, 8),
         (1, 1, 16, 64, 128), (1, 1, 3, 1536),
         (1, 1, 32, 8, 128), (1, 1, 32, 8, 128), (1, 1, 32, 8),
         (1, 1, 16, 64, 128), (1, 1, 3, 1536), (1, 1, 32, 1024)]


def kernel(**inputs):
    import numpy as _np
    import concourse.bacc as _bacc
    from concourse import mybir as _mybir
    from concourse.bass_utils import run_bass_kernel_spmd as _run

    nc = _bacc.Bacc("TRN2", target_bir_lowering=False, num_devices=1)
    arrays, args = {}, []
    for name in _INS:
        a = _np.ascontiguousarray(inputs[name])
        arrays[f"in_{name}_dram"] = a
        args.append(nc.dram_tensor(f"in_{name}_dram", a.shape, _mybir.dt.from_np(a.dtype), kind="ExternalInput").ap())
    for i, shape in enumerate(_OUTS):
        args.append(nc.dram_tensor(f"out_{i}_dram", shape, _mybir.dt.float32, kind="ExternalOutput").ap())
    hybrid_trunk(nc, *args)
    r = _run(nc, [arrays], core_ids=[0])
    return tuple(r.results[0][f"out_{i}_dram"] for i in range(len(_OUTS)))
```
